# Optimizing a Trainium2 kernel written in Bass

```python
import numpy as np
import jax
import jax.numpy as jnp
from jax import lax

D_MODEL = 1024
BATCH = 1
SEQ = 128
DEPTH = 2
DEC_BATCH = 1
DEC_SEQ = 256
PAST_LEN = 128

GRID_W = 64
EPS = 1e-6
HEADS_A = 4
DK_A = 128
DV_A = 128
CONV_K = 5
CHUNK_A = 64
HEADS_B = 4
DK_B = 64
DV_B = 128
CHUNK_B = 64
HEADS_C = 8
KV_HEADS_C = 2
HEAD_DIM_C = 64
GROUP_C = HEADS_C // KV_HEADS_C
WINDOW = 128
Q_BLOCK = 128
ROPE_BASE = 10000.0
N_EXPERTS = 16
D_EXPERT = 512
EC_CAPACITY = 2
ADA_CHUNKS = 6

IN_SIZES = (
    HEADS_A * DK_A, HEADS_A * DK_A, HEADS_A * DV_A, HEADS_A * DV_A,
    HEADS_A, HEADS_A, HEADS_A, HEADS_A,
    HEADS_B * DK_B, HEADS_B * DK_B, HEADS_B * DV_B, HEADS_B * DV_B,
    HEADS_B, HEADS_B, HEADS_B, HEADS_B,
    HEADS_C * HEAD_DIM_C, KV_HEADS_C * HEAD_DIM_C, KV_HEADS_C * HEAD_DIM_C,
    D_MODEL, D_MODEL, D_MODEL,
)
N_IN = sum(IN_SIZES)
CONV_CH_A = 2 * HEADS_A * DK_A + HEADS_A * DV_A

kernel_name = "hybrid_diffusion_delta_mlstm_swa_ec_step"

def _rms_norm(x, g):
    x32 = x.astype(jnp.float32)
    y = x32 * lax.rsqrt(jnp.mean(x32 * x32, axis=-1, keepdims=True) + EPS)
    return (y * g.astype(jnp.float32)).astype(x.dtype)

def _l2_norm(x):
    x32 = x.astype(jnp.float32)
    return x32 * lax.rsqrt(jnp.sum(x32 * x32, axis=-1, keepdims=True) + EPS)

def _flip(x):
    return jnp.flip(x, axis=1)

def _short_conv(x, w):
    return lax.conv_general_dilated(
        x, w[:, None, :].astype(x.dtype), window_strides=(1,),
        padding=((CONV_K // 2, CONV_K // 2),),
        dimension_numbers=("NWC", "WIO", "NWC"), feature_group_count=x.shape[-1])

def _to_chunks(x, size):
    b, t, h = x.shape[:3]
    rest = x.shape[3:]
    x = x.reshape((b, t // size, size, h) + rest)
    return x.transpose((1, 0, 3, 2) + tuple(range(4, x.ndim)))

def _from_chunks(x):
    n, b, h, s, d = x.shape
    return x.transpose(1, 0, 3, 2, 4).reshape(b, n * s, h, d)

def _gated_delta_scan(q, k, v, beta, g, s0):
    dv = v.shape[-1]
    q, k, v, beta, g = (_to_chunks(a, CHUNK_A) for a in (q, k, v, beta, g))
    gc = jnp.cumsum(g, axis=-1)
    idx = jnp.arange(CHUNK_A)
    incl = idx[:, None] >= idx[None, :]
    strict = idx[:, None] > idx[None, :]
    dec_incl = jnp.exp(jnp.where(incl, gc[..., :, None] - gc[..., None, :], -jnp.inf))
    dec_strict = jnp.where(strict, dec_incl, 0.0)
    kb = k * beta[..., None]
    lower = jnp.einsum("nbhtd,nbhsd->nbhts", kb, k) * dec_strict
    rhs = jnp.concatenate([v * beta[..., None], kb * jnp.exp(gc)[..., None]], axis=-1)
    sol = lax.linalg.triangular_solve(
        lower + jnp.eye(CHUNK_A, dtype=lower.dtype), rhs,
        left_side=True, lower=True, unit_diagonal=True)
    u, w = sol[..., :dv], sol[..., dv:]
    a_intra = jnp.einsum("nbhtd,nbhsd->nbhts", q, k) * dec_incl
    g_last = gc[..., -1]
    q_dec = q * jnp.exp(gc)[..., None]
    k_dec = k * jnp.exp(g_last[..., None] - gc)[..., None]

    def step(s, xs):
        qd, kd, uc, wc, ac, gl = xs
        v_new = uc - jnp.einsum("bhtk,bhkv->bhtv", wc, s)
        o = jnp.einsum("bhtk,bhkv->bhtv", qd, s) + jnp.einsum("bhts,bhsv->bhtv", ac, v_new)
        s = jnp.exp(gl)[..., None, None] * s + jnp.einsum("bhsk,bhsv->bhkv", kd, v_new)
        return s, o

    s_fin, o = lax.scan(step, s0, (q_dec, k_dec, u, w, a_intra, g_last))
    return _from_chunks(o), s_fin

def _mlstm_scan(q, k, v, ig, lf, c0, n0, m0):
    q, k, v, ig, lf = (_to_chunks(a, CHUNK_B) for a in (q, k, v, ig, lf))
    bcum = jnp.cumsum(lf, axis=-1)
    b_last = bcum[..., -1]
    idx = jnp.arange(CHUNK_B)
    causal = idx[:, None] >= idx[None, :]
    d_log = jnp.where(causal, bcum[..., :, None] - bcum[..., None, :] + ig[..., None, :], -jnp.inf)
    d_max = jnp.max(d_log, axis=-1)
    tok_log = b_last[..., None] - bcum + ig
    tok_max = jnp.max(tok_log, axis=-1)
    qk = jnp.einsum("nbhtd,nbhsd->nbhts", q, k)

    def step(carry, xs):
        c, n, m = carry
        qc, kc, vc, bc, blc, dc, dmc, tc, tmc, qkc = xs
        m_t = jnp.maximum(bc + m[..., None], dmc)
        w_inter = jnp.exp(bc + m[..., None] - m_t)
        p = jnp.exp(dc - m_t[..., None]) * qkc
        num = (w_inter[..., None] * jnp.einsum("bhtd,bhde->bhte", qc, c)
               + jnp.einsum("bhts,bhse->bhte", p, vc))
        den = w_inter * jnp.einsum("bhtd,bhd->bht", qc, n) + jnp.sum(p, axis=-1)
        h = num / jnp.maximum(jnp.abs(den), jnp.exp(-m_t))[..., None]
        m_new = jnp.maximum(blc + m, tmc)
        w_prev = jnp.exp(blc + m - m_new)
        w_tok = jnp.exp(tc - m_new[..., None])
        c = w_prev[..., None, None] * c + jnp.einsum("bhsd,bhse->bhde", kc * w_tok[..., None], vc)
        n = w_prev[..., None] * n + jnp.einsum("bhs,bhsd->bhd", w_tok, kc)
        return (c, n, m_new), h

    (c, n, m), h = lax.scan(step, (c0, n0, m0),
                            (q, k, v, bcum, b_last, d_log, d_max, tok_log, tok_max, qk))
    return _from_chunks(h), c, n, m

def _gated_delta_branch(qa, ka, va, za, beta_f, beta_b, a_f, a_b, conv_w, a_log, dt_bias, norm_g, state0):
    b, t = qa.shape[:2]
    f32 = jnp.float32
    qkv = jax.nn.silu(_short_conv(jnp.concatenate([qa, ka, va], axis=-1), conv_w))
    q, k, v = jnp.split(qkv, [HEADS_A * DK_A, 2 * HEADS_A * DK_A], axis=-1)
    q = _l2_norm(q.reshape(b, t, HEADS_A, DK_A)) * (DK_A ** -0.5)
    k = _l2_norm(k.reshape(b, t, HEADS_A, DK_A))
    v = v.reshape(b, t, HEADS_A, DV_A).astype(f32)
    rate = jnp.exp(a_log.astype(f32))
    bias = dt_bias.astype(f32)
    bt_f = jax.nn.sigmoid(beta_f.astype(f32))
    bt_b = jax.nn.sigmoid(beta_b.astype(f32))
    g_f = -rate[0] * jax.nn.softplus(a_f.astype(f32) + bias[0])
    g_b = -rate[1] * jax.nn.softplus(a_b.astype(f32) + bias[1])
    s0 = state0.astype(f32)
    o_f, s_f = _gated_delta_scan(q, k, v, bt_f, g_f, s0[:, 0])
    o_b, s_b = _gated_delta_scan(_flip(q), _flip(k), _flip(v), _flip(bt_b), _flip(g_b), s0[:, 1])
    o = _rms_norm(o_f + _flip(o_b), norm_g) * jax.nn.silu(za.reshape(b, t, HEADS_A, DV_A).astype(f32))
    return o.reshape(b, t, HEADS_A * DV_A).astype(qa.dtype), jnp.stack([s_f, s_b], axis=1)

def _mlstm_branch(qb, kb, vb, ob, i_f, i_b, f_f, f_b, i_bias, f_bias, norm_g, c0, n0, m0):
    b, t = qb.shape[:2]
    f32 = jnp.float32
    q = qb.reshape(b, t, HEADS_B, DK_B).astype(f32)
    k = kb.reshape(b, t, HEADS_B, DK_B).astype(f32) * (DK_B ** -0.5)
    v = vb.reshape(b, t, HEADS_B, DV_B).astype(f32)
    ib = i_bias.astype(f32)
    fb = f_bias.astype(f32)
    ig_f = i_f.astype(f32) + ib[0]
    ig_b = i_b.astype(f32) + ib[1]
    lf_f = jax.nn.log_sigmoid(f_f.astype(f32) + fb[0])
    lf_b = jax.nn.log_sigmoid(f_b.astype(f32) + fb[1])
    c0 = c0.astype(f32)
    n0 = n0.astype(f32)
    m0 = m0.astype(f32)
    h_f, c_f, n_f, m_f = _mlstm_scan(q, k, v, ig_f, lf_f, c0[:, 0], n0[:, 0], m0[:, 0])
    h_b, c_b, n_b, m_b = _mlstm_scan(_flip(q), _flip(k), _flip(v), _flip(ig_b), _flip(lf_b),
                                     c0[:, 1], n0[:, 1], m0[:, 1])
    h = _rms_norm(h_f + _flip(h_b), norm_g) * jax.nn.sigmoid(ob.reshape(b, t, HEADS_B, DV_B).astype(f32))
    return (h.reshape(b, t, HEADS_B * DV_B).astype(qb.dtype),
            jnp.stack([c_f, c_b], axis=1), jnp.stack([n_f, n_b], axis=1), jnp.stack([m_f, m_b], axis=1))

def _rope_2d(x):
    t_len = x.shape[1]
    n_rows = t_len // GRID_W
    rows, cols = jnp.meshgrid(jnp.arange(n_rows), jnp.arange(GRID_W), indexing="ij")
    row = rows.reshape(-1).astype(jnp.float32)
    col = cols.reshape(-1).astype(jnp.float32)
    half = HEAD_DIM_C // 2
    nf = half // 2
    inv = jnp.power(ROPE_BASE, -jnp.arange(nf, dtype=jnp.float32) / nf)

    def rot(xp, pos):
        ang = pos[:, None] * inv[None, :]
        cos = jnp.cos(ang)[None, :, None, :]
        sin = jnp.sin(ang)[None, :, None, :]
        x1, x2 = xp[..., :nf], xp[..., nf:]
        return jnp.concatenate([x1 * cos - x2 * sin, x1 * sin + x2 * cos], axis=-1)

    x32 = x.astype(jnp.float32)
    return jnp.concatenate([rot(x32[..., :half], row), rot(x32[..., half:], col)], axis=-1).astype(x.dtype)

def _ctx_attention(q, k, v, sink):
    b, p = q.shape[:2]
    nq = p // Q_BLOCK
    scale = HEAD_DIM_C ** -0.5
    qb = q.reshape(b, nq, Q_BLOCK, KV_HEADS_C, GROUP_C, HEAD_DIM_C).transpose(1, 0, 2, 3, 4, 5)
    sink_hg = sink.astype(jnp.float32).reshape(KV_HEADS_C, GROUP_C)

    def block(qi):
        s = jnp.einsum("bqhgd,bkhd->bhgqk", qi, k).astype(jnp.float32) * scale
        sk = jnp.broadcast_to(sink_hg[None, :, :, None, None], s.shape[:-1] + (1,))
        pr = jax.nn.softmax(jnp.concatenate([s, sk], axis=-1), axis=-1)[..., :-1]
        return jnp.einsum("bhgqk,bkhd->bqhgd", pr.astype(v.dtype), v)

    o = lax.map(block, qb)
    return o.transpose(1, 0, 2, 3, 4, 5).reshape(b, p, HEADS_C * HEAD_DIM_C)

def _latent_attention(q, k, v, ck, cv, sink):
    b, t = q.shape[:2]
    p_ctx = ck.shape[1]
    nb = t // Q_BLOCK
    span = Q_BLOCK + 2 * WINDOW
    scale = HEAD_DIM_C ** -0.5
    kp = jnp.pad(k, ((0, 0), (WINDOW, WINDOW), (0, 0), (0, 0)))
    vp = jnp.pad(v, ((0, 0), (WINDOW, WINDOW), (0, 0), (0, 0)))
    qb = q.reshape(b, nb, Q_BLOCK, KV_HEADS_C, GROUP_C, HEAD_DIM_C).transpose(1, 0, 2, 3, 4, 5)
    sink_hg = sink.astype(jnp.float32).reshape(KV_HEADS_C, GROUP_C)
    offs_q = jnp.arange(Q_BLOCK)
    offs_k = jnp.arange(span) - WINDOW

    def block(args):
        i, qi = args
        start = i * Q_BLOCK
        kl = lax.dynamic_slice_in_dim(kp, start, span, axis=1)
        vl = lax.dynamic_slice_in_dim(vp, start, span, axis=1)
        qpos = start + offs_q
        kpos = start + offs_k
        valid = ((jnp.abs(qpos[:, None] - kpos[None, :]) <= WINDOW)
                 & (kpos >= 0)[None, :] & (kpos < t)[None, :])
        sl = jnp.einsum("bqhgd,bkhd->bhgqk", qi, kl).astype(jnp.float32) * scale
        sl = jnp.where(valid, sl, -jnp.inf)
        sc = jnp.einsum("bqhgd,bkhd->bhgqk", qi, ck).astype(jnp.float32) * scale
        sk = jnp.broadcast_to(sink_hg[None, :, :, None, None], sl.shape[:-1] + (1,))
        pr = jax.nn.softmax(jnp.concatenate([sl, sc, sk], axis=-1), axis=-1)
        pl = pr[..., :span].astype(v.dtype)
        pc = pr[..., span:span + p_ctx].astype(cv.dtype)
        return (jnp.einsum("bhgqk,bkhd->bqhgd", pl, vl)
                + jnp.einsum("bhgqk,bkhd->bqhgd", pc, cv).astype(v.dtype))

    o = lax.map(block, (jnp.arange(nb), qb))
    return o.transpose(1, 0, 2, 3, 4, 5).reshape(b, t, HEADS_C * HEAD_DIM_C)

def _expert_choice_ffn(h, w_router, w_gate, w_up, w_down):
    b, t, _ = h.shape
    cap = EC_CAPACITY * t // N_EXPERTS
    aff = jax.nn.softmax((h @ w_router).astype(jnp.float32), axis=-1)
    gates, idx = lax.top_k(aff.transpose(0, 2, 1), cap)
    bidx = jnp.arange(b)[:, None, None]
    xs = h[bidx, idx]
    hid = (jax.nn.silu(jnp.einsum("becd,edf->becf", xs, w_gate))
           * jnp.einsum("becd,edf->becf", xs, w_up))
    ye = jnp.einsum("becf,efd->becd", hid, w_down) * gates[..., None].astype(h.dtype)
    return jnp.zeros_like(h).at[bidx, idx].add(ye)

def _token_mix(h, lw, ctx):
    b, t = h.shape[:2]
    f32 = jnp.float32
    proj = h @ lw["w_in"]
    (qa, ka, va, za, beta_f, beta_b, a_f, a_b,
     qb, kb, vb, ob, i_f, i_b, f_f, f_b,
     qc, kc, vc, ga, gb, gc) = jnp.split(proj, np.cumsum(IN_SIZES)[:-1].tolist(), axis=-1)
    if ctx is None:
        d0 = jnp.zeros((b, 2, HEADS_A, DK_A, DV_A), f32)
        c0 = jnp.zeros((b, 2, HEADS_B, DK_B, DV_B), f32)
        n0 = jnp.zeros((b, 2, HEADS_B, DK_B), f32)
        m0 = jnp.zeros((b, 2, HEADS_B), f32)
    else:
        ck, cv, d0, c0, n0, m0 = ctx
    ya, d_new = _gated_delta_branch(qa, ka, va, za, beta_f, beta_b, a_f, a_b, lw["conv_qkv_a"],
                                    lw["delta_a_log"], lw["delta_dt_bias"], lw["delta_norm_g"], d0)
    yb, c_new, n_new, m_new = _mlstm_branch(qb, kb, vb, ob, i_f, i_b, f_f, f_b, lw["mlstm_i_bias"],
                                            lw["mlstm_f_bias"], lw["mlstm_norm_g"], c0, n0, m0)
    q = qc.reshape(b, t, HEADS_C, HEAD_DIM_C)
    k = kc.reshape(b, t, KV_HEADS_C, HEAD_DIM_C)
    v = vc.reshape(b, t, KV_HEADS_C, HEAD_DIM_C)
    if ctx is None:
        yc = _ctx_attention(q, k, v, lw["attn_sink"])
        new_ctx = (k, v, d_new, c_new, n_new, m_new)
    else:
        yc = _latent_attention(_rope_2d(q), _rope_2d(k), v, ck, cv, lw["attn_sink"])
        new_ctx = None
    mixed = (jax.nn.sigmoid(ga) * (ya @ lw["w_branch_a"])
             + jax.nn.sigmoid(gb) * (yb @ lw["w_branch_b"])
             + jax.nn.sigmoid(gc) * (yc @ lw["w_branch_c"]))
    return mixed @ lw["w_out"], new_ctx

def _layer(x, cvec, lw, ctx):
    mod = jax.nn.silu(cvec) @ lw["ada_w"] + lw["ada_b"]
    sh1, sc1, g1, sh2, sc2, g2 = [m[:, None, :] for m in jnp.split(mod, ADA_CHUNKS, axis=-1)]
    h = _rms_norm(x, lw["norm1_g"]) * (1.0 + sc1) + sh1
    mix, new_ctx = _token_mix(h, lw, ctx)
    x = x + g1 * mix
    h = _rms_norm(x, lw["norm2_g"]) * (1.0 + sc2) + sh2
    x = x + g2 * _expert_choice_ffn(h, lw["w_router"], lw["w_expert_gate"],
                                    lw["w_expert_up"], lw["w_expert_down"])
    return x, new_ctx

def setup_inputs(seed: int = 0) -> dict:
    key = jax.random.key(seed)
    ks = iter(jax.random.split(key, 40))
    f32 = jnp.float32

    def nrm(shape, scale=1.0):
        return scale * jax.random.normal(next(ks), shape, f32)

    def gain(shape):
        return 1.0 + nrm(shape, 0.02)

    return {
        "x_prompt": nrm((BATCH, SEQ, D_MODEL)),
        "x_sample": nrm((DEC_BATCH, DEC_SEQ, D_MODEL)),
        "cache_attn_k": nrm((DEC_BATCH, DEPTH, PAST_LEN, KV_HEADS_C, HEAD_DIM_C)),
        "cache_attn_v": nrm((DEC_BATCH, DEPTH, PAST_LEN, KV_HEADS_C, HEAD_DIM_C)),
        "state_delta": nrm((DEC_BATCH, DEPTH, 2, HEADS_A, DK_A, DV_A), 0.2),
        "state_mlstm_c": nrm((DEC_BATCH, DEPTH, 2, HEADS_B, DK_B, DV_B), 0.2),
        "state_mlstm_n": nrm((DEC_BATCH, DEPTH, 2, HEADS_B, DK_B), 0.2),
        "state_mlstm_m": nrm((DEC_BATCH, DEPTH, 2, HEADS_B)),
        "c": nrm((DEC_BATCH, D_MODEL)),
        "c_ctx": nrm((D_MODEL,)),
        "ada_w": nrm((DEPTH, D_MODEL, ADA_CHUNKS * D_MODEL), D_MODEL ** -0.5),
        "ada_b": nrm((DEPTH, ADA_CHUNKS * D_MODEL), 0.02),
        "norm1_g": gain((DEPTH, D_MODEL)),
        "norm2_g": gain((DEPTH, D_MODEL)),
        "w_in": nrm((DEPTH, D_MODEL, N_IN), D_MODEL ** -0.5),
        "conv_qkv_a": nrm((DEPTH, CONV_K, CONV_CH_A), CONV_K ** -0.5),
        "delta_a_log": jnp.log(jax.random.uniform(next(ks), (DEPTH, 2, HEADS_A), f32, 1.0, 16.0)),
        "delta_dt_bias": nrm((DEPTH, 2, HEADS_A), 0.5) - 4.0,
        "delta_norm_g": gain((DEPTH, DV_A)),
        "mlstm_i_bias": nrm((DEPTH, 2, HEADS_B), 0.1),
        "mlstm_f_bias": nrm((DEPTH, 2, HEADS_B), 0.5) + 3.0,
        "mlstm_norm_g": gain((DEPTH, DV_B)),
        "attn_sink": nrm((DEPTH, HEADS_C), 0.5),
        "w_branch_a": nrm((DEPTH, HEADS_A * DV_A, D_MODEL), (HEADS_A * DV_A) ** -0.5),
        "w_branch_b": nrm((DEPTH, HEADS_B * DV_B, D_MODEL), (HEADS_B * DV_B) ** -0.5),
        "w_branch_c": nrm((DEPTH, HEADS_C * HEAD_DIM_C, D_MODEL), (HEADS_C * HEAD_DIM_C) ** -0.5),
        "w_out": nrm((DEPTH, D_MODEL, D_MODEL), D_MODEL ** -0.5),
        "w_router": nrm((DEPTH, D_MODEL, N_EXPERTS), D_MODEL ** -0.5),
        "w_expert_gate": nrm((DEPTH, N_EXPERTS, D_MODEL, D_EXPERT), D_MODEL ** -0.5),
        "w_expert_up": nrm((DEPTH, N_EXPERTS, D_MODEL, D_EXPERT), D_MODEL ** -0.5),
        "w_expert_down": nrm((DEPTH, N_EXPERTS, D_EXPERT, D_MODEL), D_EXPERT ** -0.5),
        "final_norm_g": gain((D_MODEL,)),
    }

def reference(x_prompt, x_sample, cache_attn_k, cache_attn_v, state_delta, state_mlstm_c, state_mlstm_n,
              state_mlstm_m, c, c_ctx, ada_w, ada_b, norm1_g, norm2_g, w_in, conv_qkv_a, delta_a_log,
              delta_dt_bias, delta_norm_g, mlstm_i_bias, mlstm_f_bias, mlstm_norm_g, attn_sink, w_branch_a,
              w_branch_b, w_branch_c, w_out, w_router, w_expert_gate, w_expert_up, w_expert_down, final_norm_g):
    def layer_weights(l):
        return {
            "ada_w": ada_w[l], "ada_b": ada_b[l], "norm1_g": norm1_g[l], "norm2_g": norm2_g[l],
            "w_in": w_in[l], "conv_qkv_a": conv_qkv_a[l], "delta_a_log": delta_a_log[l],
            "delta_dt_bias": delta_dt_bias[l], "delta_norm_g": delta_norm_g[l],
            "mlstm_i_bias": mlstm_i_bias[l], "mlstm_f_bias": mlstm_f_bias[l], "mlstm_norm_g": mlstm_norm_g[l],
            "attn_sink": attn_sink[l], "w_branch_a": w_branch_a[l], "w_branch_b": w_branch_b[l],
            "w_branch_c": w_branch_c[l], "w_out": w_out[l], "w_router": w_router[l],
            "w_expert_gate": w_expert_gate[l], "w_expert_up": w_expert_up[l], "w_expert_down": w_expert_down[l],
        }

    xp = x_prompt
    ctx_cond = c_ctx[None, :]
    ks, vs, ds, cs, ns, ms = [], [], [], [], [], []
    for l in range(DEPTH):
        xp, (k_l, v_l, d_l, c_l, n_l, m_l) = _layer(xp, ctx_cond, layer_weights(l), None)
        ks.append(k_l)
        vs.append(v_l)
        ds.append(d_l)
        cs.append(c_l)
        ns.append(n_l)
        ms.append(m_l)
    y_prompt = _rms_norm(xp, final_norm_g)
    dt = x_prompt.dtype
    new_attn_k = jnp.stack(ks, axis=1).astype(dt)
    new_attn_v = jnp.stack(vs, axis=1).astype(dt)
    new_state_delta = jnp.stack(ds, axis=1).astype(dt)
    new_state_mlstm_c = jnp.stack(cs, axis=1).astype(dt)
    new_state_mlstm_n = jnp.stack(ns, axis=1).astype(dt)
    new_state_mlstm_m = jnp.stack(ms, axis=1).astype(dt)

    xs = x_sample
    for l in range(DEPTH):
        ctx_l = (cache_attn_k[:, l], cache_attn_v[:, l], state_delta[:, l],
                 state_mlstm_c[:, l], state_mlstm_n[:, l], state_mlstm_m[:, l])
        xs, _ = _layer(xs, c, layer_weights(l), ctx_l)
    y_sample = _rms_norm(xs, final_norm_g)

    return (y_prompt, y_sample, new_attn_k, new_attn_v, new_state_delta,
            new_state_mlstm_c, new_state_mlstm_n, new_state_mlstm_m)


_drawn_inputs = setup_inputs


def setup_inputs(seed=0):
    import zlib

    import numpy as np

    out = dict(_drawn_inputs(seed))
    spreads = {}
    factors = {'mlstm_norm_g': 2.985, 'attn_sink': 5.245, 'final_norm_g': 2.89}
    for name, (base, spread) in spreads.items():
        noise = np.random.default_rng([zlib.crc32(name.encode()), seed]).standard_normal(out[name].shape)
        drawn = base * np.exp(spread * noise) if base else spread * noise
        out[name] = jnp.asarray(drawn.astype(out[name].dtype))
    for name, factor in factors.items():
        out[name] = (out[name] * factor).astype(out[name].dtype)
    return out
```

```python
from contextlib import ExitStack

import concourse.bass as bass
from concourse import mybir

F32 = mybir.dt.float32
ALU = mybir.AluOpType
ACT = mybir.ActivationFunctionType
AX = mybir.AxisListType.X

D = 1024
KT = D // 128
SEQ, DSEQ, PAST = 128, 256, 128
N = SEQ + DSEQ
TILES = N // 128
GROUPS = ((0, 0, SEQ), (1, SEQ, N))
DEPTH = 2
EPS = 1e-6
H = 4
CH = 64
DKB, VA = 64, 132
CONV_K = 5
PADW = 2 + SEQ + 4 + DSEQ + 2
HC, DC = 8, 64
NE = 16
CAP_S, CAP_P = 2 * DSEQ // NE, 2 * SEQ // NE
ROWS = CAP_S + CAP_P
SLOT_E = 64
NEG = -1.0e30
ADA_BLOCKS = 6 * D // 512
C_QA, C_GATE_A, C_QB, C_VB, C_OB, C_GATE_B, C_QC, C_KC, C_G = 0, 2048, 2064, 2576, 3088, 3600, 3616, 4128, 4384

RING = 4
MIX_BLOCKS = 3 * 3 + 2
HEAD_BLOCKS = ADA_BLOCKS + 9
ADA_GROUPS = 3
PLAIN_BLOCKS = HEAD_BLOCKS + MIX_BLOCKS
LAYER_BLOCKS = PLAIN_BLOCKS + 3 * NE
Q_BLOCK = ADA_BLOCKS + 7


def loads_in_slot(last):
    return sum(8 if i == Q_BLOCK else 1 for i in range(last % RING, last + 1, RING))


E_UNROLL = 4
assert PLAIN_BLOCKS % RING == 0 and (3 * E_UNROLL) % RING == 0

BATCHES = ((0, 0, 0), (0, 1, 0), (1, 0, 1), (2, 0, 1), (2, 1, 1), (1, 1, 1))
NB = len(BATCHES)
LEVELS = (1, 2, 4, 8, 16, 32)


class Track:

    def __init__(self, sem, steps, base):
        self.sem, self.steps, self.made, self.base = sem, list(steps), 0, base
        self.per = len(self.steps)
        self.number = {s: i + 1 for i, s in enumerate(self.steps)}
        assert len(self.number) == self.per

    def at(self, l, step):
        return l * self.per + self.base + self.number[step]

    def before(self, l):
        return l * self.per + self.base

    def mark(self, step):
        assert self.steps[self.made % self.per] == step, (self.steps[self.made % self.per], step)
        self.made += 1
        return self.sem

    def looped(self, turns, body):
        self.made += (turns - 1) * body


def const_columns():
    import numpy as np
    r = np.arange(128)[:, None]
    t = np.arange(128)[None, :]
    same = (r // CH) == (t // CH)
    tabs = {}
    tabs["ident"] = (r == t)
    tabs["ones"] = np.ones((128, 128))
    tabs["tri0"] = same & (r <= t)
    tabs["tri1"] = same & (r >= t)
    tabs["block"] = same
    tabs["half0"] = np.broadcast_to(r < CH, (128, 128))
    tabs["half1"] = np.broadcast_to(r >= CH, (128, 128))
    tabs["strict0"] = same & (r > t)
    tabs["strict1"] = same & (r < t)
    for b in LEVELS:
        pair = (r // (2 * b)) == (t // (2 * b))
        tabs[f"lev0_{b}"] = pair & (r % (2 * b) >= b) & (t % (2 * b) < b)
        tabs[f"lev1_{b}"] = pair & (r % (2 * b) < b) & (t % (2 * b) >= b)
    tabs["neg0"] = np.where(same & (r >= t), 0.0, NEG)
    tabs["neg1"] = np.where(same & (r <= t), 0.0, NEG)
    tabs["earlier"] = (t < r)
    d = np.arange(128) % DC
    nf = DC // 4
    inv = np.power(np.float32(10000.0), -np.arange(nf, dtype=np.float32) / np.float32(nf)).astype(np.float32)
    pos = np.arange(DSEQ)
    row, col = (pos // 64).astype(np.float32), (pos % 64).astype(np.float32)
    ang = np.where((d < 2 * nf)[:, None], row[None, :], col[None, :]) * inv[d % nf][:, None]
    tabs["cos"] = np.cos(ang.astype(np.float32))
    tabs["sin"] = np.sin(ang.astype(np.float32))
    first = (d % (2 * nf)) < nf
    partner = np.where(first, np.arange(128) + nf, np.arange(128) - nf)
    rot = np.zeros((128, 128))
    rot[partner, np.arange(128)] = np.where(first, -1.0, 1.0)
    tabs["rot"] = rot
    for i in range(2):
        q = i * 128 + r
        k = np.arange(DSEQ)[None, :]
        tabs[f"win{i}"] = np.concatenate([np.zeros((128, PAST)), np.where(np.abs(q - k) <= 128, 0.0, NEG)], axis=1)
    slot = np.arange(SLOT_E)
    tabs["slot_s"] = np.broadcast_to(np.where(slot < CAP_S, slot, -1), (128, SLOT_E))
    tabs["slot_p"] = np.broadcast_to(np.where((slot >= CAP_S) & (slot < ROWS), slot - CAP_S, -1), (128, SLOT_E))
    where, cols, at = {}, [], 0
    for name, a in tabs.items():
        where[name] = (at, a.shape[1])
        at += a.shape[1]
        cols.append(np.asarray(a, dtype=np.float32))
    return np.ascontiguousarray(np.concatenate(cols, axis=1)), where



def build_step(nc, args):
    (x_prompt, x_sample, cache_k, cache_v, state_delta, state_c, state_n, state_m, c_lat, c_ctx, ada_w, ada_b,
     norm1_g, norm2_g, w_in, conv_w, a_log, dt_bias, delta_g, i_bias, f_bias, mlstm_g, sink, w_a, w_b, w_c,
     w_out, w_router, w_gate, w_up, w_down, final_g, consts,
     y_prompt, y_sample, new_k, new_v, new_delta, new_c, new_n, new_m) = args
    _, where = const_columns()
    ds = bass.ds

    with ExitStack() as ctx:
        def sb(name, words):
            return ctx.enter_context(nc.sbuf_tensor(name, [128, words], F32))

        def sem(name):
            return ctx.enter_context(nc.semaphore(name))

        PS = ctx.enter_context(nc.psum_tensor("PS", [128, 8, 512], F32))

        xT_b = sb("xT", KT * N)
        hT_b = sb("hT", KT * N)
        ring = sb("ring", RING * KT * 512)
        const = sb("const", consts.shape[1])
        mod_b = sb("mod", 48 * 2)
        vec_row = sb("vec_row", 128)
        vecT = sb("vecT", 128)
        condT = sb("condT", KT * 2)
        fin_g = sb("fin_g", KT)
        affine = sb("affine", 2 * KT * 2)
        rstd = sb("rstd", N)
        ada_rows = sb("ada_rows", 512)
        small = sb("small", 1696)
        arena = sb("arena", 22304)
        xT = xT_b[:, :].rearrange("p (k n) -> p k n", k=KT)
        hT = hT_b[:, :].rearrange("p (k n) -> p k n", k=KT)
        mod = mod_b[:, :].rearrange("p (c v) -> p c v", v=2)

        def K(name):
            a, n = where[name]
            return const[:, a:a + n]

        def carve(base, at, *shape):
            n = 1
            for s in shape:
                n *= s
            assert at + n <= base.shape[1], (at, n)
            v = base[:, at:at + n]
            if len(shape) == 2:
                v = v.rearrange("p (a b) -> p a b", a=shape[0])
            if len(shape) == 3:
                v = v.rearrange("p (a b c) -> p a b c", a=shape[0], b=shape[1])
            if len(shape) == 4:
                v = v.rearrange("p (a b c d) -> p a b c d", a=shape[0], b=shape[1], c=shape[2])
            return v

        class Place:
            def __init__(self, base, at=0):
                self.base, self.at = base, at

            def __call__(self, *shape):
                n = 1
                for s in shape:
                    n *= s
                v = carve(self.base, self.at, *shape)
                self.at += n
                return v

        def over(ap, axis, n):
            shape = list(ap.shape)
            shape.insert(axis, n)
            return ap.unsqueeze(axis).broadcast_to(shape)

        P = Place(small)
        w_small = P(KT, 32)
        a_log_b = P(8)
        bias_b = P(32)
        sink_b = P(8)
        m_state = P(2, 2, H)
        mnorm_b = P(128)
        gates = P(TILES, 32)
        soft = P(TILES, 32)
        g_lf = P(TILES, 2, 2 * H)
        beta = P(TILES, 8)
        cum = P(TILES, 2, 2 * H)
        tot = P(TILES, 2, 2 * H)
        chunk_tot = P(2, TILES, 2, 2 * H)
        e_cum = P(TILES, 2, H)
        kd_f = P(TILES, 2, H)
        kbg_f = P(TILES, 2, H)
        e_chunk = P(2, TILES, 2, H)
        rcol = P(TILES, 2, H)
        neg_rate = P(8)
        stab = P(64)
        args_b = P(5, H)
        exps = P(5, H)
        wp = P(2, 2)
        mx = P(H, 2)
        dmx = P(H)
        nmax = P(2, 4)
        sums = P(2, 4)
        esink = P(2, 4)
        rinv = P(8)
        rden = P(H)
        ss4 = P(H)
        logit = P(TILES, NE)
        aff = P(TILES, NE)
        aff_x = P(TILES, NE)
        smx = P(TILES)
        rank = P(TILES, NE)
        rtmp = P(3, NE)
        w_rt = P(KT, NE)
        m_out = P(8)

        A = Place(arena)
        yT = [A(H, N) for _ in range(3)]
        phase0 = A.at

        A = Place(arena, phase0)
        qkvT = A(3 * H, N)
        pads = A(4, PADW)
        acc = A(2, PADW - 4)
        states = A(2, 2, H, 128)
        S512 = [A(H, 128) for _ in range(15)]
        (G2, dec, dinc, dstr, vb, kbg, kd, Lm, LT, av, aT, X, XT, Wm, qd) = S512
        A = Place(arena, phase0 - 2 * H * N)
        Mb = [A(H, 128) for _ in range(5)]
        er = A(H, 128)
        uv, wT, vn, Sd = Mb[0:4]
        nrm = acc

        A = Place(arena, phase0)
        qkbT = A(4, N)
        kb_tok = A(TILES, 256)
        v_aug = A(TILES, H, VA)
        ob_s = A(TILES, 512)
        hb_tok = A(TILES, H, 128)
        Cst = A(2, 2, 2, VA)
        T512 = [A(H, 128) for _ in range(8)]
        (G3, g3b, Rm, Em, Pm, PTm, hb_n, sq_b) = T512
        kw = A(H, DKB)
        QCw = A(H, VA)
        num = A(H, VA)

        A = Place(arena, phase0)
        qcT = A(4, N)
        kcT = A(N)
        kv_tok = A(TILES, 256)
        ck_tok = A(128)
        cv_tok = A(128)
        ckT = A(PAST)
        rope_a = A(5, DSEQ)
        rope_b = A(5, DSEQ)
        prob = A(2, 4, PAST + DSEQ)
        probT = A(2, 4, PAST + DSEQ)
        yc_tok = A(512)

        A = Place(arena, phase0)
        mixT = A(KT, N)
        sig = A(2, N)
        prod = A(2, N)
        norm_sq = mixT

        A = Place(arena, 0)
        xsT = A(KT, NE, ROWS)
        selGT = A(NE // 2, N)
        e0 = A.at
        h_tok = A(TILES, D)
        sel = A(TILES, NE, SLOT_E)
        selG = A(TILES, NE, SLOT_E)
        rk = carve(arena, A.at, NE, 128)
        rk_tmp = carve(arena, e0 + TILES * D, NE, 128)
        rk_m = carve(arena, e0 + TILES * D + NE * 128, NE, 128)
        diag = carve(arena, 0, NE, 128)
        ye = carve(arena, e0, NE // 2, D)
        A = Place(arena, e0 + NE // 2 * D)
        silu_g = A(512)
        hid = A(2, 512)
        hidT = A(2, 4, ROWS)
        xs_e = A(2, KT, ROWS)

        x_tok = carve(arena, phase0, TILES, D)
        cond_rows = carve(arena, phase0 + TILES * D, 128)
        y_tok = x_tok

        rng = range
        steps = {
            "ring_used": [("block", i) for i in rng(LAYER_BLOCKS)],
            "pre_pe": ["rows", "x"], "pre_act": ["vec", "x"], "pre_dve": ["clear", "x"],
            "ada_pe": ["vec"] + [s for n in rng(3) for s in (("rows", n), ("tr", n))],
            "ada_act": ["vec", "rate"] + [("rows", n) for n in rng(3)], "ada_dve": [("mod", n) for n in rng(3)],
            "nrm_pe": ["ss0", "ss1"], "nrm_act": ["sq0", "sqrt0", "h0", "sq1", "sqrt1", "h1"],
            "nrm_dve": ["rstd0", "xn0", "rstd1", "xn1"],
            "gate_pe": ["proj", "cum"], "gate_act": ["exp", "ln", "ecum"], "gate_dve": ["biased", "lf", "args", "done"],
            "conv_pe": [("p", j) for j in rng(12)] + [("ss", j) for j in rng(8)],
            "conv_act": [s for j in rng(13) for s in ([("pad", j)] if j < 12 else []) + ([("silu", j - 1)] if j else [])]
            + [("sq", j) for j in rng(8)] + [("root", j) for j in rng(8)],
            "conv_dve": [("conv", j) for j in rng(12)] + [("unit", j) for j in rng(8)],
            "delta_pe": [("row", 0), ("tok", 0), ("kk", 0)]
            + [s for b in rng(NB) for s in [("lt", b)]
               + [(x, b, i, h) for i in rng(5) for x in "wy" for h in rng(2)] + [("at", b), ("uw", b), ("ws", b, 0)]
               + ([("row", b + 1), ("tok", b + 1)] if b + 1 < NB else []) + [("os", b, 0), ("ws", b, 1)]
               + ([("kk", b + 1)] if b + 1 < NB else []) + [("os", b, 1)]],
            "delta_act": [("er", 0), ("dec", 0)]
            + [s for b in rng(NB) for s in [("ltc", b)] + [("wc", b, i, h) for i in rng(5) for h in rng(2)]
               + [("atc", b), ("wtc", b)] + ([("er", b + 1), ("dec", b + 1)] if b + 1 < NB else [])],
            "delta_dve": [("g2", 0), ("d", 0), ("vk", 0), ("qk", 0), ("la", 0)]
            + [s for b in rng(NB) for s in [("x0", b)] + [("x", b, i, h) for i in rng(5) for h in rng(2)] + [("u", b)]
               + ([("g2", b + 1)] if b + 1 < NB else []) + [("vn", b, 0)] + ([("d", b + 1)] if b + 1 < NB else [])
               + [("s", b, 0), ("vn", b, 1)] + ([("vk", b + 1)] if b + 1 < NB else []) + [("s", b, 1)]
               + ([("qk", b + 1), ("la", b + 1)] if b + 1 < NB else [])],
            "delta_pool": [("m", b) for b in rng(NB)],
            "z_pe": [("z", j) for j in rng(4)] + ["ss"], "z_act": [("z", j) for j in rng(4)] + ["sq", "root"],
            "z_dve": ["root", ("y", 0)],
            "mp_pe": [("qk", j) for j in rng(4)] + [("kt", t) for t in rng(3)] + [("v", t) for t in rng(3)]
            + [("o", t) for t in rng(3)],
            "mp_act": [("qk", j) for j in rng(4)] + [("o", t) for t in rng(3)],
            "mp_dve": ["ones"] + [("kt", t) for t in rng(3)] + [("v", t) for t in rng(3)],
            "ml_pe": [s for b in rng(NB) for s in [("row", b), ("qk", b), ("pt", b), ("pv", b)]
                      + [x for c in rng(2) for x in (("qc", b, c), ("up", b, c))]] + [("yt", t) for t in rng(3)],
            "ml_act": [s for b in rng(NB) for s in [("ex", b), ("E", b), ("ptc", b)]]
            + ["root"] + [("yt", t) for t in rng(3)],
            "ml_dve": [s for b in rng(NB) for s in [("g3", b), ("args", b), ("P", b), ("kw", b)]
                       + [("c", b, c) for c in rng(2)] + [("h", b)]] + ["ss"] + [("y", t) for t in rng(3)],
            "ap_pe": [("q", j) for j in rng(4)] + ["k"] + [("kv", t) for t in rng(3)] + ["ckT"]
            + [("rot", j) for j in rng(5)],
            "ap_act": [("q", j) for j in rng(4)] + ["k"] + ["ckT"],
            "ap_dve": [("kv", t) for t in rng(3)] + [("cos", j) for j in rng(5)] + ["rope"],
            "at_pe": [s for u in rng(6) for s in [("s", u), ("pt", u, 0), ("pt", u, 1), ("pt", u, 2), ("pv", u)]
                      + [("yt", u // 2)] * (u % 2)],
            "at_act": [s for u in rng(6) for s in [("e", u), ("ptc", u)] + [("yt", u // 2)] * (u % 2)],
            "at_dve": [s for u in rng(6) for s in [("mx", u), ("y", u)]],
            "mix_pe": [s for r in rng(3) for c in rng(KT) for s in (("g", r, c), ("y", r, c))]
            + [("o", c) for c in rng(KT)],
            "mix_act": [("sig", r, c) for r in rng(3) for c in rng(KT)],
            "mix_dve": [("m", r, c) for r in rng(3) for c in rng(KT)] + [("x", c) for c in rng(KT)],
            "rt_pe": ["logit", "affx"] + [("R", t) for t in rng(3)] + [("ht", t, u) for t in rng(3) for u in rng(2)]
            + [("sg", j) for j in rng(NE // 2)] + [("xs", k) for k in rng(KT)],
            "rt_act": ["exp"] + [("ht", t, u) for t in rng(3) for u in rng(2)],
            "rt_dve": ["max", "aff", "affx"] + [s for t in rng(3) for s in (("diag", t), ("rank", t))] + ["sel"]
            + [("sg", j) for j in rng(NE // 2)] + [("xs", k) for k in rng(KT)],
            "rt_pool": ["clear"],
            "cb_pe": [("x", k) for k in rng(KT)], "cb_dve": [("x", k) for k in rng(KT)],
            "ex_pool": [(e, "xs") for e in rng(NE)],
            "ex_pe": [(e, "t") for e in rng(NE)],
            "ex_act": [(e, s) for e in rng(NE) for s in ("silu", "ht", "d")],
            "ex_dve": [(e, s) for e in rng(NE) for s in ("hid", "d")],
        }
        def base(name):
            return RING if name == "ring_used" else 7 if name.startswith("ex_") else 1

        T = {name: Track(sem(name), s, base(name)) for name, s in steps.items()}
        by_engine = {"pe": [], "act": [], "dve": [], "pool": []}
        for name in T:
            by_engine["pe" if name == "ring_used" else name.split("_")[1]].append(name)
        slot_in = [sem(f"slot_in{s}") for s in range(RING)]
        start_in = sem("start_in")
        vec_in = sem("vec_in")
        state_in = sem("state_in")
        stored = sem("stored")
        final_stored = sem("final_stored")
        final_pe, final_act, final_dve = sem("final_pe"), sem("final_act"), sem("final_dve")
        apart = {e: sem(f"apart_{e}") for e in ("pe", "pool")}
        ADA_IN_BATCH = {1: 1, 3: 2}
        VEC_LOADS, STORES = 15, 13
        STATE_LOADS = 12

        def prime(eng, kind):
            for name in by_engine[kind]:
                eng.sem_inc(T[name].sem, base(name))

        def W(eng, l, name, step):
            eng.wait_ge(T[name].sem, T[name].at(l, step))

        def WB(eng, l, eg, i, back=0):
            t = T["ring_used"]
            eng.wait_ge(t.sem, t.at(l, ("block", i)) - 3 * back + eg * (3 * E_UNROLL))

        def WE(eng, l, eg, name, step, back=0):
            t = T[name]
            per_expert = t.per // NE
            eng.wait_ge(t.sem, t.at(l, step) - back * per_expert + eg * (E_UNROLL * per_expert))

        block = ctx.enter_context(nc.Block())

        @block.sync
        def _(sp):
            def load_block(l, i, src, e=None):
                sp.wait_ge(T["ring_used"].sem, l * LAYER_BLOCKS + 1 + i + (0 if e is None else e * 3))
                kt = src.shape[1]
                dst = ring[:, (i % RING) * KT * 512:(i % RING + 1) * KT * 512].rearrange("p (k n) -> p k n", k=kt)
                sp.dma_start(dst[:, :, 0:src.shape[2]], src).then_inc(slot_in[i % RING], 16)

            def rows(w, l, c0, c1):
                return w[ds(l, 1), :, c0:c1].rearrange("a (k p) n -> p (a k) n", p=128)

            sp.dma_start(const[:, :], consts).then_inc(start_in, 16)
            sp.dma_start(x_tok[:, 0:1, :], x_prompt.rearrange("b (t p) d -> p (b t) d", p=128)).then_inc(start_in, 16)
            sp.dma_start(x_tok[:, 1:3, :], x_sample.rearrange("b (t p) d -> p (b t) d", p=128)).then_inc(start_in, 16)
            sp.dma_start(cond_rows[0:8, :], c_ctx.rearrange("(k p) -> k p", p=128)).then_inc(start_in, 16)
            sp.dma_start(cond_rows[8:16, :], c_lat.rearrange("b (k p) -> (b k) p", p=128)).then_inc(start_in, 16)
            sp.dma_start(cond_rows[16:24, :], final_g.rearrange("(k p) -> k p", p=128)).then_inc(start_in, 16)

            with sp.Fori(0, DEPTH) as l:
                i = 0
                def load_ada(i, n):
                    for b in range(4 * n, 4 * n + 4):
                        load_block(l, i + b % 4, rows(ada_w, l, 512 * b, 512 * b + 512))
                    return i + 4

                i = load_ada(i, 0)
                for c0, c1 in ((0, 512), (512, 1024), (1024, 1536), (1536, 2048), (C_QB, C_QB + 512),
                               (C_VB, C_VB + 512), (C_OB, C_OB + 512), (C_QC, C_QC + 512), (C_KC, C_KC + 256)):
                    if c0 == 1536:
                        i = load_ada(i, 1)
                        i = load_ada(i, 2)
                    if i == Q_BLOCK:
                        sp.wait_ge(T["ring_used"].sem, l * LAYER_BLOCKS + 1 + i)
                        dst = ring[:, (i % RING) * KT * 512:(i % RING + 1) * KT * 512]
                        dst = dst.rearrange("p (k j g c) -> p g j k c", k=KT, j=4, g=2)
                        for g in range(2):
                            for j in range(4):
                                o = c0 + 256 * g + 64 * j
                                sp.dma_start(dst[:, g, j], rows(w_in, l, o, o + 64)).then_inc(slot_in[i % RING], 16)
                    else:
                        load_block(l, i, rows(w_in, l, c0, c1))
                    i += 1
                for r, w in enumerate((w_a, w_b, w_c)):
                    load_block(l, i, rows(w, l, 0, D))
                    for h in range(2):
                        c0 = C_G + r * D + 512 * h
                        load_block(l, i + 1 + h, rows(w_in, l, c0, c0 + 512))
                    i += 3
                for h in range(2):
                    load_block(l, i, rows(w_out, l, 512 * h, 512 * h + 512))
                    i += 1
                with sp.Fori(0, NE // E_UNROLL) as eg:
                    for u in range(E_UNROLL):
                        for n, w in enumerate((w_gate, w_up, w_down)):
                            src = w[ds(l, 1), ds(eg * E_UNROLL + u, 1)].rearrange("a e (k p) n -> p (a e k) n", p=128)
                            load_block(l, i + 3 * u + n, src, eg * E_UNROLL)
            sp.wait_ge(final_act, 2)
            sp.dma_start(y_prompt.rearrange("b (t p) d -> p (b t) d", p=128), y_tok[:, 0:1, :]).then_inc(final_stored, 16)
            sp.dma_start(y_sample.rearrange("b (t p) d -> p (b t) d", p=128), y_tok[:, 1:3, :]).then_inc(final_stored, 16)
            sp.wait_ge(final_stored, 32)
            sp.wait_ge(stored, 16 * STORES * DEPTH)

        @block.gpsimd
        def _(pool):
            prime(pool, "pool")
            with pool.Fori(0, DEPTH) as l:
                count = [0, 0, 0]

                def load(dst, src, which=0, slow=False):
                    pool.sem_inc(apart["pool"], 1)
                    pool.dma_start(dst, src, allow_slow_non_contiguous=slow).then_inc((vec_in, state_in, stored)[which], 16)
                    count[which] += 1

                def bcast(dst, src):
                    load(dst, src.partition_broadcast(128) if len(src.shape) == 1 else src.broadcast_to([128] + list(src.shape[1:])))

                pool.wait_ge(T["cb_dve"].sem, T["cb_dve"].before(l))
                load(vec_row[0:48, :], ada_b[ds(l, 1)].rearrange("a (k p) -> (a k) p", p=128))
                load(vec_row[48:56, :], norm1_g[ds(l, 1)].rearrange("a (k p) -> (a k) p", p=128))
                load(vec_row[56:64, :], norm2_g[ds(l, 1)].rearrange("a (k p) -> (a k) p", p=128))
                load(vec_row[64:124, :], conv_w[ds(l, 1)].rearrange("a c (j p) -> (a c j) p", p=128))
                load(vec_row[124:125, :], delta_g[ds(l, 1)])
                for dst, src in ((a_log_b, a_log), (bias_b[:, 8:16], dt_bias), (bias_b[:, 16:24], i_bias),
                                 (bias_b[:, 24:32], f_bias)):
                    bcast(dst, src[ds(l, 1)].rearrange("a d h -> a (d h)"))
                bcast(sink_b, sink[ds(l, 1)])
                bcast(mnorm_b, mlstm_g[ds(l, 1)])
                bcast(m_state[:, 1].rearrange("p d h -> p (d h)"), state_m[:, ds(l, 1)].rearrange("b a d h -> (b a) (d h)"))
                load(w_small[:, :, 0:16], w_in[ds(l, 1), :, C_GATE_A:C_GATE_A + 16].rearrange("a (k p) n -> p (a k) n", p=128))
                load(w_small[:, :, 16:32], w_in[ds(l, 1), :, C_GATE_B:C_GATE_B + 16].rearrange("a (k p) n -> p (a k) n", p=128))
                load(w_rt, w_router[ds(l, 1)].rearrange("a (k p) n -> p (a k) n", p=128))
                for d in range(2):
                    load(states[:, 1, d], state_delta[:, ds(l, 1), d].rearrange("b a h k v -> k (b a h) v"), 1)
                for b, (tile, d, g) in enumerate(BATCHES):
                    W(pool, l, "delta_act", ("ltc", b))
                    for i, lev in enumerate(LEVELS[1:]):
                        ins = nc.gpsimd.tensor_tensor(Mb[i], LT, over(K(f"lev{1 - d}_{lev}"), 1, H), ALU.mult)
                    ins.then_inc(T["delta_pool"].mark(("m", b)), 1)
                W(pool, l, "delta_dve", ("s", NB - 1, 1))
                for d in range(2):
                    load(new_delta[:, ds(l, 1), d].rearrange("b a h k v -> k (b a h) v"), states[:, 0, d], 2)
                pool.wait_ge(stored, 16 * 2 + l * (16 * STORES))
                for d in range(2):
                    for q in range(2):
                        part = slice(64 * q, 64 * q + 64)
                        src = state_c[:, ds(l, 1), d].rearrange("b a (j q) k v -> q k (b a j) v", q=2)[q]
                        load(Cst[part, 1, d, :, 0:128], src, 1)
                        src = state_n[:, ds(l, 1), d].rearrange("b a (j q) k -> q k (b a j)", q=2)[q]
                        load(Cst[part, 1, d, :, 128:129], src.unsqueeze(2), 1, slow=True)
                W(pool, l, "ml_dve", ("h", NB - 1))
                for d in range(2):
                    for q in range(2):
                        part = slice(64 * q, 64 * q + 64)
                        dst = new_c[:, ds(l, 1), d].rearrange("b a (j q) k v -> q k (b a j) v", q=2)[q]
                        load(dst, Cst[part, 0, d, :, 0:128], 2)
                        dst = new_n[:, ds(l, 1), d].rearrange("b a (j q) k -> q k (b a j)", q=2)[q]
                        load(dst.unsqueeze(2), Cst[part, 0, d, :, 128:129], 2, slow=True)
                load(new_m[:, ds(l, 1)].rearrange("b a d h -> (b a) d h"), m_state[0:1, 0], 2)
                pool.wait_ge(stored, 16 * 11 + l * (16 * STORES))
                W(pool, l, "ml_dve", ("y", 2))
                W(pool, l, "ml_act", ("yt", 2))
                load(ck_tok, cache_k[:, ds(l, 1)].rearrange("b a p h d -> p (b a h d)"), 1)
                load(cv_tok, cache_v[:, ds(l, 1)].rearrange("b a p h d -> p (b a h d)"), 1)
                W(pool, l, "ap_dve", ("kv", 0))
                load(new_k[:, ds(l, 1)].rearrange("b a p h d -> p (b a h d)"), kv_tok[:, 0, 0:128], 2)
                load(new_v[:, ds(l, 1)].rearrange("b a p h d -> p (b a h d)"), kv_tok[:, 0, 128:256], 2)
                pool.wait_ge(stored, 16 * 13 + l * (16 * STORES))
                W(pool, l, "rt_pe", ("xs", KT - 1))
                W(pool, l, "rt_pe", ("sg", NE // 2 - 1))
                pool.sem_inc(apart["pool"], 1)
                nc.gpsimd.memset(ye[32:64], 0.0)
                nc.gpsimd.memset(ye[96:128], 0.0).then_inc(T["rt_pool"].mark("clear"), 1)
                with pool.Fori(0, NE // E_UNROLL) as eg:
                    W(pool, l, "rt_dve", ("xs", KT - 1))
                    W(pool, l, "rt_pool", "clear")
                    for u in range(E_UNROLL):
                        WB(pool, l, eg, PLAIN_BLOCKS + 3 * u + 1, 2)
                        pool.sem_inc(apart["pool"], 1)
                        nc.gpsimd.tensor_copy(xs_e[:, u % 2], xsT[:, :, ds(eg * E_UNROLL + u, 1), :].rearrange("p k a r -> p k (a r)"))\
                            .then_inc(T["ex_pool"].mark((u, "xs")), 1)
                T["ex_pool"].looped(NE // E_UNROLL, E_UNROLL)
                assert count == [VEC_LOADS, STATE_LOADS, STORES], count

        @block.tensor
        def _(pe):
            mm = nc.tensor.matmul
            ident, ones = K("ident"), K("ones")

            def tr(out, in_, n=128):
                return nc.tensor.transpose(out, in_, ident[0:n, 0:n])

            def block_view(i, kt=KT):
                return ring[:, (i % RING) * KT * 512:(i % RING + 1) * KT * 512].rearrange("p (k n) -> p k n", k=kt)

            def landed(l, i, e=None):
                whole = loads_in_slot(LAYER_BLOCKS - RING + i % RING)
                pe.wait_ge(slot_in[i % RING], l * (16 * whole) + 16 * loads_in_slot(i)
                           + (0 if e is None else e * (48 // RING)))

            def used(i):
                return T["ring_used"].mark(("block", i))

            def channels(i, c, out):
                w = block_view(i)
                for k in range(KT):
                    ins = mm(out, w[:, k, 128 * c:128 * c + 128], hT[:, k, :], start=k == 0, stop=k == KT - 1)
                return ins

            def tokens(i, t, out, c0=0, c1=512):
                w = block_view(i)
                for k in range(KT):
                    ins = mm(out, hT[:, k, 128 * t:128 * t + 128], w[:, k, c0:c1], start=k == 0, stop=k == KT - 1)
                return ins

            def column_sums(l, which):
                W(pe, l, "nrm_act", f"sq{which}")
                for k in range(KT):
                    ins = mm(PS[:, 5, 0:N], ones, norm_sq[:, k, :], start=k == 0, stop=k == KT - 1)
                ins.then_inc(T["nrm_pe"].mark(f"ss{which}"), 1)

            prime(pe, "pe")
            pe.wait_ge(start_in, 16 * 6)
            tr(PS[:, 7, 384:408], cond_rows[0:24, :], 24).then_inc(T["pre_pe"].mark("rows"), 1)
            pe.wait_ge(T["pre_act"].sem, T["pre_act"].at(0, "vec"))
            for k in range(KT):
                for t in range(TILES):
                    ins = tr(PS[:, k, 128 * t:128 * t + 128], x_tok[:, t, 128 * k:128 * k + 128])
            ins.then_inc(T["pre_pe"].mark("x"), 1)
            pe.wait_ge(T["pre_act"].sem, T["pre_act"].at(0, "x"))
            pe.wait_ge(T["pre_dve"].sem, T["pre_dve"].at(0, "x"))

            with pe.Fori(0, DEPTH) as l:
                blk = 0
                pe.wait_ge(vec_in, 16 * VEC_LOADS + l * (16 * VEC_LOADS))
                pe.wait_ge(T["cb_dve"].sem, T["cb_dve"].before(l))
                tr(PS[:, 6, 0:125], vec_row[0:125, :], 125).then_inc(T["ada_pe"].mark("vec"), 1)
                column_sums(l, 0)
                def ada_block(blk, n, bank, b):
                    landed(l, blk)
                    w = block_view(blk)
                    for k in range(KT):
                        for q in range(4):
                            ins = mm(PS[32 * q:32 * q + 2, bank, 128 * b:128 * b + 128], condT[:, 2 * k:2 * k + 2],
                                     w[:, k, 128 * q:128 * q + 128], start=k == 0, stop=k == KT - 1)
                    ins.then_inc(used(blk), 1)
                    if b == 3:
                        pe.drain().then_inc(T["ada_pe"].mark(("rows", n)), 1)
                    return blk + 1

                def ada_turn(n, bank):
                    W(pe, l, "ada_act", ("rows", n))
                    for b in range(4):
                        ins = tr(PS[:, bank, 128 * b:128 * b + 128], ada_rows[:, 128 * b:128 * b + 128])
                    ins.then_inc(T["ada_pe"].mark(("tr", n)), 1)

                for b in range(4):
                    blk = ada_block(blk, 0, 7, b)
                ada_turn(0, 7)

                W(pe, l, "nrm_act", "h0")
                for t in range(TILES):
                    for k in range(KT):
                        ins = mm(PS[:, 4, 32 * t:32 * t + 32], hT[:, k, 128 * t:128 * t + 128], w_small[:, k, :],
                                 start=k == 0, stop=k == KT - 1)
                ins.then_inc(T["gate_pe"].mark("proj"), 1)
                W(pe, l, "gate_dve", "lf")
                for t in range(TILES):
                    for d in range(2):
                        mm(PS[:, 6, 16 * t + 8 * d:16 * t + 8 * d + 8], K(f"tri{d}"), g_lf[:, t, d, :], start=True, stop=True)
                gl = g_lf.rearrange("p t d h -> p (t d h)")
                for n, m in enumerate(("block", "half0", "half1")):
                    ins = mm(PS[:, 6, 48 + 48 * n:96 + 48 * n], K(m), gl, start=True, stop=True)
                ins.then_inc(T["gate_pe"].mark("cum"), 1)

                for j in range(12):
                    if j % 4 == 0:
                        landed(l, blk)
                    if j >= 4:
                        W(pe, l, "conv_act", ("pad", j - 4))
                    ins = channels(blk, j % 4, PS[:, j % 4, 0:N])
                    ins.then_inc(T["conv_pe"].mark(("p", j)), 1)
                    if j % 4 == 3:
                        pe.drain().then_inc(used(blk), 1)
                        blk += 1
                W(pe, l, "gate_dve", "done")
                for j in range(8):
                    W(pe, l, "conv_act", ("sq", j))
                    mm(PS[:, j, 0:N], ones, (X if j % 2 else XT).rearrange("p h s -> p (h s)")[:, 0:N],
                       start=True, stop=True).then_inc(T["conv_pe"].mark(("ss", j)), 1)

                def heads_of(h):
                    return (2 * h, 2 * h + 1)

                def delta_row(b):
                    W(pe, l, "delta_dve", ("g2", b))
                    mm(PS[:, 0, :], ones, G2.rearrange("p h s -> p (h s)"), start=True, stop=True)\
                        .then_inc(T["delta_pe"].mark(("row", b)), 1)

                def delta_tok(b):
                    t = BATCHES[b][0]
                    tok = slice(128 * t, 128 * t + 128)
                    for h in range(H):
                        tr(PS[:, 1, 128 * h:128 * h + 128], qkvT[:, 4 + h, tok])
                        ins = tr(PS[:, 2, 128 * h:128 * h + 128], qkvT[:, 8 + h, tok])
                    ins.then_inc(T["delta_pe"].mark(("tok", b)), 1)

                def delta_kk(b):
                    t = BATCHES[b][0]
                    tok = slice(128 * t, 128 * t + 128)
                    for h in range(H):
                        mm(PS[:, 3, 128 * h:128 * h + 128], qkvT[:, 4 + h, tok], qkvT[:, 4 + h, tok], start=True, stop=True)
                        ins = mm(PS[:, 4, 128 * h:128 * h + 128], qkvT[:, h, tok], qkvT[:, 4 + h, tok], start=True, stop=True)
                    ins.then_inc(T["delta_pe"].mark(("kk", b)), 1)

                W(pe, l, "conv_dve", ("unit", 7))
                delta_row(0)
                delta_tok(0)
                delta_kk(0)
                for b, (t, d, g) in enumerate(BATCHES):
                    more = b + 1 < NB
                    W(pe, l, "delta_dve", ("la", b))
                    for h in range(H):
                        ins = tr(PS[:, 5, 128 * h:128 * h + 128], Lm[:, h, :])
                    ins.then_inc(T["delta_pe"].mark(("lt", b)), 1)
                    W(pe, l, "delta_pool", ("m", b))
                    for i in range(5):
                        for hf in range(2):
                            W(pe, l, "delta_dve", ("x0", b) if i == 0 else ("x", b, i - 1, hf))
                            for n, h in enumerate(heads_of(hf)):
                                ins = mm(PS[:, 6 - hf, 128 * n:128 * n + 128], Mb[i][:, h, :], X[:, h, :], start=True, stop=True)
                            ins.then_inc(T["delta_pe"].mark(("w", b, i, hf)), 1)
                        if b in ADA_IN_BATCH and i < 4:
                            blk = ada_block(blk, ADA_IN_BATCH[b], 3, i)
                        for hf in range(2):
                            W(pe, l, "delta_act", ("wc", b, i, hf))
                            for n, h in enumerate(heads_of(hf)):
                                mm(PS[:, (7, 0)[hf], 128 * n:128 * n + 128], XT[:, h, :], Wm[:, h, :], start=True, stop=True)
                                ins = mm(PS[:, (7, 0)[hf], 256 + 128 * n:384 + 128 * n], Wm[:, h, :], XT[:, h, :],
                                         start=True, stop=True)
                            ins.then_inc(T["delta_pe"].mark(("y", b, i, hf)), 1)
                    for h in range(H):
                        ins = tr(PS[:, 5, 128 * h:128 * h + 128], av[:, h, :])
                    ins.then_inc(T["delta_pe"].mark(("at", b)), 1)
                    if b in ADA_IN_BATCH:
                        ada_turn(ADA_IN_BATCH[b], 3)
                    W(pe, l, "delta_dve", ("x", b, 4, 1))
                    for h in range(H):
                        mm(PS[:, 1, 128 * h:128 * h + 128], XT[:, h, :], vb[:, h, :], start=True, stop=True)
                        ins = mm(PS[:, 2, 128 * h:128 * h + 128], kbg[:, h, :], XT[:, h, :], start=True, stop=True)
                    ins.then_inc(T["delta_pe"].mark(("uw", b)), 1)
                    W(pe, l, "delta_act", ("wtc", b))
                    W(pe, l, "delta_dve", ("u", b))
                    if b == 2:
                        pe.wait_ge(state_in, 16 * 2 + l * (16 * STATE_LOADS))
                    for c in range(2):
                        cc = c if d == 0 else 1 - c
                        ch = slice(CH * cc, CH * cc + CH)
                        S = states[:, g, d]
                        if c:
                            W(pe, l, "delta_dve", ("s", b, 0))
                        elif b:
                            W(pe, l, "delta_dve", ("s", b - 1, 1))
                        for h in range(H):
                            ins = mm(PS[ch, 5, 128 * h:128 * h + 128], wT[:, h, ch], S[:, h, :], start=True, stop=True)
                        ins.then_inc(T["delta_pe"].mark(("ws", b, c)), 1)
                        if more and c == 0:
                            delta_row(b + 1)
                            delta_tok(b + 1)
                        if more and c == 1:
                            if b in ADA_IN_BATCH:
                                W(pe, l, "ada_dve", ("mod", ADA_IN_BATCH[b]))
                            delta_kk(b + 1)
                        W(pe, l, "delta_dve", ("vn", b, c))
                        for h in range(H):
                            mm(PS[:, 6, CH * h:CH * h + CH], S[:, h, :], qd[:, h, ch], start=True, stop=False)
                            mm(PS[:, 6, CH * h:CH * h + CH], vn[ch, h, :], aT[ch, h, ch], start=False, stop=True)
                        for h in range(H):
                            ins = mm(PS[:, 7, 128 * h:128 * h + 128], kd[ch, h, :], vn[ch, h, :], start=True, stop=True)
                        ins.then_inc(T["delta_pe"].mark(("os", b, c)), 1)

                W(pe, l, "delta_dve", ("s", NB - 1, 1))
                landed(l, blk)
                for j in range(4):
                    ins = channels(blk, j, PS[:, j, 0:N])
                    ins.then_inc(T["z_pe"].mark(("z", j)), 1)
                pe.drain().then_inc(used(blk), 1)
                blk += 1
                W(pe, l, "z_act", "sq")
                for h in range(H):
                    ins = mm(PS[:, 4 + h, 0:N], ones, qkvT[:, 4 + h, :], start=True, stop=True)
                ins.then_inc(T["z_pe"].mark("ss"), 1)

                W(pe, l, "z_dve", ("y", 0))
                landed(l, blk)
                for j in range(4):
                    ins = channels(blk, j, PS[:, j, 0:N])
                    ins.then_inc(T["mp_pe"].mark(("qk", j)), 1)
                for t in range(TILES):
                    if t == 2:
                        W(pe, l, "mp_dve", ("kt", 0))
                    ins = tokens(blk, t, PS[:, 4 + t % 2, 0:256], 256, 512)
                    ins.then_inc(T["mp_pe"].mark(("kt", t)), 1)
                pe.drain().then_inc(used(blk), 1)
                blk += 1
                landed(l, blk)
                for t in range(TILES):
                    if t == 2:
                        W(pe, l, "mp_dve", ("v", 0))
                    ins = tokens(blk, t, PS[:, 6 + t % 2, :])
                    ins.then_inc(T["mp_pe"].mark(("v", t)), 1)
                pe.drain().then_inc(used(blk), 1)
                blk += 1
                landed(l, blk)
                W(pe, l, "mp_act", ("qk", 3))
                for t in range(TILES):
                    ins = tokens(blk, t, PS[:, t, :])
                    ins.then_inc(T["mp_pe"].mark(("o", t)), 1)
                pe.drain().then_inc(used(blk), 1)
                blk += 1

                W(pe, l, "mp_dve", ("v", 2))
                W(pe, l, "mp_act", ("o", 2))
                for b, (t, d, g) in enumerate(BATCHES):
                    W(pe, l, "ml_dve", ("g3", b))
                    mm(PS[:, 0, :], ones, G3.rearrange("p h s -> p (h s)"), start=True, stop=True)\
                        .then_inc(T["ml_pe"].mark(("row", b)), 1)
                    for h in range(H):
                        q, j = h % 2, h // 2
                        rows_, tok = slice(64 * q, 64 * q + 64), slice(128 * t, 128 * t + 128)
                        ins = mm(PS[:, (1, 7)[q], 128 * j:128 * j + 128], qkbT[rows_, j, tok], qkbT[rows_, 2 + j, tok],
                                 start=True, stop=True)
                    ins.then_inc(T["ml_pe"].mark(("qk", b)), 1)
                    W(pe, l, "ml_dve", ("P", b))
                    for h in range(H):
                        ins = tr(PS[:, 2, 128 * h:128 * h + 128], Pm[:, h, :])
                    ins.then_inc(T["ml_pe"].mark(("pt", b)), 1)
                    W(pe, l, "ml_act", ("ptc", b))
                    for h in range(H):
                        ins = mm(PS[:, 3 + h // 2, (h % 2) * VA:(h % 2) * VA + 129], PTm[:, h, :], v_aug[:, t, h, 0:129],
                                 start=True, stop=True)
                    ins.then_inc(T["ml_pe"].mark(("pv", b)), 1)
                    if b == 2:
                        pe.wait_ge(state_in, 16 * 10 + l * (16 * STATE_LOADS))
                    W(pe, l, "ml_dve", ("kw", b))
                    for c in range(2):
                        cc = c if d == 0 else 1 - c
                        ch = slice(CH * cc, CH * cc + CH)
                        if c:
                            W(pe, l, "ml_dve", ("c", b, 0))
                        pe.sem_inc(apart["pe"], 1)
                        for h in range(H):
                            q, j = h % 2, h // 2
                            rows_ = slice(64 * q, 64 * q + 64)
                            ins = mm(PS[ch, 5 + q, j * VA:j * VA + 129],
                                     qkbT[rows_, j, 128 * t + CH * cc:128 * t + CH * cc + CH], Cst[rows_, g, d, j, 0:129],
                                     start=True, stop=True)
                        ins.then_inc(T["ml_pe"].mark(("qc", b, c)), 1)
                        for h in range(H):
                            q, j = h % 2, h // 2
                            ins = mm(PS[64 * q:64 * q + 64, 0, j * VA:j * VA + 129], kw[ch, h, :], v_aug[ch, t, h, 0:129],
                                     start=True, stop=True)
                        ins.then_inc(T["ml_pe"].mark(("up", b, c)), 1)
                for t in range(TILES):
                    W(pe, l, "ml_dve", ("y", t))
                    for h in range(H):
                        ins = tr(PS[:, 1 + t, 128 * h:128 * h + 128], hb_tok[:, t, h, :])
                    ins.then_inc(T["ml_pe"].mark(("yt", t)), 1)

                W(pe, l, "ml_act", ("yt", 2))
                landed(l, blk)
                for j in range(4):
                    ins = channels(blk, j, PS[:, j, 0:N])
                    ins.then_inc(T["ap_pe"].mark(("q", j)), 1)
                pe.drain().then_inc(used(blk), 1)
                blk += 1
                landed(l, blk)
                channels(blk, 0, PS[:, 4, 0:N]).then_inc(T["ap_pe"].mark("k"), 1)
                for t in range(TILES):
                    ins = tokens(blk, t, PS[:, 5 + t, 0:256], 0, 256)
                    ins.then_inc(T["ap_pe"].mark(("kv", t)), 1)
                pe.drain().then_inc(used(blk), 1)
                blk += 1
                W(pe, l, "ap_act", "k")
                pe.wait_ge(state_in, 16 * STATE_LOADS + l * (16 * STATE_LOADS))
                tr(PS[:, 0, 0:PAST], ck_tok).then_inc(T["ap_pe"].mark("ckT"), 1)
                for j in range(5):
                    src = qcT[:, j, SEQ:N] if j < 4 else kcT[:, SEQ:N]
                    if j == 4:
                        W(pe, l, "ap_dve", ("kv", 2))
                    mm(PS[:, 1 + j, 0:DSEQ], K("rot"), src, start=True, stop=True)\
                        .then_inc(T["ap_pe"].mark(("rot", j)), 1)

                W(pe, l, "ap_dve", "rope")
                W(pe, l, "ap_act", "ckT")
                for u in range(6):
                    t, g = u // 2, u % 2
                    part = slice(64 * g, 64 * g + 64)
                    keys = SEQ if t == 0 else PAST + DSEQ
                    if u:
                        W(pe, l, "at_dve", ("mx", u - 1))
                    for j in range(4):
                        q = qcT[part, j, 128 * t:128 * t + 128]
                        if t == 0:
                            ins = mm(PS[:, j, 0:SEQ], q, kcT[part, 0:SEQ], start=True, stop=True)
                        else:
                            mm(PS[:, j, 0:PAST], q, ckT[part, :], start=True, stop=True)
                            ins = mm(PS[:, j, PAST:keys], q, kcT[part, SEQ:N], start=True, stop=True)
                    ins.then_inc(T["at_pe"].mark(("s", u)), 1)
                    W(pe, l, "at_act", ("e", u))
                    for m in range(3):
                        if m < keys // 128:
                            for j in range(4):
                                ins = tr(PS[:, 4 + m, 128 * j:128 * j + 128], prob[:, u % 2, j, 128 * m:128 * m + 128])
                            ins.then_inc(T["at_pe"].mark(("pt", u, m)), 1)
                        else:
                            pe.drain().then_inc(T["at_pe"].mark(("pt", u, m)), 1)
                    W(pe, l, "at_act", ("ptc", u))
                    if u:
                        W(pe, l, "at_dve", ("y", u - 1))
                        if g == 0:
                            W(pe, l, "at_act", ("yt", t - 1))
                    for j in range(4):
                        for m in range(keys // 128):
                            if t == 0:
                                v = kv_tok[:, 0, 128 + 64 * g:192 + 64 * g]
                            elif m == 0:
                                v = cv_tok[:, 64 * g:64 * g + 64]
                            else:
                                v = kv_tok[:, m, 128 + 64 * g:192 + 64 * g]
                            ins = mm(PS[:, 7, 64 * j:64 * j + 64], probT[:, u % 2, j, 128 * m:128 * m + 128], v,
                                     start=m == 0, stop=m == keys // 128 - 1)
                    ins.then_inc(T["at_pe"].mark(("pv", u)), 1)
                    if g == 1:
                        W(pe, l, "at_dve", ("y", u))
                        for j in range(4):
                            ins = tr(PS[:, 7, 128 * j:128 * j + 128], yc_tok[:, 128 * j:128 * j + 128])
                        ins.then_inc(T["at_pe"].mark(("yt", t)), 1)

                W(pe, l, "at_act", ("yt", 2))
                for r in range(3):
                    for c in range(KT):
                        n = r * KT + c
                        if c == 0:
                            landed(l, blk)
                        if c % 4 == 0:
                            landed(l, blk + 1 + c // 4)
                        if n >= 2:
                            W(pe, l, "mix_dve", ("m", (n - 2) // KT, (n - 2) % KT))
                        channels(blk + 1 + c // 4, c % 4, PS[:, n % 2, 0:N]).then_inc(T["mix_pe"].mark(("g", r, c)), 1)
                        w = block_view(blk, 4)
                        for k in range(4):
                            ins = mm(PS[:, 2 + n % 2, 0:N], w[:, k, 128 * c:128 * c + 128], yT[r][:, k, :],
                                     start=k == 0, stop=k == 3)
                        ins.then_inc(T["mix_pe"].mark(("y", r, c)), 1)
                    for _ in range(3):
                        pe.drain().then_inc(used(blk), 1)
                        blk += 1
                W(pe, l, "mix_dve", ("m", 2, KT - 1))
                for c in range(KT):
                    if c % 4 == 0:
                        landed(l, blk)
                    if c >= 4:
                        W(pe, l, "mix_dve", ("x", c - 4))
                    w = block_view(blk)
                    for k in range(KT):
                        ins = mm(PS[:, 4 + c % 4, 0:N], w[:, k, 128 * (c % 4):128 * (c % 4) + 128], mixT[:, k, :],
                                 start=k == 0, stop=k == KT - 1)
                    ins.then_inc(T["mix_pe"].mark(("o", c)), 1)
                    if c % 4 == 3:
                        pe.drain().then_inc(used(blk), 1)
                        blk += 1

                column_sums(l, 1)
                W(pe, l, "nrm_act", "h1")
                for t in range(TILES):
                    for k in range(KT):
                        ins = mm(PS[:, 7, 16 * t:16 * t + 16], hT[:, k, 128 * t:128 * t + 128], w_rt[:, k, :],
                                 start=k == 0, stop=k == KT - 1)
                ins.then_inc(T["rt_pe"].mark("logit"), 1)
                W(pe, l, "rt_dve", "aff")
                mm(PS[:, 7, 64:64 + TILES * NE], ident, aff.rearrange("p t e -> p (t e)"), start=True, stop=True)\
                    .then_inc(T["rt_pe"].mark("affx"), 1)
                for t in range(TILES):
                    W(pe, l, "rt_dve", ("diag", t))
                    if t:
                        W(pe, l, "rt_dve", ("rank", t - 1))
                    for n in range(4):
                        ins = mm(PS[:, n, :], ones, diag[:, 4 * n:4 * n + 4, :].rearrange("p e s -> p (e s)"),
                                 start=True, stop=True)
                    ins.then_inc(T["rt_pe"].mark(("R", t)), 1)
                for t in range(TILES):
                    for u in range(2):
                        if 2 * t + u >= 2:
                            W(pe, l, "rt_act", ("ht", (2 * t + u - 2) // 2, u))
                        for k in range(4):
                            ins = tr(PS[:, 5 + u, 128 * k:128 * k + 128], hT[:, 4 * u + k, 128 * t:128 * t + 128])
                        ins.then_inc(T["rt_pe"].mark(("ht", t, u)), 1)
                W(pe, l, "rt_dve", "sel")
                W(pe, l, "rt_act", ("ht", 2, 1))
                for j in range(NE // 2):
                    if j >= 2:
                        W(pe, l, "rt_dve", ("sg", j - 2))
                    for t in range(TILES):
                        ins = tr(PS[:, j % 2, 128 * t:128 * t + 128], selG[:, t, 2 * j:2 * j + 2, :].rearrange("p e s -> p (e s)"))
                    ins.then_inc(T["rt_pe"].mark(("sg", j)), 1)
                for k in range(KT):
                    if k >= 2:
                        W(pe, l, "rt_dve", ("xs", k - 2))
                    for t in (1, 2):
                        mm(PS[:, 2 + k % 2, :], h_tok[:, t, 128 * k:128 * k + 128], sel[:, t, :, 0:CAP_S],
                           start=t == 1, stop=t == 2)
                    ins = mm(PS[:, 4 + k % 2, 0:NE * CAP_P], h_tok[:, 0, 128 * k:128 * k + 128], sel[:, 0, :, CAP_S:ROWS],
                             start=True, stop=True)
                    ins.then_inc(T["rt_pe"].mark(("xs", k)), 1)

                base_blk = blk
                with pe.Fori(0, NE // E_UNROLL) as eg:
                    W(pe, l, "rt_dve", ("xs", KT - 1))
                    for u in range(E_UNROLL):
                        gu = base_blk + 3 * u
                        WE(pe, l, eg, "ex_pool", (u, "xs"))
                        landed(l, gu, eg * E_UNROLL)
                        landed(l, gu + 1, eg * E_UNROLL)
                        for k in range(KT):
                            for n in range(2):
                                ins = mm(PS[64 * n:64 * n + ROWS, u % 2, :],
                                         xs_e[:, u % 2, k, :],
                                         block_view(gu + n)[:, k, :], start=k == 0, stop=k == KT - 1)
                                if k == KT - 1:
                                    ins.then_inc(used(gu + n), 1)
                        WE(pe, l, eg, "ex_dve", (u, "hid"))
                        pe.sem_inc(apart["pe"], 1)
                        for f in range(4):
                            ins = tr(PS[:, 2 + u % 2, ROWS * f:ROWS * f + ROWS], hid[0:ROWS, u % 2, 128 * f:128 * f + 128], ROWS)
                        ins.then_inc(T["ex_pe"].mark((u, "t")), 1)
                        landed(l, gu + 2, eg * E_UNROLL)
                        WE(pe, l, eg, "ex_act", (u, "ht"))
                        WE(pe, l, eg, "ex_dve", (u, "d"), 2)
                        WE(pe, l, eg, "ex_act", (u, "d"), 2)
                        for f in range(4):
                            for n in range(2):
                                ins = mm(PS[64 * n:64 * n + ROWS, 4 + u % 2, :], hidT[:, u % 2, f, :],
                                         block_view(gu + 2, 4)[:, f, 512 * n:512 * n + 512], start=f == 0, stop=f == 3)
                        ins.then_inc(used(gu + 2), 1)
                T["ring_used"].looped(NE // E_UNROLL, 3 * E_UNROLL)
                T["ex_pe"].looped(NE // E_UNROLL, E_UNROLL)

                W(pe, l, "ex_dve", (NE - 1, "d"))
                W(pe, l, "ex_act", (NE - 1, "d"))
                W(pe, l, "rt_pool", "clear")
                for k in range(KT):
                    if k >= 4:
                        W(pe, l, "cb_dve", ("x", k - 4))
                    for j in range(NE // 2):
                        ins = mm(PS[:, k % 4, 0:N], ye[:, j, 128 * k:128 * k + 128], selGT[:, j, :],
                                 start=j == 0, stop=j == NE // 2 - 1)
                    ins.then_inc(T["cb_pe"].mark(("x", k)), 1)

            pe.wait_ge(final_dve, 1)
            for k in range(KT):
                ins = mm(PS[:, 5, 0:N], ones, norm_sq[:, k, :], start=k == 0, stop=k == KT - 1)
            ins.then_inc(final_pe, 1)
            pe.wait_ge(final_dve, 2)
            for t in range(TILES):
                for u in range(2):
                    for k in range(4):
                        ins = tr(PS[:, 2 * t + u if t < 2 else 6 + u, 128 * k:128 * k + 128], hT[:, 4 * u + k, 128 * t:128 * t + 128])
            ins.then_inc(final_pe, 1)

        @block.scalar
        def _(act):
            f = nc.scalar.activation
            flat = lambda v: v.rearrange("p h s -> p (h s)")

            def copy(out, in_):
                return f(out, in_, ACT.Copy)

            def ada_out(n, bank):
                W(act, l, "ada_pe", ("rows", n))
                if n:
                    W(act, l, "ada_pe", ("tr", n - 1))
                for q in range(4):
                    ins = copy(ada_rows[32 * q:32 * q + 2, :], PS[32 * q:32 * q + 2, bank, :])
                ins.then_inc(T["ada_act"].mark(("rows", n)), 1)

            def norm(l, which, sh, a):
                if which == 0:
                    act.wait_ge(T["cb_dve"].sem, T["cb_dve"].before(l))
                else:
                    W(act, l, "mix_dve", ("x", KT - 1))
                    W(act, l, "mix_pe", ("o", KT - 1))
                f(norm_sq, xT, ACT.Square).then_inc(T["nrm_act"].mark(f"sq{which}"), 1)
                W(act, l, "nrm_pe", f"ss{which}")
                f(rstd[:, :], PS[:, 5, 0:N], ACT.Sqrt, bias=EPS, scale=1.0 / D).then_inc(T["nrm_act"].mark(f"sqrt{which}"), 1)
                if which == 0:
                    ada_out(0, 7)
                W(act, l, "nrm_dve", f"xn{which}")
                W(act, l, "ada_dve", ("mod", which * 2))
                for k in range(KT):
                    for g, a0, a1 in GROUPS:
                        n = 2 * (KT * which + k) + g
                        ins = f(hT[:, k, a0:a1], hT[:, k, a0:a1], ACT.Identity, bias=mod[:, sh + k, g:g + 1],
                                scale=affine[:, n:n + 1])
                ins.then_inc(T["nrm_act"].mark(f"h{which}"), 1)

            prime(act, "act")
            act.wait_ge(T["pre_pe"].sem, T["pre_pe"].at(0, "rows"))
            f(condT[:, :].rearrange("p (k v) -> p v k", v=2), PS[:, 7, 384:400].rearrange("p (v k) -> p v k", v=2), ACT.Silu)
            copy(fin_g[:, :], PS[:, 7, 400:408]).then_inc(T["pre_act"].mark("vec"), 1)
            act.wait_ge(T["pre_pe"].sem, T["pre_pe"].at(0, "x"))
            copy(xT[:, 0:4, :], PS[:, 0:4, 0:N]).then_inc(T["pre_act"].mark("x"), 1)
            act.wait_ge(T["pre_dve"].sem, T["pre_dve"].at(0, "x"))
            act.drain()

            with act.Fori(0, DEPTH) as l:
                W(act, l, "ada_pe", "vec")
                copy(vecT[:, 0:125], PS[:, 6, 0:125]).then_inc(T["ada_act"].mark("vec"), 1)
                act.wait_ge(vec_in, 16 * VEC_LOADS + l * (16 * VEC_LOADS))
                f(neg_rate, a_log_b, ACT.Exp).then_inc(T["ada_act"].mark("rate"), 1)
                norm(l, 0, 0, 0)

                W(act, l, "gate_dve", "biased")
                f(gates[:, :, 0:8], gates[:, :, 0:8], ACT.Exp, scale=-1.0)
                f(soft, soft, ACT.Exp, scale=-1.0)
                act.drain().then_inc(T["gate_act"].mark("exp"), 1)
                f(soft, soft, ACT.Ln, bias=1.0).then_inc(T["gate_act"].mark("ln"), 1)
                W(act, l, "gate_dve", "args")
                f(e_cum, cum[:, :, :, 0:H], ACT.Exp)
                for c in range(2):
                    f(e_chunk[:, c], chunk_tot[:, c, :, :, 0:H], ACT.Exp)
                f(kd_f, kd_f, ACT.Exp).then_inc(T["gate_act"].mark("ecum"), 1)

                for j in range(13):
                    if j < 12:
                        W(act, l, "conv_pe", ("p", j))
                        if j >= 4:
                            W(act, l, "conv_dve", ("conv", j - 4))
                        copy(pads[:, j % 4, 2:2 + SEQ], PS[:, j % 4, 0:SEQ])
                        copy(pads[:, j % 4, 6 + SEQ:6 + N], PS[:, j % 4, SEQ:N]).then_inc(T["conv_act"].mark(("pad", j)), 1)
                    if j:
                        W(act, l, "conv_dve", ("conv", j - 1))
                        f(qkvT[:, j - 1, 0:SEQ], acc[:, (j - 1) % 2, 0:SEQ], ACT.Silu)
                        f(qkvT[:, j - 1, SEQ:N], acc[:, (j - 1) % 2, SEQ + 4:N + 4], ACT.Silu)\
                            .then_inc(T["conv_act"].mark(("silu", j - 1)), 1)
                act.drain()
                for j in range(8):
                    if j >= 2:
                        W(act, l, "conv_pe", ("ss", j - 2))
                    f((X if j % 2 else XT).rearrange("p h s -> p (h s)")[:, 0:N], qkvT[:, j, :], ACT.Square)\
                        .then_inc(T["conv_act"].mark(("sq", j)), 1)
                for j in range(8):
                    W(act, l, "conv_pe", ("ss", j))
                    if j == 0:
                        W(act, l, "conv_dve", ("conv", 11))
                    if j >= 2:
                        W(act, l, "conv_dve", ("unit", j - 2))
                    s = 128.0 if j < 4 else 1.0
                    f(nrm[:, j % 2, 0:N], PS[:, j, 0:N], ACT.Sqrt, bias=EPS * s, scale=s).then_inc(T["conv_act"].mark(("root", j)), 1)

                def delta_decay(b):
                    W(act, l, "delta_dve", ("d", b))
                    f(flat(er), PS[:, 0, :], ACT.Exp).then_inc(T["delta_act"].mark(("er", b)), 1)
                    f(flat(dec), flat(dec), ACT.Exp, scale=-1.0).then_inc(T["delta_act"].mark(("dec", b)), 1)

                delta_decay(0)
                for b in range(NB):
                    W(act, l, "delta_pe", ("lt", b))
                    copy(flat(LT), PS[:, 5, :]).then_inc(T["delta_act"].mark(("ltc", b)), 1)
                    for i in range(5):
                        for hf in range(2):
                            W(act, l, "delta_pe", ("w", b, i, hf))
                            copy(flat(Wm)[:, 256 * hf:256 * hf + 256], PS[:, 6 - hf, 0:256])\
                                .then_inc(T["delta_act"].mark(("wc", b, i, hf)), 1)
                    if b in ADA_IN_BATCH:
                        ada_out(ADA_IN_BATCH[b], 3)
                    W(act, l, "delta_pe", ("at", b))
                    copy(flat(aT), PS[:, 5, :]).then_inc(T["delta_act"].mark(("atc", b)), 1)
                    W(act, l, "delta_pe", ("uw", b))
                    copy(flat(wT), PS[:, 2, :]).then_inc(T["delta_act"].mark(("wtc", b)), 1)
                    if b + 1 < NB:
                        delta_decay(b + 1)

                for j in range(4):
                    W(act, l, "z_pe", ("z", j))
                    f(qkvT[:, j, :], PS[:, j, 0:N], ACT.Silu).then_inc(T["z_act"].mark(("z", j)), 1)
                f(qkvT[:, 4:8, :], yT[0], ACT.Square).then_inc(T["z_act"].mark("sq"), 1)
                W(act, l, "z_pe", "ss")
                f(qkvT[:, 4:8, :], PS[:, 4:8, 0:N], ACT.Sqrt, bias=EPS, scale=1.0 / 128).then_inc(T["z_act"].mark("root"), 1)

                for j in range(4):
                    W(act, l, "mp_pe", ("qk", j))
                    f(qkbT[:, j, :], PS[:, j, 0:N], ACT.Copy, scale=1.0 if j < 2 else DKB ** -0.5)\
                        .then_inc(T["mp_act"].mark(("qk", j)), 1)
                for t in range(TILES):
                    W(act, l, "mp_pe", ("o", t))
                    f(ob_s[:, t, :], PS[:, t, :], ACT.Sigmoid).then_inc(T["mp_act"].mark(("o", t)), 1)

                for b in range(NB):
                    W(act, l, "ml_dve", ("args", b))
                    f(exps, args_b, ACT.Exp).then_inc(T["ml_act"].mark(("ex", b)), 1)
                    f(flat(Em), flat(Em), ACT.Exp).then_inc(T["ml_act"].mark(("E", b)), 1)
                    W(act, l, "ml_pe", ("pt", b))
                    copy(flat(PTm), PS[:, 2, :]).then_inc(T["ml_act"].mark(("ptc", b)), 1)
                W(act, l, "ml_dve", "ss")
                f(stab[:, 0:12], stab[:, 0:12], ACT.Sqrt, bias=EPS, scale=1.0 / 128).then_inc(T["ml_act"].mark("root"), 1)
                for t in range(TILES):
                    W(act, l, "ml_pe", ("yt", t))
                    copy(yT[1][:, :, 128 * t:128 * t + 128], PS[:, 1 + t, :].rearrange("p (h s) -> p h s", h=4))\
                        .then_inc(T["ml_act"].mark(("yt", t)), 1)

                for j in range(4):
                    W(act, l, "ap_pe", ("q", j))
                    f(qcT[:, j, :], PS[:, j, 0:N], ACT.Copy, scale=DC ** -0.5).then_inc(T["ap_act"].mark(("q", j)), 1)
                W(act, l, "ap_pe", "k")
                copy(kcT, PS[:, 4, 0:N]).then_inc(T["ap_act"].mark("k"), 1)
                W(act, l, "ap_pe", "ckT")
                copy(ckT, PS[:, 0, 0:PAST]).then_inc(T["ap_act"].mark("ckT"), 1)

                for u in range(6):
                    t, g = u // 2, u % 2
                    keys = SEQ if t == 0 else PAST + DSEQ
                    W(act, l, "at_dve", ("mx", u))
                    for j in range(4):
                        f(prob[:, u % 2, j, 0:keys], prob[:, u % 2, j, 0:keys], ACT.Exp, bias=nmax[:, u % 2, j:j + 1],
                          accum_out=sums[:, u % 2, j:j + 1])
                    f(esink[:, u % 2, :], esink[:, u % 2, :], ACT.Exp).then_inc(T["at_act"].mark(("e", u)), 1)
                    for m in range(keys // 128):
                        W(act, l, "at_pe", ("pt", u, m))
                        ins = copy(probT[:, u % 2, :, 128 * m:128 * m + 128],
                                   PS[:, 4 + m, :].rearrange("p (j s) -> p j s", j=4))
                    ins.then_inc(T["at_act"].mark(("ptc", u)), 1)
                    if g == 1:
                        W(act, l, "at_pe", ("yt", t))
                        copy(yT[2][:, :, 128 * t:128 * t + 128], PS[:, 7, :].rearrange("p (j s) -> p j s", j=4))\
                            .then_inc(T["at_act"].mark(("yt", t)), 1)

                for r in range(3):
                    for c in range(KT):
                        n = r * KT + c
                        W(act, l, "mix_pe", ("g", r, c))
                        if n >= 2:
                            W(act, l, "mix_dve", ("m", (n - 2) // KT, (n - 2) % KT))
                        f(sig[:, n % 2, :], PS[:, n % 2, 0:N], ACT.Sigmoid).then_inc(T["mix_act"].mark(("sig", r, c)), 1)
                norm(l, 1, 24, 1)

                W(act, l, "rt_dve", "max")
                f(aff, logit, ACT.Exp).then_inc(T["rt_act"].mark("exp"), 1)
                for t in range(TILES):
                    for u in range(2):
                        W(act, l, "rt_pe", ("ht", t, u))
                        copy(h_tok[:, t, 512 * u:512 * u + 512], PS[:, 5 + u, :]).then_inc(T["rt_act"].mark(("ht", t, u)), 1)

                with act.Fori(0, NE // E_UNROLL) as eg:
                    W(act, l, "rt_pool", "clear")
                    for u in range(E_UNROLL):
                        gu = PLAIN_BLOCKS + 3 * u
                        WB(act, l, eg, gu + 1)
                        f(silu_g[64:64 + ROWS], PS[0:ROWS, u % 2, :], ACT.Silu).then_inc(T["ex_act"].mark((u, "silu")), 1)
                        WE(act, l, eg, "ex_pe", (u, "t"))
                        copy(hidT[:, u % 2].rearrange("p f r -> p (f r)"), PS[:, 2 + u % 2, 0:4 * ROWS])\
                            .then_inc(T["ex_act"].mark((u, "ht")), 1)
                        WB(act, l, eg, gu + 2)
                        o = SLOT_E * (u % 2)
                        dst = ye[o:o + ROWS, ds(eg * (E_UNROLL // 2) + u // 2, 1), 0:512].rearrange("p a n -> p (a n)")
                        copy(dst, PS[0:ROWS, 4 + u % 2, :]).then_inc(T["ex_act"].mark((u, "d")), 1)
                T["ex_act"].looped(NE // E_UNROLL, 3 * E_UNROLL)

            act.wait_ge(final_pe, 1)
            f(rstd[:, :], PS[:, 5, 0:N], ACT.Sqrt, bias=EPS, scale=1.0 / D).then_inc(final_act, 1)
            act.wait_ge(final_pe, 2)
            for t in range(TILES):
                for u in range(2):
                    ins = copy(y_tok[:, t, 512 * u:512 * u + 512], PS[:, 2 * t + u if t < 2 else 6 + u, :])
            ins.then_inc(final_act, 1)

        @block.vector
        def _(v):
            V = nc.vector
            TT, TS, STT, RED = V.tensor_tensor, V.tensor_scalar, V.scalar_tensor_tensor, V.tensor_reduce
            flat = lambda a: a.rearrange("p h s -> p (h s)")

            def heads(bank):
                return PS[:, bank, :].rearrange("p (h s) -> p h s", h=H)

            def norm(l, which):
                W(v, l, "nrm_act", f"sqrt{which}")
                V.reciprocal(rstd[:, :], rstd[:, :]).then_inc(T["nrm_dve"].mark(f"rstd{which}"), 1)
                v.drain()
                TT(hT, xT, over(rstd[:, :], 1, KT), ALU.mult).then_inc(T["nrm_dve"].mark(f"xn{which}"), 1)

            prime(v, "dve")
            V.memset(ada_rows[:, :], 0.0)
            V.memset(bias_b[:, 0:8], 0.0).then_inc(T["pre_dve"].mark("clear"), 1)
            v.wait_ge(T["pre_pe"].sem, T["pre_pe"].at(0, "x"))
            V.tensor_copy(xT[:, 4:8, :], PS[:, 4:8, 0:N]).then_inc(T["pre_dve"].mark("x"), 1)
            v.wait_ge(T["pre_act"].sem, T["pre_act"].at(0, "x"))
            v.drain()

            with v.Fori(0, DEPTH) as l:
                V.memset(pads, 0.0)
                norm(l, 0)

                def ada_mod(n, bank):
                    W(v, l, "ada_pe", ("tr", n))
                    out = mod[:, 16 * n:16 * n + 16, :].rearrange("p (b q) v -> p b q v", q=4)
                    src = PS[:, bank, :].rearrange("p (b q r) -> p b q r", b=4, q=4)[:, :, :, 0:2]
                    for g in range(2):
                        ins = TT(out[:, :, :, g], src[:, :, :, g],
                                 vecT[:, 16 * n:16 * n + 16].rearrange("p (b q) -> p b q", q=4), ALU.add)
                    if n == 1:
                        ins.then_inc(T["ada_dve"].mark(("mod", n)), 1)
                        return
                    v.drain()
                    m = n // 2
                    STT(affine[:, 16 * m:16 * m + 16].rearrange("p (k v) -> p k v", v=2),
                        mod[:, 24 * m + 8:24 * m + 16, :], 1.0, over(vecT[:, 48 + 8 * m:56 + 8 * m], 2, 2),
                        ALU.add, ALU.mult).then_inc(T["ada_dve"].mark(("mod", n)), 1)

                W(v, l, "ada_act", "vec")
                ada_mod(0, 7)

                W(v, l, "gate_pe", "proj")
                TT(gates, PS[:, 4, 0:96].rearrange("p (t c) -> p t c", c=32), over(bias_b, 1, TILES), ALU.add)
                v.drain()
                STT(soft, gates, -1.0, gates, ALU.mult, ALU.max).then_inc(T["gate_dve"].mark("biased"), 1)
                W(v, l, "gate_act", "ln")
                W(v, l, "ada_act", "rate")
                TS(beta, gates[:, :, 0:8], 1.0, None, ALU.add)
                for d in range(2):
                    STT(g_lf[:, :, d, 0:H], gates[:, :, 8 + 4 * d:12 + 4 * d], 0.0, soft[:, :, 8 + 4 * d:12 + 4 * d],
                        ALU.max, ALU.add)
                    STT(g_lf[:, :, d, H:2 * H], gates[:, :, 24 + 4 * d:28 + 4 * d], 0.0, soft[:, :, 24 + 4 * d:28 + 4 * d],
                        ALU.min, ALU.subtract)
                v.drain()
                V.reciprocal(beta, beta)
                for d in range(2):
                    ins = STT(g_lf[:, :, d, 0:H], g_lf[:, :, d, 0:H], -1.0, over(neg_rate[:, 4 * d:4 * d + 4], 1, TILES),
                              ALU.mult, ALU.mult)
                ins.then_inc(T["gate_dve"].mark("lf"), 1)
                W(v, l, "gate_pe", "cum")
                V.tensor_copy(cum.rearrange("p t d h -> p (t d h)"), PS[:, 6, 0:48])
                V.tensor_copy(tot.rearrange("p t d h -> p (t d h)"), PS[:, 6, 48:96])
                V.tensor_copy(chunk_tot.rearrange("p c t d h -> p (c t d h)"), PS[:, 6, 96:192])
                v.drain()
                TT(kd_f, tot[:, :, :, 0:H], cum[:, :, :, 0:H], ALU.subtract)
                TT(rcol, gates[:, :, 16:24].rearrange("p t (d h) -> p t d h", d=2), cum[:, :, :, H:2 * H], ALU.subtract)\
                    .then_inc(T["gate_dve"].mark("args"), 1)
                W(v, l, "gate_act", "ecum")
                TT(kbg_f, beta.rearrange("p t (d h) -> p t d h", d=2), e_cum, ALU.mult)\
                    .then_inc(T["gate_dve"].mark("done"), 1)

                for j in range(12):
                    W(v, l, "conv_act", ("pad", j))
                    if j >= 2:
                        W(v, l, "conv_act", ("silu", j - 2))
                    o = acc[:, j % 2, :]
                    for k in range(CONV_K):
                        x = pads[:, j % 4, k:k + PADW - 4]
                        n = 64 + 12 * k + j
                        if k == 0:
                            ins = TS(o, x, vecT[:, n:n + 1], None, ALU.mult)
                        else:
                            ins = STT(o, x, vecT[:, n:n + 1], o, ALU.mult, ALU.add)
                        if k < CONV_K - 1:
                            v.drain()
                    ins.then_inc(T["conv_dve"].mark(("conv", j)), 1)
                for j in range(8):
                    W(v, l, "conv_act", ("root", j))
                    V.reciprocal(nrm[:, j % 2, 0:N], nrm[:, j % 2, 0:N])
                    v.drain()
                    TT(qkvT[:, j, :], qkvT[:, j, :], nrm[:, j % 2, 0:N], ALU.mult).then_inc(T["conv_dve"].mark(("unit", j)), 1)

                D_ = T["delta_dve"]

                def delta_g2(b):
                    t, d, g = BATCHES[b]
                    TT(G2, over(K(f"tri{d}"), 1, H), over(g_lf[:, t, d, 0:H], 2, 128), ALU.mult).then_inc(D_.mark(("g2", b)), 1)

                def delta_d(b):
                    t, d, g = BATCHES[b]
                    W(v, l, "delta_pe", ("row", b))
                    for h in range(H):
                        ins = TS(dec[:, h, :], PS[:, 0, 128 * h:128 * h + 128], cum[:, t, d, h:h + 1], 0.0, ALU.subtract, ALU.max)
                    ins.then_inc(D_.mark(("d", b)), 1)

                def delta_vk(b):
                    t, d, g = BATCHES[b]
                    W(v, l, "delta_pe", ("tok", b))
                    TT(vb, heads(2), over(beta[:, t, 4 * d:4 * d + 4], 2, 128), ALU.mult)
                    TT(kbg, heads(1), over(kbg_f[:, t, d, :], 2, 128), ALU.mult).then_inc(D_.mark(("vk", b)), 1)

                def delta_la(b):
                    t, d, g = BATCHES[b]
                    tok = slice(128 * t, 128 * t + 128)
                    W(v, l, "delta_act", ("er", b))
                    TT(qd, qkvT[:, 0:4, tok], er, ALU.mult)
                    TT(kd, heads(1), over(kd_f[:, t, d, :], 2, 128), ALU.mult).then_inc(D_.mark(("qk", b)), 1)
                    W(v, l, "delta_act", ("dec", b))
                    TT(dstr, dec, over(K(f"strict{d}"), 1, H), ALU.mult)
                    TT(dinc, dec, over(K(f"tri{1 - d}"), 1, H), ALU.mult)
                    v.drain()
                    W(v, l, "delta_pe", ("kk", b))
                    for h in range(H):
                        STT(Lm[:, h, :], PS[:, 3, 128 * h:128 * h + 128], beta[:, t, 4 * d + h:4 * d + h + 1], dstr[:, h, :],
                            ALU.mult, ALU.mult)
                    TT(av, heads(4), dinc, ALU.mult).then_inc(D_.mark(("la", b)), 1)

                for d in range(2):
                    V.memset(states[:, 0, d], 0.0)
                delta_g2(0)
                delta_d(0)
                delta_vk(0)
                delta_la(0)
                for b, (t, d, g) in enumerate(BATCHES):
                    more = b + 1 < NB
                    v.drain()
                    TT(X, Lm, over(K(f"lev{d}_1"), 1, H), ALU.mult)
                    W(v, l, "delta_act", ("ltc", b))
                    TT(XT, LT, over(K(f"lev{1 - d}_1"), 1, H), ALU.mult)
                    v.drain()
                    TT(X, over(K("ident"), 1, H), X, ALU.subtract)
                    TT(XT, over(K("ident"), 1, H), XT, ALU.subtract).then_inc(D_.mark(("x0", b)), 1)
                    for i in range(5):
                        for hf in range(2):
                            v.drain()
                            W(v, l, "delta_pe", ("y", b, i, hf))
                            two = slice(2 * hf, 2 * hf + 2)
                            y = PS[:, (7, 0)[hf], :].rearrange("p (m h s) -> p m h s", m=2, h=2)
                            TT(X[:, two], X[:, two], y[:, 0], ALU.subtract)
                            TT(XT[:, two], XT[:, two], y[:, 1], ALU.subtract).then_inc(D_.mark(("x", b, i, hf)), 1)
                    W(v, l, "delta_pe", ("uw", b))
                    V.tensor_copy(flat(uv), PS[:, 1, :]).then_inc(D_.mark(("u", b)), 1)
                    if b in ADA_IN_BATCH:
                        ada_mod(ADA_IN_BATCH[b], 3)
                    if more:
                        delta_g2(b + 1)
                    v.drain()
                    if b == 2:
                        v.wait_ge(state_in, 16 * 2 + l * (16 * STATE_LOADS))
                    for c in range(2):
                        cc = c if d == 0 else 1 - c
                        ch = slice(CH * cc, CH * cc + CH)
                        S = states[:, g, d]
                        W(v, l, "delta_pe", ("ws", b, c))
                        TT(vn[ch], uv[ch], PS[ch, 5, :].rearrange("p (h s) -> p h s", h=H), ALU.subtract)\
                            .then_inc(D_.mark(("vn", b, c)), 1)
                        TT(Sd, S, over(e_chunk[:, cc, t, d, :], 2, 128), ALU.mult)
                        if more:
                            (delta_d, delta_vk)[c](b + 1)
                        v.drain()
                        W(v, l, "delta_pe", ("os", b, c))
                        o = yT[0][:, :, 128 * t + CH * cc:128 * t + CH * cc + CH]
                        po = PS[:, 6, 0:H * CH].rearrange("p (h s) -> p h s", h=H)
                        if d == 0:
                            V.tensor_copy(o, po)
                        else:
                            TT(o, o, po, ALU.add)
                        TT(S, Sd, heads(7), ALU.add).then_inc(D_.mark(("s", b, c)), 1)
                        v.drain()
                    if more:
                        delta_la(b + 1)

                W(v, l, "z_act", "root")
                V.reciprocal(qkvT[:, 4:8, :], qkvT[:, 4:8, :]).then_inc(T["z_dve"].mark("root"), 1)
                TS(yT[0], yT[0], vecT[:, 124:125], None, ALU.mult)
                v.drain()
                TT(yT[0], yT[0], qkvT[:, 4:8, :], ALU.mult)
                v.drain()
                TT(yT[0], yT[0], qkvT[:, 0:4, :], ALU.mult).then_inc(T["z_dve"].mark(("y", 0)), 1)

                v.drain()
                V.memset(v_aug[:, :, :, 128:129], 1.0)
                V.memset(m_state[:, 0], 0.0)
                W(v, l, "delta_pe", ("os", NB - 1, 1))
                v.wait_ge(stored, 16 * 2 + l * (16 * STORES))
                V.memset(Cst[:, 0], 0.0).then_inc(T["mp_dve"].mark("ones"), 1)
                for t in range(TILES):
                    W(v, l, "mp_pe", ("kt", t))
                    TS(kb_tok[:, t, :], PS[:, 4 + t % 2, 0:256], DKB ** -0.5, None, ALU.mult).then_inc(T["mp_dve"].mark(("kt", t)), 1)
                for t in range(TILES):
                    W(v, l, "mp_pe", ("v", t))
                    V.tensor_copy(v_aug[:, t, :, 0:128], heads(6 + t % 2)).then_inc(T["mp_dve"].mark(("v", t)), 1)
                v.drain()

                for b, (t, d, g) in enumerate(BATCHES):
                    D_ = T["ml_dve"]
                    TT(G3, over(K("ident"), 1, H), over(gates[:, t, 16 + 4 * d:20 + 4 * d], 2, 128), ALU.mult)
                    TT(g3b, over(K(f"tri{d}"), 1, H), over(g_lf[:, t, d, H:2 * H], 2, 128), ALU.mult)
                    v.drain()
                    TT(G3, G3, g3b, ALU.subtract).then_inc(D_.mark(("g3", b)), 1)
                    W(v, l, "ml_pe", ("row", b))
                    RED(mx, PS[:, 0, :].rearrange("p (a s) -> p a s", s=CH), AX, ALU.max)
                    TT(Rm, heads(0), over(K(f"neg{d}"), 1, H), ALU.add)
                    v.drain()
                    RED(dmx, Rm, AX, ALU.max)
                    c0, c1 = (0, 1) if d == 0 else (1, 0)
                    m0 = m_state[:, g, d]
                    cm = [chunk_tot[:, c, t, d, H:2 * H] for c in range(2)]
                    mm0, m1, mm1, mprev, mmx, mr = (stab[:, 16 + 4 * n:20 + 4 * n] for n in range(6))
                    if b == 2:
                        v.wait_ge(vec_in, 16 * VEC_LOADS + l * (16 * VEC_LOADS))
                    TT(mm0, m0, mx[:, :, c0], ALU.max)
                    v.drain()
                    TT(m1, mm0, cm[c0], ALU.add)
                    v.drain()
                    TT(mm1, m1, mx[:, :, c1], ALU.max)
                    for c, mp, mq in ((c0, m0, mm0), (c1, m1, mm1)):
                        ch = slice(CH * c, CH * c + CH)
                        V.tensor_copy(mprev[ch], mp[ch])
                        if c == c1:
                            v.drain()
                        V.tensor_copy(mmx[ch], mq[ch])
                    v.drain()
                    TT(mr, mprev, dmx, ALU.max)
                    TT(args_b[:, 3, :], m0, mm0, ALU.subtract)
                    TT(args_b[:, 4, :], m1, mm1, ALU.subtract)
                    TT(args_b[:, 1, :], rcol[:, t, d, :], mmx, ALU.subtract)
                    v.drain()
                    TT(m0, mm1, cm[c1], ALU.add)
                    TT(args_b[:, 0, :], mprev, mr, ALU.subtract)
                    TT(Em, Rm, over(mr, 2, 128), ALU.subtract)
                    TT(args_b[:, 2, :], cum[:, t, d, H:2 * H], mr, ALU.add)
                    v.drain()
                    TS(args_b[:, 2, :], args_b[:, 2, :], -1.0, None, ALU.mult).then_inc(D_.mark(("args", b)), 1)
                    W(v, l, "ml_pe", ("qk", b))
                    W(v, l, "ml_act", ("E", b))
                    for q in range(2):
                        o = Pm.rearrange("p (j q) s -> p q j s", q=2)[:, q]
                        e = Em.rearrange("p (j q) s -> p q j s", q=2)[:, q]
                        ins = TT(o, e, PS[:, (1, 7)[q], 0:256].rearrange("p (j s) -> p j s", j=2), ALU.mult)
                    ins.then_inc(D_.mark(("P", b)), 1)
                    TT(kw, kb_tok[:, t, :].rearrange("p (h s) -> p h s", h=H), over(exps[:, 1, :], 2, DKB), ALU.mult)
                    for q in range(2):
                        r_ = slice(64 * q, 64 * q + 64)
                        ins = V.tensor_copy(wp[r_], exps[r_, 3:5, :].rearrange("p c (j q) -> p q c j", q=2)[:, q])
                    ins.then_inc(D_.mark(("kw", b)), 1)
                    v.drain()
                    if b == 2:
                        v.wait_ge(state_in, 16 * 10 + l * (16 * STATE_LOADS))
                    for c in range(2):
                        W(v, l, "ml_pe", ("up", b, c))
                        C_ = Cst[:, g, d, :, 0:129]
                        TT(C_, C_, over(wp[:, c, :], 2, 129), ALU.mult)
                        v.drain()
                        TT(C_, C_, PS[:, 0, 0:2 * VA].rearrange("p (j s) -> p j s", j=2)[:, :, 0:129], ALU.add)\
                            .then_inc(D_.mark(("c", b, c)), 1)
                        v.drain()
                    for q in range(2):
                        TT(QCw.rearrange("p (j q) s -> p q j s", q=2)[:, q, :, 0:129],
                           PS[:, 5 + q, 0:2 * VA].rearrange("p (j s) -> p j s", j=2)[:, :, 0:129],
                           over(exps[:, 0, :].rearrange("p (j q) -> p q j", q=2)[:, q], 2, 129), ALU.mult)
                    v.drain()
                    for j in range(2):
                        TT(num[:, 2 * j:2 * j + 2, 0:129], QCw[:, 2 * j:2 * j + 2, 0:129],
                           PS[:, 3 + j, 0:2 * VA].rearrange("p (q s) -> p q s", q=2)[:, :, 0:129], ALU.add)
                    v.drain()
                    STT(rden, num[:, :, 128], -1.0, num[:, :, 128], ALU.mult, ALU.max)
                    v.drain()
                    TT(rden, rden, exps[:, 2, :], ALU.max)
                    v.drain()
                    V.reciprocal(rden, rden)
                    v.drain()
                    if d == 0:
                        TT(hb_tok[:, t], num[:, :, 0:128], over(rden, 2, 128), ALU.mult).then_inc(D_.mark(("h", b)), 1)
                    else:
                        TT(num[:, :, 0:128], num[:, :, 0:128], over(rden, 2, 128), ALU.mult)
                        v.drain()
                        TT(hb_tok[:, t], hb_tok[:, t], num[:, :, 0:128], ALU.add).then_inc(D_.mark(("h", b)), 1)
                    v.drain()
                for t in range(TILES):
                    TT(sq_b, hb_tok[:, t], hb_tok[:, t], ALU.mult)
                    v.drain()
                    RED(stab[:, 4 * t:4 * t + 4], sq_b, AX, ALU.add)
                    v.drain()
                v.drain().then_inc(T["ml_dve"].mark("ss"), 1)
                W(v, l, "ml_act", "root")
                V.reciprocal(stab[:, 0:12], stab[:, 0:12])
                v.drain()
                for t in range(TILES):
                    TT(hb_tok[:, t], hb_tok[:, t], over(stab[:, 4 * t:4 * t + 4], 2, 128), ALU.mult)
                    v.drain()
                    TT(hb_tok[:, t], hb_tok[:, t], over(mnorm_b, 1, H), ALU.mult)
                    v.drain()
                    TT(hb_tok[:, t], hb_tok[:, t], ob_s[:, t, :].rearrange("p (h s) -> p h s", h=H), ALU.mult)\
                        .then_inc(T["ml_dve"].mark(("y", t)), 1)

                W(v, l, "ml_act", ("yt", 2))
                for t in range(TILES):
                    W(v, l, "ap_pe", ("kv", t))
                    V.tensor_copy(kv_tok[:, t, :], PS[:, 5 + t, 0:256]).then_inc(T["ap_dve"].mark(("kv", t)), 1)
                W(v, l, "ap_act", "k")
                for j in range(5):
                    x = qcT[:, j, SEQ:N] if j < 4 else kcT[:, SEQ:N]
                    TT(rope_a[:, j, :], x, K("cos"), ALU.mult)
                    W(v, l, "ap_pe", ("rot", j))
                    TT(rope_b[:, j, :], PS[:, 1 + j, 0:DSEQ], K("sin"), ALU.mult).then_inc(T["ap_dve"].mark(("cos", j)), 1)
                v.drain()
                TT(qcT[:, :, SEQ:N], rope_a[:, 0:4, :], rope_b[:, 0:4, :], ALU.add)
                TT(kcT[:, SEQ:N], rope_a[:, 4, :], rope_b[:, 4, :], ALU.add).then_inc(T["ap_dve"].mark("rope"), 1)

                def attend_out(u):
                    t, g = u // 2, u % 2
                    W(v, l, "at_act", ("e", u))
                    r = rinv[:, 4 * g:4 * g + 4]
                    TT(r, sums[:, u % 2, :], esink[:, u % 2, :], ALU.add)
                    v.drain()
                    V.reciprocal(r, r)
                    v.drain()
                    W(v, l, "at_pe", ("pv", u))
                    TT(yc_tok[:, 256 * g:256 * g + 256].rearrange("p (j s) -> p j s", j=4),
                       PS[:, 7, 0:256].rearrange("p (j s) -> p j s", j=4), over(r, 2, 64), ALU.mult)\
                        .then_inc(T["at_dve"].mark(("y", u)), 1)
                    v.drain()

                for u in range(6):
                    t, g = u // 2, u % 2
                    keys = SEQ if t == 0 else PAST + DSEQ
                    W(v, l, "at_pe", ("s", u))
                    pr = prob[:, u % 2, :, 0:keys]
                    if t == 0:
                        V.tensor_copy(pr, PS[:, 0:4, 0:keys])
                    else:
                        TT(pr, PS[:, 0:4, 0:keys], over(K(f"win{t - 1}"), 1, 4), ALU.add)
                    v.drain()
                    nm = nmax[:, u % 2, :]
                    RED(nm, pr, AX, ALU.max)
                    v.drain()
                    TT(nm, nm, sink_b[:, 4 * g:4 * g + 4], ALU.max)
                    v.drain()
                    TT(esink[:, u % 2, :], sink_b[:, 4 * g:4 * g + 4], nm, ALU.subtract)
                    v.drain()
                    TS(nm, nm, -1.0, None, ALU.mult).then_inc(T["at_dve"].mark(("mx", u)), 1)
                    attend_out(u)

                v.wait_ge(stored, 16 * STORES + l * (16 * STORES))
                for r in range(3):
                    for c in range(KT):
                        n = r * KT + c
                        W(v, l, "mix_act", ("sig", r, c))
                        W(v, l, "mix_pe", ("y", r, c))
                        ps, s = PS[:, 2 + n % 2, 0:N], sig[:, n % 2, :]
                        if r == 0:
                            TT(mixT[:, c, :], ps, s, ALU.mult).then_inc(T["mix_dve"].mark(("m", r, c)), 1)
                        else:
                            TT(prod[:, n % 2, :], ps, s, ALU.mult)
                            v.drain()
                            TT(mixT[:, c, :], mixT[:, c, :], prod[:, n % 2, :], ALU.add)\
                                .then_inc(T["mix_dve"].mark(("m", r, c)), 1)
                for c in range(KT):
                    W(v, l, "mix_pe", ("o", c))
                    for g, a0, a1 in GROUPS:
                        ins = STT(xT[:, c, a0:a1], PS[:, 4 + c % 4, a0:a1], mod[:, 16 + c, g:g + 1], xT[:, c, a0:a1],
                                  ALU.mult, ALU.add)
                    ins.then_inc(T["mix_dve"].mark(("x", c)), 1)
                v.drain()
                norm(l, 1)

                W(v, l, "rt_pe", "logit")
                lg = PS[:, 7, 0:TILES * NE].rearrange("p (t e) -> p t e", e=NE)
                RED(smx, lg, AX, ALU.max)
                v.drain()
                TT(logit, lg, over(smx, 2, NE), ALU.subtract).then_inc(T["rt_dve"].mark("max"), 1)
                W(v, l, "rt_act", "exp")
                RED(smx, aff, AX, ALU.add)
                v.drain()
                V.reciprocal(smx, smx)
                v.drain()
                TT(aff, aff, over(smx, 2, NE), ALU.mult).then_inc(T["rt_dve"].mark("aff"), 1)
                W(v, l, "rt_pe", "affx")
                V.tensor_copy(aff_x, PS[:, 7, 64:64 + TILES * NE].rearrange("p (t e) -> p t e", e=NE))\
                    .then_inc(T["rt_dve"].mark("affx"), 1)
                v.drain()
                for t in range(TILES):
                    TT(diag, over(K("ident"), 1, NE), over(aff[:, t, :], 2, 128), ALU.mult)\
                        .then_inc(T["rt_dve"].mark(("diag", t)), 1)
                    W(v, l, "rt_pe", ("R", t))
                    R = PS[:, 0:4, :].rearrange("p n (e s) -> p (n e) s", s=128)
                    mine = over(aff_x[:, t, :], 2, 128)
                    TT(rk, R, mine, ALU.is_gt)
                    TT(rk_tmp, R, mine, ALU.is_equal)
                    v.drain()
                    TT(rk_m, rk_tmp, over(K("earlier"), 1, NE), ALU.mult)
                    v.drain()
                    TT(rk, rk, rk_m, ALU.add)
                    v.drain()
                    if t == 0:
                        RED(rank[:, 0, :], rk, AX, ALU.add)
                    else:
                        RED(rtmp[:, 0, :], rk, AX, ALU.add)
                        other = 3 - t
                        v.drain()
                        TT(rk, R, over(aff_x[:, other, :], 2, 128), ALU.is_gt if t == 2 else ALU.is_ge)
                        v.drain()
                        RED(rtmp[:, other, :], rk, AX, ALU.add)
                        v.drain()
                        if t == 1:
                            V.tensor_copy(rank[:, 1, :], rtmp[:, 0, :])
                        else:
                            TT(rank[:, 2, :], rtmp[:, 0, :], rtmp[:, 2, :], ALU.add)
                            TT(rank[:, 1, :], rank[:, 1, :], rtmp[:, 1, :], ALU.add)
                    v.drain()
                    v.drain().then_inc(T["rt_dve"].mark(("rank", t)), 1)
                for t in range(TILES):
                    TT(sel[:, t], over(K("slot_s" if t else "slot_p"), 1, NE), over(rank[:, t, :], 2, SLOT_E), ALU.is_equal)
                v.drain()
                TT(selG.rearrange("p t e s -> p (t e) s"), sel.rearrange("p t e s -> p (t e) s"),
                   over(aff.rearrange("p t e -> p (t e)"), 2, SLOT_E), ALU.mult).then_inc(T["rt_dve"].mark("sel"), 1)
                for j in range(NE // 2):
                    W(v, l, "rt_pe", ("sg", j))
                    V.tensor_copy(selGT[:, j, :], PS[:, j % 2, 0:N]).then_inc(T["rt_dve"].mark(("sg", j)), 1)
                for k in range(KT):
                    W(v, l, "rt_pe", ("xs", k))
                    V.tensor_copy(xsT[:, k, :, 0:CAP_S], PS[:, 2 + k % 2, :].rearrange("p (e r) -> p e r", e=NE))
                    V.tensor_copy(xsT[:, k, :, CAP_S:ROWS], PS[:, 4 + k % 2, 0:NE * CAP_P].rearrange("p (e r) -> p e r", e=NE))\
                        .then_inc(T["rt_dve"].mark(("xs", k)), 1)

                with v.Fori(0, NE // E_UNROLL) as eg:
                    W(v, l, "rt_pool", "clear")
                    for u in range(E_UNROLL):
                        gu = PLAIN_BLOCKS + 3 * u
                        WE(v, l, eg, "ex_act", (u, "silu"))
                        TT(hid[0:ROWS, u % 2, :], silu_g[64:64 + ROWS], PS[64:64 + ROWS, u % 2, :], ALU.mult)\
                            .then_inc(T["ex_dve"].mark((u, "hid")), 1)
                        WB(v, l, eg, gu + 2)
                        o = SLOT_E * (u % 2)
                        dst = ye[o:o + ROWS, ds(eg * (E_UNROLL // 2) + u // 2, 1), 512:1024].rearrange("p a n -> p (a n)")
                        V.tensor_copy(dst, PS[64:64 + ROWS, 4 + u % 2, :]).then_inc(T["ex_dve"].mark((u, "d")), 1)
                T["ex_dve"].looped(NE // E_UNROLL, 2 * E_UNROLL)

                for k in range(KT):
                    W(v, l, "cb_pe", ("x", k))
                    for g, a0, a1 in GROUPS:
                        ins = STT(xT[:, k, a0:a1], PS[:, k % 4, a0:a1], mod[:, 40 + k, g:g + 1], xT[:, k, a0:a1],
                                  ALU.mult, ALU.add)
                    ins.then_inc(T["cb_dve"].mark(("x", k)), 1)
                v.drain()

            TT(norm_sq, xT, xT, ALU.mult).then_inc(final_dve, 1)
            v.wait_ge(final_act, 1)
            V.reciprocal(rstd[:, :], rstd[:, :])
            v.drain()
            TT(hT, xT, over(rstd[:, :], 1, KT), ALU.mult)
            v.drain()
            for k in range(KT):
                ins = TS(hT[:, k, :], hT[:, k, :], fin_g[:, k:k + 1], None, ALU.mult)
            ins.then_inc(final_dve, 1)


_INS = ["x_prompt", "x_sample", "cache_attn_k", "cache_attn_v", "state_delta", "state_mlstm_c", "state_mlstm_n",
        "state_mlstm_m", "c", "c_ctx", "ada_w", "ada_b", "norm1_g", "norm2_g", "w_in", "conv_qkv_a", "delta_a_log",
        "delta_dt_bias", "delta_norm_g", "mlstm_i_bias", "mlstm_f_bias", "mlstm_norm_g", "attn_sink", "w_branch_a",
        "w_branch_b", "w_branch_c", "w_out", "w_router", "w_expert_gate", "w_expert_up", "w_expert_down",
        "final_norm_g"]
_OUTS = [(1, SEQ, D), (1, DSEQ, D), (1, DEPTH, SEQ, 2, DC), (1, DEPTH, SEQ, 2, DC), (1, DEPTH, 2, H, 128, 128),
         (1, DEPTH, 2, H, DKB, 128), (1, DEPTH, 2, H, DKB), (1, DEPTH, 2, H)]


def kernel(**inputs):
    import numpy as _np
    import concourse.bacc as _bacc
    from concourse import mybir as _mybir
    from concourse.bass_utils import run_bass_kernel_spmd as _run

    nc = _bacc.Bacc("TRN2", target_bir_lowering=False, num_devices=1)
    arrays, args = {}, []
    for name in _INS:
        a = _np.ascontiguousarray(inputs[name])
        arrays[f"in_{name}_dram"] = a
        args.append(nc.dram_tensor(f"in_{name}_dram", a.shape, _mybir.dt.from_np(a.dtype), kind="ExternalInput").ap())
    a = const_columns()[0]
    arrays["in_consts_dram"] = a
    args.append(nc.dram_tensor("in_consts_dram", a.shape, F32, kind="ExternalInput").ap())
    for i, shape in enumerate(_OUTS):
        args.append(nc.dram_tensor(f"out_{i}_dram", shape, F32, kind="ExternalOutput").ap())
    build_step(nc, args)
    r = _run(nc, [arrays], core_ids=[0])
    return tuple(r.results[0][f"out_{i}_dram"] for i in range(len(_OUTS)))
```

```python
from contextlib import ExitStack

import concourse.bass as bass
from concourse import mybir

F32 = mybir.dt.float32
ALU = mybir.AluOpType
ACT = mybir.ActivationFunctionType
AX = mybir.AxisListType.X

D = 1024
KT = D // 128
SEQ, DSEQ, PAST = 128, 256, 128
N = SEQ + DSEQ
TILES = N // 128
GROUPS = ((0, 0, SEQ), (1, SEQ, N))
DEPTH = 2
EPS = 1e-6
H = 4
CH = 64
DKB, VA = 64, 132
CONV_K = 5
PADW = 2 + SEQ + 4 + DSEQ + 2
HC, DC = 8, 64
NE = 16
CAP_S, CAP_P = 2 * DSEQ // NE, 2 * SEQ // NE
ROWS = CAP_S + CAP_P
SLOT_E = 64
NEG = -1.0e30
ADA_BLOCKS = 6 * D // 512
C_QA, C_GATE_A, C_QB, C_VB, C_OB, C_GATE_B, C_QC, C_KC, C_G = 0, 2048, 2064, 2576, 3088, 3600, 3616, 4128, 4384

RING = 4
MIX_BLOCKS = 3 * 3 + 2
HEAD_BLOCKS = ADA_BLOCKS + 9
PLAIN_BLOCKS = HEAD_BLOCKS + MIX_BLOCKS
LAYER_BLOCKS = PLAIN_BLOCKS + 3 * NE
Q_BLOCK = ADA_BLOCKS + 7 + 3


def loads_in_slot(last):
    return sum(8 if i == Q_BLOCK else 1 for i in range(last % RING, last + 1, RING))


E_UNROLL = 8
assert PLAIN_BLOCKS % RING == 0 and (3 * E_UNROLL) % RING == 0

BATCHES = ((0, 0, 0), (0, 1, 0), (1, 0, 1), (2, 0, 1), (2, 1, 1), (1, 1, 1))
NB = len(BATCHES)
LEVELS = (1, 2, 4, 8, 16, 32)


class Track:

    def __init__(self, sem, steps, base):
        self.sem, self.steps, self.made, self.base = sem, list(steps), 0, base
        self.per = len(self.steps)
        self.number = {s: i + 1 for i, s in enumerate(self.steps)}
        assert len(self.number) == self.per

    def at(self, l, step):
        return l * self.per + self.base + self.number[step]

    def before(self, l):
        return l * self.per + self.base

    def mark(self, step):
        assert self.steps[self.made % self.per] == step, (self.steps[self.made % self.per], step)
        self.made += 1
        return self.sem

    def looped(self, turns, body):
        self.made += (turns - 1) * body


def const_columns():
    import numpy as np
    r = np.arange(128)[:, None]
    t = np.arange(128)[None, :]
    same = (r // CH) == (t // CH)
    tabs = {}
    tabs["ident"] = (r == t)
    tabs["ones"] = np.ones((128, 128))
    tabs["tri0"] = same & (r <= t)
    tabs["tri1"] = same & (r >= t)
    tabs["block"] = same
    tabs["half0"] = np.broadcast_to(r < CH, (128, 128))
    tabs["half1"] = np.broadcast_to(r >= CH, (128, 128))
    tabs["strict0"] = same & (r > t)
    tabs["strict1"] = same & (r < t)
    for b in LEVELS:
        pair = (r // (2 * b)) == (t // (2 * b))
        tabs[f"lev0_{b}"] = pair & (r % (2 * b) >= b) & (t % (2 * b) < b)
        tabs[f"lev1_{b}"] = pair & (r % (2 * b) < b) & (t % (2 * b) >= b)
    tabs["neg0"] = np.where(same & (r >= t), 0.0, NEG)
    tabs["neg1"] = np.where(same & (r <= t), 0.0, NEG)
    tabs["earlier"] = (t < r)
    d = np.arange(128) % DC
    nf = DC // 4
    inv = np.power(np.float32(10000.0), -np.arange(nf, dtype=np.float32) / np.float32(nf)).astype(np.float32)
    pos = np.arange(DSEQ)
    row, col = (pos // 64).astype(np.float32), (pos % 64).astype(np.float32)
    ang = np.where((d < 2 * nf)[:, None], row[None, :], col[None, :]) * inv[d % nf][:, None]
    tabs["cos"] = np.cos(ang.astype(np.float32))
    tabs["sin"] = np.sin(ang.astype(np.float32))
    first = (d % (2 * nf)) < nf
    partner = np.where(first, np.arange(128) + nf, np.arange(128) - nf)
    rot = np.zeros((128, 128))
    rot[partner, np.arange(128)] = np.where(first, -1.0, 1.0)
    tabs["rot"] = rot
    for i in range(2):
        q = i * 128 + r
        k = np.arange(DSEQ)[None, :]
        tabs[f"win{i}"] = np.concatenate([np.zeros((128, PAST)), np.where(np.abs(q - k) <= 128, 0.0, NEG)], axis=1)
    slot = np.arange(SLOT_E)
    tabs["slot_s"] = np.broadcast_to(np.where(slot < CAP_S, slot, -1), (128, SLOT_E))
    tabs["slot_p"] = np.broadcast_to(np.where((slot >= CAP_S) & (slot < ROWS), slot - CAP_S, -1), (128, SLOT_E))
    where, cols, at = {}, [], 0
    for name, a in tabs.items():
        where[name] = (at, a.shape[1])
        at += a.shape[1]
        cols.append(np.asarray(a, dtype=np.float32))
    return np.ascontiguousarray(np.concatenate(cols, axis=1)), where



def build_step(nc, args):
    (x_prompt, x_sample, cache_k, cache_v, state_delta, state_c, state_n, state_m, c_lat, c_ctx, ada_w, ada_b,
     norm1_g, norm2_g, w_in, conv_w, a_log, dt_bias, delta_g, i_bias, f_bias, mlstm_g, sink, w_a, w_b, w_c,
     w_out, w_router, w_gate, w_up, w_down, final_g, consts,
     y_prompt, y_sample, new_k, new_v, new_delta, new_c, new_n, new_m) = args
    _, where = const_columns()
    ds = bass.ds

    with ExitStack() as ctx:
        def sb(name, words):
            return ctx.enter_context(nc.sbuf_tensor(name, [128, words], F32))

        def sem(name):
            return ctx.enter_context(nc.semaphore(name))

        PS = ctx.enter_context(nc.psum_tensor("PS", [128, 8, 512], F32))

        xT_b = sb("xT", KT * N)
        hT_b = sb("hT", KT * N)
        ring = sb("ring", RING * KT * 512)
        const = sb("const", consts.shape[1])
        mod_b = sb("mod", 48 * 2)
        vec_row = sb("vec_row", 128)
        vecT = sb("vecT", 128)
        condT = sb("condT", KT * 2)
        fin_g = sb("fin_g", KT)
        affine = sb("affine", 2 * KT * 2)
        rstd = sb("rstd", N)
        ada_rows = sb("ada_rows", 512)
        small = sb("small", 1696)
        arena = sb("arena", 22304)
        xT = xT_b[:, :].rearrange("p (k n) -> p k n", k=KT)
        hT = hT_b[:, :].rearrange("p (k n) -> p k n", k=KT)
        mod = mod_b[:, :].rearrange("p (c v) -> p c v", v=2)

        def K(name):
            a, n = where[name]
            return const[:, a:a + n]

        def carve(base, at, *shape):
            n = 1
            for s in shape:
                n *= s
            assert at + n <= base.shape[1], (at, n)
            v = base[:, at:at + n]
            if len(shape) == 2:
                v = v.rearrange("p (a b) -> p a b", a=shape[0])
            if len(shape) == 3:
                v = v.rearrange("p (a b c) -> p a b c", a=shape[0], b=shape[1])
            if len(shape) == 4:
                v = v.rearrange("p (a b c d) -> p a b c d", a=shape[0], b=shape[1], c=shape[2])
            return v

        class Place:
            def __init__(self, base, at=0):
                self.base, self.at = base, at

            def __call__(self, *shape):
                n = 1
                for s in shape:
                    n *= s
                v = carve(self.base, self.at, *shape)
                self.at += n
                return v

        def over(ap, axis, n):
            shape = list(ap.shape)
            shape.insert(axis, n)
            return ap.unsqueeze(axis).broadcast_to(shape)

        P = Place(small)
        w_small = P(KT, 32)
        a_log_b = P(8)
        bias_b = P(32)
        sink_b = P(8)
        m_state = P(2, 2, H)
        mnorm_b = P(128)
        gates = P(TILES, 32)
        soft = P(TILES, 32)
        g_lf = P(TILES, 2, 2 * H)
        beta = P(TILES, 8)
        cum = P(TILES, 2, 2 * H)
        tot = P(TILES, 2, 2 * H)
        chunk_tot = P(2, TILES, 2, 2 * H)
        e_cum = P(TILES, 2, H)
        kd_f = P(TILES, 2, H)
        kbg_f = P(TILES, 2, H)
        e_chunk = P(2, TILES, 2, H)
        rcol = P(TILES, 2, H)
        neg_rate = P(8)
        stab = P(64)
        args_b = P(5, H)
        exps_b = P(2, 5, H)
        wp = P(2, 2)
        mx = P(H, 2)
        dmx = P(H)
        nmax = P(2, 4)
        sums = P(2, 4)
        esink = P(2, 4)
        rinv = P(8)
        rden = P(H)
        logit = P(TILES, NE)
        aff = P(TILES, NE)
        aff_x = P(TILES, NE)
        smx = P(TILES)
        rank = P(TILES, NE)
        rtmp = P(3, NE)
        w_rt = P(KT, NE)

        A = Place(arena)
        yT = [A(H, N) for _ in range(3)]
        phase0 = A.at

        A = Place(arena, phase0)
        qkvT = A(3 * H, N)
        pads_at = arena[:, A.at:A.at + 4 * PADW]
        pads = A(4, PADW)
        acc = A(2, PADW - 4)
        states = A(2, 2, H, 128)
        nrm = carve(arena, A.at, 2, 512)
        S512 = [A(H, 128) for _ in range(15)]
        (G2, dec, dinc, dstr, vb, kbg, kd, Lm, LT, av, aT, X, XT, Wm, qd) = S512
        A = Place(arena, phase0 - 2 * H * N)
        Mb = [A(H, 128) for _ in range(5)]
        er = A(H, 128)
        uv, wT, vn, Sd = Mb[0:4]
        silu_z = carve(pads_at, 0, H, N)

        A = Place(arena, phase0)
        qkbT = A(4, N)
        kb_tok = A(TILES, 256)
        v_aug = A(TILES, H, VA)
        ob_s = A(TILES, 512)
        hb_tok = A(TILES, H, 128)
        Cst = A(2, 2, 2, VA)
        T512 = [A(H, 128) for _ in range(7)]
        (G3, g3b, Rm, Em, Pm, PTm, sq_b) = T512
        kw = A(H, DKB)
        QCw = A(H, VA)
        num = A(H, VA)

        A = Place(arena, phase0)
        qcT = A(4, N)
        kcT = A(N)
        kv_tok = A(TILES, 256)
        ck_tok = A(128)
        cv_tok = A(128)
        ckT = A(PAST)
        rope_a = A(5, DSEQ)
        rope_b = A(5, DSEQ)
        prob = A(2, 4, PAST + DSEQ)
        probT = A(2, 4, PAST + DSEQ)
        yc_tok = A(512)

        mixT = carve(arena, arena.shape[1] - KT * N, KT, N)
        sig_a = carve(arena, arena.shape[1] - (KT + 1) * N, N)
        A = Place(arena, phase0 + KT * N)
        sig = A(2, N)
        prod = A(2, N)
        norm_sq = hT

        A = Place(arena, 0)
        xsT = A(KT, NE, ROWS)
        selGT = A(NE // 2, N)
        e0 = A.at
        h_tok = A(TILES, D)
        sel = A(TILES, NE, SLOT_E)
        selG = A(TILES, NE, SLOT_E)
        rk = carve(arena, e0 + TILES * D + 2 * NE * 128, NE, 128)
        rk_tmp = carve(arena, e0 + TILES * D, NE, 128)
        rk_m = carve(arena, e0 + TILES * D + NE * 128, NE, 128)
        diag = carve(arena, 0, 2, NE, 128)
        ye = carve(arena, e0 + TILES * (D + 2 * NE * SLOT_E), 2, D)
        A = Place(arena, e0)
        silu_g = A(512)
        hid = A(2, 512)
        hidT = A(2, 4, ROWS)
        xs_e = A(2, KT, ROWS)

        x_tok = carve(arena, phase0, TILES, D)
        cond_rows = carve(arena, phase0 + TILES * D, 128)
        y_tok = x_tok

        rng = range
        steps = {
            "ring_used": [("block", i) for i in rng(LAYER_BLOCKS)],
            "pre_pe": ["rows", "x"], "pre_act": ["vec", "x"], "pre_dve": ["clear", "x"],
            "ada_pe": ["vec"] + [s for n in rng(3) for s in [("rows", n, b) for b in rng(4)] + [("tr", n)]],
            "ada_act": ["vec", "rate"] + [("rows", n, b) for n in rng(3) for b in rng(4)], "ada_dve": [("mod", n) for n in rng(3)],
            "nrm_pe": ["ss0", "ss1"], "nrm_act": ["sq0", "sqrt0", "h0"] + [("sq1", k) for k in rng(KT)] + ["sqrt1", "h1"],
            "nrm_dve": [s for w in rng(2) for s in (f"rstd{w}", ("xn", w, 0), ("xn", w, 1))],
            "gate_pe": ["proj", "cum"], "gate_act": ["exp", "ln", "ecum"], "gate_dve": ["biased", "lf", "args", "done"],
            "conv_pe": [s for j in rng(12) for s in [("p", j)] + [("ss", j - 4)] * (j >= 4)],
            "conv_act": [s for j in rng(13) for s in [("pad", j)] * (j < 12) + [("silu", j - 1)] * (j > 0)
                         + [("sq", j - 3)] * (3 <= j < 11) + [("root", j - 4)] * (4 <= j < 12)],
            "conv_dve": [s for j in rng(12) for s in [("conv", j)] + [("unit", j - 4)] * (j >= 4)],
            "delta_pe": [("row", 0), ("tok", 0), ("kk", 0)]
            + [s for b in rng(NB) for s in [("lt", b)]
               + [(x, b, i, h) for i in rng(5) for x in "wy" for h in rng(2)] + [("at", b), ("uw", b), ("ws", b, 0)]
               + ([("row", b + 1), ("tok", b + 1)] if b + 1 < NB else []) + [("os", b, 0), ("ws", b, 1)]
               + ([("kk", b + 1)] if b + 1 < NB else []) + [("os", b, 1)]],
            "delta_act": [("er", 0), ("dec", 0)]
            + [s for b in rng(NB) for s in [("ltc", b)] + [("wc", b, i, h) for i in rng(5) for h in rng(2)]
               + [("atc", b), ("wtc", b)] + ([("er", b + 1), ("dec", b + 1)] if b + 1 < NB else [])],
            "delta_dve": [("g2", 0), ("d", 0), ("vk", 0), ("qk", 0), ("la", 0)]
            + [s for b in rng(NB) for s in [("x0", b)] + [("x", b, i, h) for i in rng(5) for h in rng(2)] + [("u", b)]
               + ([("g2", b + 1)] if b + 1 < NB else []) + [("vn", b, 0)] + ([("d", b + 1)] if b + 1 < NB else [])
               + [("s", b, 0), ("vn", b, 1)] + ([("vk", b + 1)] if b + 1 < NB else []) + [("s", b, 1)]
               + ([("qk", b + 1), ("la", b + 1)] if b + 1 < NB else [])],
            "delta_pool": [("m", b) for b in rng(NB)],
            "z_pe": [("z", j) for j in (0, 1, 2, 3)] + ["ss"], "z_act": [("z", j) for j in (0, 1, 2, 3)] + ["sq", "root"],
            "z_dve": ["root", ("y", 0)],
            "mp_pe": [("qk", j) for j in rng(4)] + [("kt", t) for t in rng(3)] + [("v", t) for t in rng(3)]
            + [("o", t) for t in rng(3)],
            "mp_act": [("qk", j) for j in rng(4)] + [("o", t) for t in rng(3)],
            "mp_dve": ["ones"] + [("kt", t) for t in rng(3)] + [("v", t) for t in rng(3)],
            "ml_pe": [("row", 0), ("qk", 0)]
            + [s for b in rng(NB) for s in [("pt", b), ("pv", b), ("qc", b, 0), ("up", b, 0)]
               + [("row", b + 1)] * (b + 1 < NB) + [("qc", b, 1), ("up", b, 1)]
               + [("qk", b + 1)] * (b + 1 < NB)] + [("yt", t) for t in rng(3)],
            "ml_act": [("ex", 0), ("E", 0)] + [s for b in rng(NB) for s in [("ptc", b)]
                                               + [("ex", b + 1), ("E", b + 1)] * (b + 1 < NB)]
            + ["root"] + [("yt", t) for t in rng(3)],
            "ml_dve": [("g3", 0), ("args", 0)]
            + [s for b in rng(NB) for s in [("P", b), ("kw", b)] + [("g3", b + 1)] * (b + 1 < NB)
               + [("c", b, 0), ("c", b, 1)] + [("args", b + 1)] * (b + 1 < NB) + [("h", b)]]
            + ["ss"] + [("y", t) for t in rng(3)],
            "ap_pe": [("q", j) for j in rng(4)] + ["k"] + [("kv", t) for t in rng(3)] + ["ckT"]
            + [("rot", j) for j in rng(5)],
            "ap_act": [("q", j) for j in rng(4)] + ["k"] + ["ckT"],
            "ap_dve": [("kv", t) for t in rng(3)] + [("cos", j) for j in rng(5)] + ["rope"],
            "at_pe": [("s", 0)]
            + [s for u in rng(6) for s in [("s", u + 1)] * (u < 5) + [("pt", u, 0), ("pt", u, 1), ("pt", u, 2)]
               + [("yt", u // 2 - 1)] * (u in (2, 4)) + [("pv", u)]] + [("yt", 2)],
            "at_act": [("e", 0)] + [s for u in rng(6) for s in [("ptc", u)] + [("yt", u // 2 - 1)] * (u in (2, 4))
                                    + [("e", u + 1)] * (u < 5)] + [("yt", 2)],
            "at_dve": [("mx", 0)] + [s for u in rng(6) for s in [("mx", u + 1)] * (u < 5) + [("y", u)]],
            "ma_pe": [s for c in rng(KT) for s in (("g", c), ("y", c))], "ma_act": [("sig", c) for c in rng(KT)],
            "ma_dve": [("m", c) for c in rng(KT)],
            "mix_pe": [s for r in (1, 2) for c in rng(KT) for s in (("g", r, c), ("y", r, c))]
            + [("o", c) for c in rng(KT)],
            "mix_act": [("sig", r, c) for r in (1, 2) for c in rng(KT)],
            "mix_dve": [("m", r, c) for r in (1, 2) for c in rng(KT)] + [("x", c) for c in rng(KT)],
            "rt_pe": ["logit", "affx"] + [("R", t) for t in rng(3)] + [("ht", t, u) for t in rng(3) for u in rng(2)]
            + [("sg", j) for j in rng(NE // 2)] + [("xs", k) for k in rng(KT)],
            "rt_act": ["exp"] + [("ht", t, u) for t in rng(3) for u in rng(2)],
            "rt_dve": ["max", "aff", ("diag", 0), "affx", ("diag", 1), ("rank", 0), ("diag", 2), ("rank", 1), ("rank", 2), "sel"]
            + [("sg", j) for j in rng(NE // 2)] + [("xs", k) for k in rng(KT)],
            "rt_pool": ["clear"],
            "exc_pe": [(p, k) for p in rng(NE // 2) for k in rng(KT)],
            "exc_dve": [(p, k) for p in rng(NE // 2) for k in rng(KT)],
            "ex_pool": [(e, "xs") for e in rng(NE)],
            "ex_pe": [(e, "t") for e in rng(NE)],
            "ex_act": [(e, s) for e in rng(NE) for s in ("silu", "ht", "d")],
            "ex_dve": [(e, s) for e in rng(NE) for s in ("hid", "d")],
        }
        def base(name):
            return RING if name == "ring_used" else 7 if name.startswith("ex") else 1

        T = {name: Track(sem(name), s, base(name)) for name, s in steps.items()}
        by_engine = {"pe": [], "act": [], "dve": [], "pool": []}
        for name in T:
            by_engine["pe" if name == "ring_used" else name.split("_")[1]].append(name)
        slot_in = [sem(f"slot_in{s}") for s in range(RING)]
        start_in = sem("start_in")
        vec_in = sem("vec_in")
        state_in = sem("state_in")
        stored = sem("stored")
        final_stored = sem("final_stored")
        final_pe, final_act, final_dve = sem("final_pe"), sem("final_act"), sem("final_dve")
        apart = {e: sem(f"apart_{e}") for e in ("pe", "pool")}
        EARLY_ADA = {1: (1, 1), 2: (1, 3), 3: (2, 1), 4: (2, 3)}
        LATE_ADA = {0: (1, 0), 1: (1, 2), 2: (2, 0), 3: (2, 2)}
        EARLY_Z, LATE_Z = {5: 1}, {4: 0, 5: 2}
        ADA_TURN = {2: 1, 4: 2}
        VEC_LOADS, STORES = 15, 13
        STATE_LOADS = 12

        def prime(eng, kind):
            for name in by_engine[kind]:
                eng.sem_inc(T[name].sem, base(name))

        done = {name: T[name].sem for name in T}

        def at(name, l, step):
            return T[name].at(l, step)

        def at_block(l, eg, i, back=0):
            return at("ring_used", l, ("block", i)) - 3 * back + eg * (3 * E_UNROLL)

        def at_expert(name, l, eg, step, back=0):
            per_expert = T[name].per // NE
            return at(name, l, step) - back * per_expert + eg * (E_UNROLL * per_expert)

        def at_pair(name, l, eg, p, k):
            return at(name, l, (p, k)) + eg * (E_UNROLL // 2 * KT)

        block = ctx.enter_context(nc.Block())

        @block.sync
        def _(sp):
            def load_block(l, i, src, e=None):
                sp.wait_ge(T["ring_used"].sem, l * LAYER_BLOCKS + 1 + i + (0 if e is None else e * 3))
                kt = src.shape[1]
                dst = ring[:, (i % RING) * KT * 512:(i % RING + 1) * KT * 512].rearrange("p (k n) -> p k n", k=kt)
                sp.dma_start(dst[:, :, 0:src.shape[2]], src).then_inc(slot_in[i % RING], 16)

            def rows(w, l, c0, c1):
                return w[ds(l, 1), :, c0:c1].rearrange("a (k p) n -> p (a k) n", p=128)

            sp.dma_start(const[:, :], consts).then_inc(start_in, 16)
            sp.dma_start(x_tok[:, 0:1, :], x_prompt.rearrange("b (t p) d -> p (b t) d", p=128)).then_inc(start_in, 16)
            sp.dma_start(x_tok[:, 1:3, :], x_sample.rearrange("b (t p) d -> p (b t) d", p=128)).then_inc(start_in, 16)
            sp.dma_start(cond_rows[0:8, :], c_ctx.rearrange("(k p) -> k p", p=128)).then_inc(start_in, 16)
            sp.dma_start(cond_rows[8:16, :], c_lat.rearrange("b (k p) -> (b k) p", p=128)).then_inc(start_in, 16)
            sp.dma_start(cond_rows[16:24, :], final_g.rearrange("(k p) -> k p", p=128)).then_inc(start_in, 16)

            with sp.Fori(0, DEPTH) as l:
                i = 0
                def load_ada(i, n):
                    for b in range(4 * n, 4 * n + 4):
                        load_block(l, i + b % 4, rows(ada_w, l, 512 * b, 512 * b + 512))
                    return i + 4

                def load_merge(i, r, w):
                    load_block(l, i, rows(w, l, 0, D))
                    for h in range(2):
                        c0 = C_G + r * D + 512 * h
                        load_block(l, i + 1 + h, rows(w_in, l, c0, c0 + 512))
                    return i + 3

                i = load_ada(i, 0)
                for c0, c1 in ((0, 512), (512, 1024), (1024, 1536), (1536, 2048), (C_QB, C_QB + 512),
                               (C_VB, C_VB + 512), (C_OB, C_OB + 512), (C_QC, C_QC + 512), (C_KC, C_KC + 256)):
                    if c0 == 1536:
                        i = load_ada(i, 1)
                        i = load_ada(i, 2)
                    if c0 == C_QC:
                        i = load_merge(i, 0, w_a)
                    if i == Q_BLOCK:
                        sp.wait_ge(T["ring_used"].sem, l * LAYER_BLOCKS + 1 + i)
                        dst = ring[:, (i % RING) * KT * 512:(i % RING + 1) * KT * 512]
                        dst = dst.rearrange("p (k j g c) -> p g j k c", k=KT, j=4, g=2)
                        for g in range(2):
                            for j in range(4):
                                o = c0 + 256 * g + 64 * j
                                sp.dma_start(dst[:, g, j], rows(w_in, l, o, o + 64)).then_inc(slot_in[i % RING], 16)
                    else:
                        load_block(l, i, rows(w_in, l, c0, c1))
                    i += 1
                i = load_merge(i, 1, w_b)
                i = load_merge(i, 2, w_c)
                for h in range(2):
                    load_block(l, i, rows(w_out, l, 512 * h, 512 * h + 512))
                    i += 1
                with sp.Fori(0, NE // E_UNROLL) as eg:
                    for u in range(E_UNROLL):
                        for n, w in enumerate((w_gate, w_up, w_down)):
                            src = w[ds(l, 1), ds(eg * E_UNROLL + u, 1)].rearrange("a e (k p) n -> p (a e k) n", p=128)
                            load_block(l, i + 3 * u + n, src, eg * E_UNROLL)
            sp.wait_ge(final_act, 2)
            sp.dma_start(y_prompt.rearrange("b (t p) d -> p (b t) d", p=128), y_tok[:, 0:1, :]).then_inc(final_stored, 16)
            sp.dma_start(y_sample.rearrange("b (t p) d -> p (b t) d", p=128), y_tok[:, 1:3, :]).then_inc(final_stored, 16)
            sp.wait_ge(final_stored, 32)
            sp.wait_ge(stored, 16 * STORES * DEPTH)

        @block.gpsimd
        def _(pool):
            prime(pool, "pool")
            with pool.Fori(0, DEPTH) as l:
                count = [0, 0, 0]

                def load(dst, src, which=0, slow=False):
                    pool.sem_inc(apart["pool"], 1)
                    pool.dma_start(dst, src, allow_slow_non_contiguous=slow).then_inc((vec_in, state_in, stored)[which], 16)
                    count[which] += 1

                def bcast(dst, src):
                    load(dst, src.partition_broadcast(128) if len(src.shape) == 1 else src.broadcast_to([128] + list(src.shape[1:])))

                pool.wait_ge(T["exc_dve"].sem, T["exc_dve"].before(l))
                load(vec_row[0:48, :], ada_b[ds(l, 1)].rearrange("a (k p) -> (a k) p", p=128))
                load(vec_row[48:56, :], norm1_g[ds(l, 1)].rearrange("a (k p) -> (a k) p", p=128))
                load(vec_row[56:64, :], norm2_g[ds(l, 1)].rearrange("a (k p) -> (a k) p", p=128))
                load(vec_row[64:124, :], conv_w[ds(l, 1)].rearrange("a c (j p) -> (a c j) p", p=128))
                load(vec_row[124:125, :], delta_g[ds(l, 1)])
                for dst, src in ((a_log_b, a_log), (bias_b[:, 8:16], dt_bias), (bias_b[:, 16:24], i_bias),
                                 (bias_b[:, 24:32], f_bias)):
                    bcast(dst, src[ds(l, 1)].rearrange("a d h -> a (d h)"))
                bcast(sink_b, sink[ds(l, 1)])
                bcast(mnorm_b, mlstm_g[ds(l, 1)])
                bcast(m_state[:, 1].rearrange("p d h -> p (d h)"), state_m[:, ds(l, 1)].rearrange("b a d h -> (b a) (d h)"))
                load(w_small[:, :, 0:16], w_in[ds(l, 1), :, C_GATE_A:C_GATE_A + 16].rearrange("a (k p) n -> p (a k) n", p=128))
                load(w_small[:, :, 16:32], w_in[ds(l, 1), :, C_GATE_B:C_GATE_B + 16].rearrange("a (k p) n -> p (a k) n", p=128))
                load(w_rt, w_router[ds(l, 1)].rearrange("a (k p) n -> p (a k) n", p=128))
                for d in range(2):
                    load(states[:, 1, d], state_delta[:, ds(l, 1), d].rearrange("b a h k v -> k (b a h) v"), 1)
                for b, (tile, d, g) in enumerate(BATCHES):
                    pool.wait_ge(done["delta_act"], at("delta_act", l, ("ltc", b)))
                    for i, lev in enumerate(LEVELS[1:]):
                        ins = nc.gpsimd.tensor_tensor(Mb[i], LT, over(K(f"lev{1 - d}_{lev}"), 1, H), ALU.mult)
                    ins.then_inc(T["delta_pool"].mark(("m", b)), 1)
                pool.wait_ge(done["delta_dve"], at("delta_dve", l, ("s", NB - 1, 1)))
                for d in range(2):
                    load(new_delta[:, ds(l, 1), d].rearrange("b a h k v -> k (b a h) v"), states[:, 0, d], 2)
                pool.wait_ge(stored, 16 * 2 + l * (16 * STORES))
                for d in range(2):
                    for q in range(2):
                        part = slice(64 * q, 64 * q + 64)
                        src = state_c[:, ds(l, 1), d].rearrange("b a (j q) k v -> q k (b a j) v", q=2)[q]
                        load(Cst[part, 1, d, :, 0:128], src, 1)
                        src = state_n[:, ds(l, 1), d].rearrange("b a (j q) k -> q k (b a j)", q=2)[q]
                        load(Cst[part, 1, d, :, 128:129], src.unsqueeze(2), 1, slow=True)
                pool.wait_ge(done["ml_dve"], at("ml_dve", l, ("h", NB - 1)))
                for d in range(2):
                    for q in range(2):
                        part = slice(64 * q, 64 * q + 64)
                        dst = new_c[:, ds(l, 1), d].rearrange("b a (j q) k v -> q k (b a j) v", q=2)[q]
                        load(dst, Cst[part, 0, d, :, 0:128], 2)
                        dst = new_n[:, ds(l, 1), d].rearrange("b a (j q) k -> q k (b a j)", q=2)[q]
                        load(dst.unsqueeze(2), Cst[part, 0, d, :, 128:129], 2, slow=True)
                load(new_m[:, ds(l, 1)].rearrange("b a d h -> (b a) d h"), m_state[0:1, 0], 2)
                pool.wait_ge(stored, 16 * 11 + l * (16 * STORES))
                pool.wait_ge(done["ml_dve"], at("ml_dve", l, ("y", 2)))
                pool.wait_ge(done["ml_act"], at("ml_act", l, ("yt", 2)))
                load(ck_tok, cache_k[:, ds(l, 1)].rearrange("b a p h d -> p (b a h d)"), 1)
                load(cv_tok, cache_v[:, ds(l, 1)].rearrange("b a p h d -> p (b a h d)"), 1)
                pool.wait_ge(done["ap_dve"], at("ap_dve", l, ("kv", 0)))
                load(new_k[:, ds(l, 1)].rearrange("b a p h d -> p (b a h d)"), kv_tok[:, 0, 0:128], 2)
                load(new_v[:, ds(l, 1)].rearrange("b a p h d -> p (b a h d)"), kv_tok[:, 0, 128:256], 2)
                pool.wait_ge(stored, 16 * 13 + l * (16 * STORES))
                pool.wait_ge(done["nrm_pe"], at("nrm_pe", l, "ss1"))
                pool.sem_inc(apart["pool"], 1)
                nc.gpsimd.memset(ye[32:64], 0.0)
                nc.gpsimd.memset(ye[96:128], 0.0).then_inc(T["rt_pool"].mark("clear"), 1)
                with pool.Fori(0, NE // E_UNROLL) as eg:
                    pool.wait_ge(done["rt_dve"], at("rt_dve", l, ("xs", KT - 1)))
                    pool.wait_ge(done["rt_pool"], at("rt_pool", l, "clear"))
                    for u in range(E_UNROLL):
                        pool.wait_ge(done["ring_used"], at_block(l, eg, PLAIN_BLOCKS + 3 * u + 1, 2))
                        pool.sem_inc(apart["pool"], 1)
                        nc.gpsimd.tensor_copy(xs_e[:, u % 2], xsT[:, :, ds(eg * E_UNROLL + u, 1), :].rearrange("p k a r -> p k (a r)"))\
                            .then_inc(T["ex_pool"].mark((u, "xs")), 1)
                T["ex_pool"].looped(NE // E_UNROLL, E_UNROLL)
                assert count == [VEC_LOADS, STATE_LOADS, STORES], count

        @block.tensor
        def _(pe):
            mm = nc.tensor.matmul
            ident, ones = K("ident"), K("ones")

            def tr(out, in_, n=128):
                return nc.tensor.transpose(out, in_, ident[0:n, 0:n])

            def block_view(i, kt=KT):
                return ring[:, (i % RING) * KT * 512:(i % RING + 1) * KT * 512].rearrange("p (k n) -> p k n", k=kt)

            def landed(l, i, e=None):
                whole = loads_in_slot(LAYER_BLOCKS - RING + i % RING)
                pe.wait_ge(slot_in[i % RING], l * (16 * whole) + 16 * loads_in_slot(i)
                           + (0 if e is None else e * (48 // RING)))

            def used(i):
                return T["ring_used"].mark(("block", i))

            def channels(i, c, out):
                w = block_view(i)
                for k in range(KT):
                    ins = mm(out, w[:, k, 128 * c:128 * c + 128], hT[:, k, :], start=k == 0, stop=k == KT - 1)
                return ins

            def tokens(i, t, out, c0=0, c1=512):
                w = block_view(i)
                for k in range(KT):
                    ins = mm(out, hT[:, k, 128 * t:128 * t + 128], w[:, k, c0:c1], start=k == 0, stop=k == KT - 1)
                return ins

            def column_sums(l):
                pe.wait_ge(done["nrm_act"], at("nrm_act", l, "sq0"))
                for k in range(KT):
                    ins = mm(PS[:, 5, 0:N], ones, norm_sq[:, k, :], start=k == 0, stop=k == KT - 1)
                ins.then_inc(T["nrm_pe"].mark("ss0"), 1)

            prime(pe, "pe")
            pe.wait_ge(start_in, 16 * 6)
            tr(PS[:, 7, 384:408], cond_rows[0:24, :], 24).then_inc(T["pre_pe"].mark("rows"), 1)
            pe.wait_ge(T["pre_act"].sem, T["pre_act"].at(0, "vec"))
            for k in range(KT):
                for t in range(TILES):
                    ins = tr(PS[:, k, 128 * t:128 * t + 128], x_tok[:, t, 128 * k:128 * k + 128])
            ins.then_inc(T["pre_pe"].mark("x"), 1)
            pe.wait_ge(T["pre_act"].sem, T["pre_act"].at(0, "x"))
            pe.wait_ge(T["pre_dve"].sem, T["pre_dve"].at(0, "x"))

            with pe.Fori(0, DEPTH) as l:
                blk = 0
                pe.wait_ge(vec_in, 16 * VEC_LOADS + l * (16 * VEC_LOADS))
                pe.wait_ge(T["exc_dve"].sem, T["exc_dve"].before(l))
                tr(PS[:, 6, 0:125], vec_row[0:125, :], 125).then_inc(T["ada_pe"].mark("vec"), 1)
                column_sums(l)
                def ada_block(blk, n, bank, b):
                    landed(l, blk)
                    w = block_view(blk)
                    for k in range(KT):
                        for q in range(4):
                            ins = mm(PS[32 * q:32 * q + 2, bank, 128 * b:128 * b + 128], condT[:, 2 * k:2 * k + 2],
                                     w[:, k, 128 * q:128 * q + 128], start=k == 0, stop=k == KT - 1)
                    ins.then_inc(used(blk), 1)
                    pe.drain().then_inc(T["ada_pe"].mark(("rows", n, b)), 1)
                    return blk + 1

                def ada_turn(n, bank):
                    pe.wait_ge(done["ada_act"], at("ada_act", l, ("rows", n, 3)))
                    for b in range(4):
                        ins = tr(PS[:, bank, 128 * b:128 * b + 128], ada_rows[:, 128 * b:128 * b + 128])
                    ins.then_inc(T["ada_pe"].mark(("tr", n)), 1)

                for b in range(4):
                    blk = ada_block(blk, 0, b, b)
                ada_turn(0, 7)

                pe.wait_ge(done["nrm_act"], at("nrm_act", l, "h0"))
                for t in range(TILES):
                    for k in range(KT):
                        ins = mm(PS[:, 4, 32 * t:32 * t + 32], hT[:, k, 128 * t:128 * t + 128], w_small[:, k, :],
                                 start=k == 0, stop=k == KT - 1)
                ins.then_inc(T["gate_pe"].mark("proj"), 1)

                def conv_channels(blk, j):
                    if j % 4 == 0:
                        landed(l, blk)
                    if j >= 4:
                        pe.wait_ge(done["conv_act"], at("conv_act", l, ("pad", j - 4)))
                    channels(blk, j % 4, PS[:, j % 4, 0:N]).then_inc(T["conv_pe"].mark(("p", j)), 1)
                    if j % 4 == 3:
                        pe.drain().then_inc(used(blk), 1)
                    return blk + (j % 4 == 3)

                def squared_length(j):
                    pe.wait_ge(done["conv_act"], at("conv_act", l, ("sq", j)))
                    if j >= 4:
                        pe.wait_ge(done["conv_act"], at("conv_act", l, ("root", j - 4)))
                    mm(PS[:, 4 + j % 4, 0:N], ones, (X if j % 2 else XT).rearrange("p h s -> p (h s)")[:, 0:N],
                       start=True, stop=True).then_inc(T["conv_pe"].mark(("ss", j)), 1)

                for j in range(3):
                    blk = conv_channels(blk, j)
                pe.wait_ge(done["gate_dve"], at("gate_dve", l, "lf"))
                for t in range(TILES):
                    for d in range(2):
                        mm(PS[:, 6, 16 * t + 8 * d:16 * t + 8 * d + 8], K(f"tri{d}"), g_lf[:, t, d, :], start=True, stop=True)
                gl = g_lf.rearrange("p t d h -> p (t d h)")
                for n, m in enumerate(("block", "half0", "half1")):
                    ins = mm(PS[:, 6, 48 + 48 * n:96 + 48 * n], K(m), gl, start=True, stop=True)
                ins.then_inc(T["gate_pe"].mark("cum"), 1)

                for j in range(3, 12):
                    blk = conv_channels(blk, j)
                    if j == 4:
                        pe.wait_ge(done["gate_dve"], at("gate_dve", l, "done"))
                    if j >= 4:
                        squared_length(j - 4)
                def heads_of(h):
                    return (2 * h, 2 * h + 1)

                def delta_row(b):
                    pe.wait_ge(done["delta_dve"], at("delta_dve", l, ("g2", b)))
                    mm(PS[:, 0, :], ones, G2.rearrange("p h s -> p (h s)"), start=True, stop=True)\
                        .then_inc(T["delta_pe"].mark(("row", b)), 1)

                def delta_tok(b):
                    t = BATCHES[b][0]
                    tok = slice(128 * t, 128 * t + 128)
                    for h in range(H):
                        tr(PS[:, 1, 128 * h:128 * h + 128], qkvT[:, 4 + h, tok])
                        ins = tr(PS[:, 2, 128 * h:128 * h + 128], qkvT[:, 8 + h, tok])
                    ins.then_inc(T["delta_pe"].mark(("tok", b)), 1)

                def delta_kk(b):
                    t = BATCHES[b][0]
                    tok = slice(128 * t, 128 * t + 128)
                    for h in range(H):
                        mm(PS[:, 3, 128 * h:128 * h + 128], qkvT[:, 4 + h, tok], qkvT[:, 4 + h, tok], start=True, stop=True)
                        ins = mm(PS[:, 4, 128 * h:128 * h + 128], qkvT[:, h, tok], qkvT[:, 4 + h, tok], start=True, stop=True)
                    ins.then_inc(T["delta_pe"].mark(("kk", b)), 1)

                def z_channels(j, bank):
                    landed(l, blk)
                    channels(blk, j, PS[:, bank, 0:N]).then_inc(T["z_pe"].mark(("z", j)), 1)

                pe.wait_ge(done["conv_dve"], at("conv_dve", l, ("unit", 7)))
                pe.wait_ge(done["conv_act"], at("conv_act", l, ("silu", 11)))
                delta_row(0)
                delta_tok(0)
                delta_kk(0)
                for b, (t, d, g) in enumerate(BATCHES):
                    more = b + 1 < NB
                    if b in EARLY_ADA:
                        blk = ada_block(blk, EARLY_ADA[b][0], 5, EARLY_ADA[b][1])
                        pe.wait_ge(done["ada_act"], at("ada_act", l, ("rows", *EARLY_ADA[b])))
                    if b in EARLY_Z:
                        z_channels(EARLY_Z[b], 5)
                        pe.wait_ge(done["z_act"], at("z_act", l, ("z", EARLY_Z[b])))
                    pe.wait_ge(done["delta_dve"], at("delta_dve", l, ("la", b)))
                    for h in range(H):
                        ins = tr(PS[:, 5, 128 * h:128 * h + 128], Lm[:, h, :])
                    ins.then_inc(T["delta_pe"].mark(("lt", b)), 1)
                    if b in ADA_TURN:
                        ada_turn(ADA_TURN[b], 4)
                    if b in LATE_ADA:
                        blk = ada_block(blk, LATE_ADA[b][0], 3, LATE_ADA[b][1])
                    if b in LATE_Z:
                        z_channels(LATE_Z[b], 3)
                    pe.wait_ge(done["delta_pool"], at("delta_pool", l, ("m", b)))
                    for i in range(5):
                        for hf in range(2):
                            pe.wait_ge(done["delta_dve"], at("delta_dve", l, ("x0", b) if i == 0 else ("x", b, i - 1, hf)))
                            for n, h in enumerate(heads_of(hf)):
                                ins = mm(PS[:, 6 - hf, 128 * n:128 * n + 128], Mb[i][:, h, :], X[:, h, :], start=True, stop=True)
                            ins.then_inc(T["delta_pe"].mark(("w", b, i, hf)), 1)
                        for hf in range(2):
                            pe.wait_ge(done["delta_act"], at("delta_act", l, ("wc", b, i, hf)))
                            for n, h in enumerate(heads_of(hf)):
                                mm(PS[:, (7, 0)[hf], 128 * n:128 * n + 128], XT[:, h, :], Wm[:, h, :], start=True, stop=True)
                                ins = mm(PS[:, (7, 0)[hf], 256 + 128 * n:384 + 128 * n], Wm[:, h, :], XT[:, h, :],
                                         start=True, stop=True)
                            ins.then_inc(T["delta_pe"].mark(("y", b, i, hf)), 1)
                    for h in range(H):
                        ins = tr(PS[:, 5, 128 * h:128 * h + 128], av[:, h, :])
                    ins.then_inc(T["delta_pe"].mark(("at", b)), 1)
                    pe.wait_ge(done["delta_dve"], at("delta_dve", l, ("x", b, 4, 1)))
                    for h in range(H):
                        mm(PS[:, 1, 128 * h:128 * h + 128], XT[:, h, :], vb[:, h, :], start=True, stop=True)
                        ins = mm(PS[:, 2, 128 * h:128 * h + 128], kbg[:, h, :], XT[:, h, :], start=True, stop=True)
                    ins.then_inc(T["delta_pe"].mark(("uw", b)), 1)
                    pe.wait_ge(done["delta_act"], at("delta_act", l, ("wtc", b)))
                    pe.wait_ge(done["delta_dve"], at("delta_dve", l, ("u", b)))
                    if b == 2:
                        pe.wait_ge(state_in, 16 * 2 + l * (16 * STATE_LOADS))
                    for c in range(2):
                        cc = c if d == 0 else 1 - c
                        ch = slice(CH * cc, CH * cc + CH)
                        S = states[:, g, d]
                        if c:
                            pe.wait_ge(done["delta_dve"], at("delta_dve", l, ("s", b, 0)))
                        elif b:
                            pe.wait_ge(done["delta_dve"], at("delta_dve", l, ("s", b - 1, 1)))
                        for h in range(H):
                            ins = mm(PS[ch, 5, 128 * h:128 * h + 128], wT[:, h, ch], S[:, h, :], start=True, stop=True)
                        ins.then_inc(T["delta_pe"].mark(("ws", b, c)), 1)
                        if more and c == 0:
                            delta_row(b + 1)
                            delta_tok(b + 1)
                        if more and c == 1:
                            if b in LATE_ADA:
                                pe.wait_ge(done["ada_act"], at("ada_act", l, ("rows", *LATE_ADA[b])))
                            if b in LATE_Z:
                                pe.wait_ge(done["z_act"], at("z_act", l, ("z", LATE_Z[b])))
                            if b in ADA_TURN:
                                pe.wait_ge(done["ada_dve"], at("ada_dve", l, ("mod", ADA_TURN[b])))
                            delta_kk(b + 1)
                        pe.wait_ge(done["delta_dve"], at("delta_dve", l, ("vn", b, c)))
                        for h in range(H):
                            mm(PS[:, 6, CH * h:CH * h + CH], S[:, h, :], qd[:, h, ch], start=True, stop=False)
                            mm(PS[:, 6, CH * h:CH * h + CH], vn[ch, h, :], aT[ch, h, ch], start=False, stop=True)
                        for h in range(H):
                            ins = mm(PS[:, 7, 128 * h:128 * h + 128], kd[ch, h, :], vn[ch, h, :], start=True, stop=True)
                        ins.then_inc(T["delta_pe"].mark(("os", b, c)), 1)

                z_channels(3, 4)
                pe.drain().then_inc(used(blk), 1)
                blk += 1
                landed(l, blk)
                for j in range(2):
                    channels(blk, j, PS[:, j, 0:N]).then_inc(T["mp_pe"].mark(("qk", j)), 1)
                pe.wait_ge(done["z_act"], at("z_act", l, "sq"))
                for h in range(H):
                    ins = mm(PS[:, 4 + h, 0:N], ones, qkvT[:, 4 + h, :], start=True, stop=True)
                ins.then_inc(T["z_pe"].mark("ss"), 1)

                for j in range(2, 4):
                    ins = channels(blk, j, PS[:, j, 0:N])
                    ins.then_inc(T["mp_pe"].mark(("qk", j)), 1)
                pe.wait_ge(done["z_act"], at("z_act", l, "root"))
                for t in range(TILES):
                    if t == 2:
                        pe.wait_ge(done["mp_dve"], at("mp_dve", l, ("kt", 0)))
                    ins = tokens(blk, t, PS[:, 4 + t % 2, 0:256], 256, 512)
                    ins.then_inc(T["mp_pe"].mark(("kt", t)), 1)
                pe.drain().then_inc(used(blk), 1)
                blk += 1
                landed(l, blk)
                for t in range(TILES):
                    if t == 2:
                        pe.wait_ge(done["mp_dve"], at("mp_dve", l, ("v", 0)))
                    ins = tokens(blk, t, PS[:, 6 + t % 2, :])
                    ins.then_inc(T["mp_pe"].mark(("v", t)), 1)
                pe.drain().then_inc(used(blk), 1)
                blk += 1
                landed(l, blk)
                pe.wait_ge(done["mp_act"], at("mp_act", l, ("qk", 3)))
                for t in range(TILES):
                    ins = tokens(blk, t, PS[:, t, :])
                    ins.then_inc(T["mp_pe"].mark(("o", t)), 1)
                pe.drain().then_inc(used(blk), 1)
                blk += 1

                pe.wait_ge(done["mp_dve"], at("mp_dve", l, ("v", 2)))
                pe.wait_ge(done["mp_act"], at("mp_act", l, ("o", 2)))
                merge_a = blk
                blk += 3

                def gate_of_a(c):
                    if c % 4 == 0:
                        landed(l, merge_a + 1 + c // 4)
                    if c:
                        pe.wait_ge(done["ma_dve"], at("ma_dve", l, ("m", c - 1)))
                    channels(merge_a + 1 + c // 4, c % 4, PS[:, 7, 0:N]).then_inc(T["ma_pe"].mark(("g", c)), 1)

                def product_of_a(c):
                    if c == 0:
                        landed(l, merge_a)
                    pe.wait_ge(done["ma_act"], at("ma_act", l, ("sig", c)))
                    w = block_view(merge_a, 4)
                    for k in range(4):
                        ins = mm(PS[:, 7, 0:N], w[:, k, 128 * c:128 * c + 128], yT[0][:, k, :], start=k == 0, stop=k == 3)
                    ins.then_inc(T["ma_pe"].mark(("y", c)), 1)

                def mlstm_row(b):
                    pe.wait_ge(done["ml_dve"], at("ml_dve", l, ("g3", b)))
                    mm(PS[:, 0, :], ones, G3.rearrange("p h s -> p (h s)"), start=True, stop=True)\
                        .then_inc(T["ml_pe"].mark(("row", b)), 1)

                def mlstm_qk(b):
                    t, d, g = BATCHES[b]
                    if b:
                        pe.wait_ge(done["ml_dve"], at("ml_dve", l, ("c", b - 1, 1)))
                    for h in range(H):
                        q, j = h % 2, h // 2
                        rows_, tok = slice(64 * q, 64 * q + 64), slice(128 * t, 128 * t + 128)
                        ins = mm(PS[:, 1 + q, 128 * j:128 * j + 128], qkbT[rows_, j, tok], qkbT[rows_, 2 + j, tok],
                                 start=True, stop=True)
                    ins.then_inc(T["ml_pe"].mark(("qk", b)), 1)

                mlstm_row(0)
                mlstm_qk(0)
                gate_of_a(0)
                product_of_a(0)
                for b, (t, d, g) in enumerate(BATCHES):
                    pe.wait_ge(done["ml_dve"], at("ml_dve", l, ("P", b)))
                    for h in range(H):
                        ins = tr(PS[:, 2, 128 * h:128 * h + 128], Pm[:, h, :])
                    ins.then_inc(T["ml_pe"].mark(("pt", b)), 1)
                    pe.wait_ge(done["ml_act"], at("ml_act", l, ("ptc", b)))
                    for h in range(H):
                        ins = mm(PS[:, 3 + h // 2, (h % 2) * VA:(h % 2) * VA + 129], PTm[:, h, :], v_aug[:, t, h, 0:129],
                                 start=True, stop=True)
                    ins.then_inc(T["ml_pe"].mark(("pv", b)), 1)
                    if b == 2:
                        pe.wait_ge(state_in, 16 * 10 + l * (16 * STATE_LOADS))
                    pe.wait_ge(done["ml_dve"], at("ml_dve", l, ("kw", b)))
                    for c in range(2):
                        cc = c if d == 0 else 1 - c
                        ch = slice(CH * cc, CH * cc + CH)
                        if c:
                            if b + 1 < NB:
                                mlstm_row(b + 1)
                            pe.wait_ge(done["ml_dve"], at("ml_dve", l, ("c", b, 0)))
                        pe.sem_inc(apart["pe"], 1)
                        for h in range(H):
                            q, j = h % 2, h // 2
                            rows_ = slice(64 * q, 64 * q + 64)
                            ins = mm(PS[ch, 5 + q, j * VA:j * VA + 129],
                                     qkbT[rows_, j, 128 * t + CH * cc:128 * t + CH * cc + CH], Cst[rows_, g, d, j, 0:129],
                                     start=True, stop=True)
                        ins.then_inc(T["ml_pe"].mark(("qc", b, c)), 1)
                        for h in range(H):
                            q, j = h % 2, h // 2
                            ins = mm(PS[64 * q:64 * q + 64, 2, j * VA:j * VA + 129], kw[ch, h, :], v_aug[ch, t, h, 0:129],
                                     start=True, stop=True)
                        ins.then_inc(T["ml_pe"].mark(("up", b, c)), 1)
                    gate_of_a(b + 1)
                    if b + 1 < NB:
                        mlstm_qk(b + 1)
                    product_of_a(b + 1)
                gate_of_a(KT - 1)
                product_of_a(KT - 1)
                for _ in range(3):
                    pe.drain().then_inc(used(merge_a), 1)
                    merge_a += 1

                pe.wait_ge(done["ml_dve"], at("ml_dve", l, ("h", NB - 1)))
                landed(l, blk)
                for j in range(4):
                    ins = channels(blk, j, PS[:, j, 0:N])
                    ins.then_inc(T["ap_pe"].mark(("q", j)), 1)
                pe.drain().then_inc(used(blk), 1)
                blk += 1
                for t in range(TILES):
                    pe.wait_ge(done["ml_dve"], at("ml_dve", l, ("y", t)))
                    for h in range(H):
                        ins = tr(PS[:, 4 + t, 128 * h:128 * h + 128], hb_tok[:, t, h, :])
                    ins.then_inc(T["ml_pe"].mark(("yt", t)), 1)
                pe.wait_ge(done["ml_act"], at("ml_act", l, ("yt", 2)))
                landed(l, blk)
                channels(blk, 0, PS[:, 4, 0:N]).then_inc(T["ap_pe"].mark("k"), 1)
                for t in range(TILES):
                    ins = tokens(blk, t, PS[:, 5 + t, 0:256], 0, 256)
                    ins.then_inc(T["ap_pe"].mark(("kv", t)), 1)
                pe.drain().then_inc(used(blk), 1)
                blk += 1
                pe.wait_ge(done["ap_act"], at("ap_act", l, "k"))
                pe.wait_ge(state_in, 16 * STATE_LOADS + l * (16 * STATE_LOADS))
                tr(PS[:, 0, 0:PAST], ck_tok).then_inc(T["ap_pe"].mark("ckT"), 1)
                for j in range(5):
                    src = qcT[:, j, SEQ:N] if j < 4 else kcT[:, SEQ:N]
                    if j == 4:
                        pe.wait_ge(done["ap_dve"], at("ap_dve", l, ("kv", 2)))
                    mm(PS[:, 1 + j, 0:DSEQ], K("rot"), src, start=True, stop=True)\
                        .then_inc(T["ap_pe"].mark(("rot", j)), 1)

                pe.wait_ge(done["ap_dve"], at("ap_dve", l, "rope"))
                pe.wait_ge(done["ap_act"], at("ap_act", l, "ckT"))
                def scores_of(u):
                    t, g = u // 2, u % 2
                    part = slice(64 * g, 64 * g + 64)
                    keys = SEQ if t == 0 else PAST + DSEQ
                    if u:
                        pe.wait_ge(done["at_dve"], at("at_dve", l, ("mx", u - 1)))
                    for j in range(4):
                        q = qcT[part, j, 128 * t:128 * t + 128]
                        if t == 0:
                            ins = mm(PS[:, j, 0:SEQ], q, kcT[part, 0:SEQ], start=True, stop=True)
                        else:
                            mm(PS[:, j, 0:PAST], q, ckT[part, :], start=True, stop=True)
                            ins = mm(PS[:, j, PAST:keys], q, kcT[part, SEQ:N], start=True, stop=True)
                    ins.then_inc(T["at_pe"].mark(("s", u)), 1)

                def outputs_turned(t):
                    pe.wait_ge(done["at_dve"], at("at_dve", l, ("y", 2 * t + 1)))
                    for j in range(4):
                        ins = tr(PS[:, 7, 128 * j:128 * j + 128], yc_tok[:, 128 * j:128 * j + 128])
                    ins.then_inc(T["at_pe"].mark(("yt", t)), 1)

                scores_of(0)
                for u in range(6):
                    t, g = u // 2, u % 2
                    keys = SEQ if t == 0 else PAST + DSEQ
                    if u < 5:
                        scores_of(u + 1)
                    pe.wait_ge(done["at_act"], at("at_act", l, ("e", u)))
                    for m in range(3):
                        if m < keys // 128:
                            for j in range(4):
                                ins = tr(PS[:, 4 + m, 128 * j:128 * j + 128], prob[:, u % 2, j, 128 * m:128 * m + 128])
                            ins.then_inc(T["at_pe"].mark(("pt", u, m)), 1)
                        else:
                            pe.drain().then_inc(T["at_pe"].mark(("pt", u, m)), 1)
                    if g == 0 and u:
                        outputs_turned(t - 1)
                    pe.wait_ge(done["at_act"], at("at_act", l, ("ptc", u)))
                    if u:
                        pe.wait_ge(done["at_dve"], at("at_dve", l, ("y", u - 1)))
                        if g == 0:
                            pe.wait_ge(done["at_act"], at("at_act", l, ("yt", t - 1)))
                    for j in range(4):
                        for m in range(keys // 128):
                            if t == 0:
                                v = kv_tok[:, 0, 128 + 64 * g:192 + 64 * g]
                            elif m == 0:
                                v = cv_tok[:, 64 * g:64 * g + 64]
                            else:
                                v = kv_tok[:, m, 128 + 64 * g:192 + 64 * g]
                            ins = mm(PS[:, 7, 64 * j:64 * j + 64], probT[:, u % 2, j, 128 * m:128 * m + 128], v,
                                     start=m == 0, stop=m == keys // 128 - 1)
                    ins.then_inc(T["at_pe"].mark(("pv", u)), 1)
                outputs_turned(TILES - 1)

                pe.wait_ge(done["at_act"], at("at_act", l, ("yt", 2)))
                for r in (1, 2):
                    for c in range(KT):
                        n = (r - 1) * KT + c
                        if c == 0:
                            landed(l, blk)
                        if c % 4 == 0:
                            landed(l, blk + 1 + c // 4)
                        if n >= 2:
                            pe.wait_ge(done["mix_dve"], at("mix_dve", l, ("m", 1 + (n - 2) // KT, (n - 2) % KT)))
                        channels(blk + 1 + c // 4, c % 4, PS[:, n % 2, 0:N]).then_inc(T["mix_pe"].mark(("g", r, c)), 1)
                        w = block_view(blk, 4)
                        for k in range(4):
                            ins = mm(PS[:, 2 + n % 2, 0:N], w[:, k, 128 * c:128 * c + 128], yT[r][:, k, :],
                                     start=k == 0, stop=k == 3)
                        ins.then_inc(T["mix_pe"].mark(("y", r, c)), 1)
                    for _ in range(3):
                        pe.drain().then_inc(used(blk), 1)
                        blk += 1
                pe.wait_ge(done["mix_dve"], at("mix_dve", l, ("m", 2, KT - 1)))

                def square_sum(k):
                    pe.wait_ge(done["nrm_act"], at("nrm_act", l, ("sq1", k)))
                    ins = mm(PS[:, 0, 0:N], ones, norm_sq[:, k, :], start=k == 0, stop=k == KT - 1)
                    if k == KT - 1:
                        ins.then_inc(T["nrm_pe"].mark("ss1"), 1)

                for c in range(KT):
                    if c % 4 == 0:
                        landed(l, blk)
                    if c >= 4:
                        pe.wait_ge(done["mix_dve"], at("mix_dve", l, ("x", c - 4)))
                    w = block_view(blk)
                    for k in range(KT):
                        ins = mm(PS[:, 4 + c % 4, 0:N], w[:, k, 128 * (c % 4):128 * (c % 4) + 128], mixT[:, k, :],
                                 start=k == 0, stop=k == KT - 1)
                    ins.then_inc(T["mix_pe"].mark(("o", c)), 1)
                    if c % 4 == 3:
                        pe.drain().then_inc(used(blk), 1)
                        blk += 1
                    if c:
                        square_sum(c - 1)

                square_sum(KT - 1)
                pe.wait_ge(done["nrm_act"], at("nrm_act", l, "h1"))
                for t in range(TILES):
                    for k in range(KT):
                        ins = mm(PS[:, 7, 16 * t:16 * t + 16], hT[:, k, 128 * t:128 * t + 128], w_rt[:, k, :],
                                 start=k == 0, stop=k == KT - 1)
                ins.then_inc(T["rt_pe"].mark("logit"), 1)
                pe.wait_ge(done["rt_dve"], at("rt_dve", l, "aff"))
                mm(PS[:, 7, 64:64 + TILES * NE], ident, aff.rearrange("p t e -> p (t e)"), start=True, stop=True)\
                    .then_inc(T["rt_pe"].mark("affx"), 1)
                for t in range(TILES):
                    pe.wait_ge(done["rt_dve"], at("rt_dve", l, ("diag", t)))
                    for n in range(4):
                        ins = mm(PS[:, 4 * (t % 2) + n, :], ones, diag[:, t % 2, 4 * n:4 * n + 4, :].rearrange("p e s -> p (e s)"),
                                 start=True, stop=True)
                    ins.then_inc(T["rt_pe"].mark(("R", t)), 1)
                pe.wait_ge(done["rt_dve"], at("rt_dve", l, ("rank", 1)))
                for t in range(TILES):
                    for u in range(2):
                        if 2 * t + u >= 2:
                            pe.wait_ge(done["rt_act"], at("rt_act", l, ("ht", (2 * t + u - 2) // 2, u)))
                        for k in range(4):
                            ins = tr(PS[:, 5 + u, 128 * k:128 * k + 128], hT[:, 4 * u + k, 128 * t:128 * t + 128])
                        ins.then_inc(T["rt_pe"].mark(("ht", t, u)), 1)
                pe.wait_ge(done["rt_dve"], at("rt_dve", l, "sel"))
                pe.wait_ge(done["rt_act"], at("rt_act", l, ("ht", 2, 1)))
                for j in range(NE // 2):
                    if j >= 2:
                        pe.wait_ge(done["rt_dve"], at("rt_dve", l, ("sg", j - 2)))
                    for t in range(TILES):
                        ins = tr(PS[:, j % 2, 128 * t:128 * t + 128], selG[:, t, 2 * j:2 * j + 2, :].rearrange("p e s -> p (e s)"))
                    ins.then_inc(T["rt_pe"].mark(("sg", j)), 1)
                for k in range(KT):
                    if k >= 2:
                        pe.wait_ge(done["rt_dve"], at("rt_dve", l, ("xs", k - 2)))
                    for t in (1, 2):
                        mm(PS[:, 2 + k % 2, :], h_tok[:, t, 128 * k:128 * k + 128], sel[:, t, :, 0:CAP_S],
                           start=t == 1, stop=t == 2)
                    ins = mm(PS[:, 4 + k % 2, 0:NE * CAP_P], h_tok[:, 0, 128 * k:128 * k + 128], sel[:, 0, :, CAP_S:ROWS],
                             start=True, stop=True)
                    ins.then_inc(T["rt_pe"].mark(("xs", k)), 1)

                def combine(eg, p, blocks=range(KT)):
                    for k in blocks:
                        pe.wait_ge(done["exc_dve"], at_pair("exc_dve", l, eg, p, k) - 2)
                        pe.sem_inc(apart["pe"], 1)
                        mm(PS[:, 6 + k % 2, 0:N], ye[:, p % 2, 128 * k:128 * k + 128],
                           selGT[:, ds(eg * (E_UNROLL // 2) + p, 1), :].rearrange("p a n -> p (a n)"),
                           start=True, stop=True).then_inc(T["exc_pe"].mark((p, k)), 1)

                base_blk = blk
                with pe.Fori(0, NE // E_UNROLL) as eg:
                    pe.wait_ge(done["rt_dve"], at("rt_dve", l, ("xs", KT - 1)))
                    pe.wait_ge(done["rt_pool"], at("rt_pool", l, "clear"))
                    for u in range(E_UNROLL):
                        gu = base_blk + 3 * u
                        pe.wait_ge(done["ex_pool"], at_expert("ex_pool", l, eg, (u, "xs")))
                        landed(l, gu, eg * E_UNROLL)
                        landed(l, gu + 1, eg * E_UNROLL)
                        for k in range(KT):
                            for n in range(2):
                                ins = mm(PS[64 * n:64 * n + ROWS, u % 2, :],
                                         xs_e[:, u % 2, k, :],
                                         block_view(gu + n)[:, k, :], start=k == 0, stop=k == KT - 1)
                                if k == KT - 1:
                                    ins.then_inc(used(gu + n), 1)
                        if u >= 2 and u % 2 == 0:
                            pe.wait_ge(done["ex_act"], at_expert("ex_act", l, eg, (u - 1, "d")))
                            pe.wait_ge(done["ex_dve"], at_expert("ex_dve", l, eg, (u - 1, "d")))
                        if u >= 2:
                            combine(eg, u // 2 - 1, range(4 * (u % 2), 4 * (u % 2) + 2))
                        pe.wait_ge(done["ex_dve"], at_expert("ex_dve", l, eg, (u, "hid")))
                        pe.sem_inc(apart["pe"], 1)
                        for f in range(4):
                            ins = tr(PS[:, 2 + u % 2, ROWS * f:ROWS * f + ROWS], hid[0:ROWS, u % 2, 128 * f:128 * f + 128], ROWS)
                        ins.then_inc(T["ex_pe"].mark((u, "t")), 1)
                        if u >= 2:
                            combine(eg, u // 2 - 1, range(4 * (u % 2) + 2, 4 * (u % 2) + 4))
                        landed(l, gu + 2, eg * E_UNROLL)
                        pe.wait_ge(done["ex_act"], at_expert("ex_act", l, eg, (u, "ht")))
                        pe.wait_ge(done["ex_dve"], at_expert("ex_dve", l, eg, (u, "d"), 2))
                        pe.wait_ge(done["ex_act"], at_expert("ex_act", l, eg, (u, "d"), 2))
                        for f in range(4):
                            for n in range(2):
                                ins = mm(PS[64 * n:64 * n + ROWS, 4 + u % 2, :], hidT[:, u % 2, f, :],
                                         block_view(gu + 2, 4)[:, f, 512 * n:512 * n + 512], start=f == 0, stop=f == 3)
                        ins.then_inc(used(gu + 2), 1)
                    pe.wait_ge(done["ex_act"], at_expert("ex_act", l, eg, (E_UNROLL - 1, "d")))
                    pe.wait_ge(done["ex_dve"], at_expert("ex_dve", l, eg, (E_UNROLL - 1, "d")))
                    combine(eg, E_UNROLL // 2 - 1)
                T["ring_used"].looped(NE // E_UNROLL, 3 * E_UNROLL)
                T["ex_pe"].looped(NE // E_UNROLL, E_UNROLL)
                T["exc_pe"].looped(NE // E_UNROLL, E_UNROLL // 2 * KT)

            pe.wait_ge(final_dve, 1)
            for k in range(KT):
                ins = mm(PS[:, 5, 0:N], ones, norm_sq[:, k, :], start=k == 0, stop=k == KT - 1)
            ins.then_inc(final_pe, 1)
            pe.wait_ge(final_dve, 2)
            for t in range(TILES):
                for u in range(2):
                    for k in range(4):
                        ins = tr(PS[:, 2 * t + u if t < 2 else 6 + u, 128 * k:128 * k + 128], hT[:, 4 * u + k, 128 * t:128 * t + 128])
            ins.then_inc(final_pe, 1)

        @block.scalar
        def _(act):
            f = nc.scalar.activation
            flat = lambda v: v.rearrange("p h s -> p (h s)")

            def copy(out, in_):
                return f(out, in_, ACT.Copy)

            def ada_out(n, b, bank):
                act.wait_ge(done["ada_pe"], at("ada_pe", l, ("rows", n, b)))
                if n and b == 0:
                    act.wait_ge(done["ada_pe"], at("ada_pe", l, ("tr", n - 1)))
                for q in range(4):
                    ins = copy(ada_rows[32 * q:32 * q + 2, 128 * b:128 * b + 128],
                               PS[32 * q:32 * q + 2, bank, 128 * b:128 * b + 128])
                ins.then_inc(T["ada_act"].mark(("rows", n, b)), 1)

            def norm(l, which, sh, a):
                if which == 0:
                    act.wait_ge(T["exc_dve"].sem, T["exc_dve"].before(l))
                    f(norm_sq, xT, ACT.Square).then_inc(T["nrm_act"].mark("sq0"), 1)
                else:
                    for k in range(KT):
                        act.wait_ge(done["mix_dve"], at("mix_dve", l, ("x", k)))
                        f(norm_sq[:, k, :], xT[:, k, :], ACT.Square).then_inc(T["nrm_act"].mark(("sq1", k)), 1)
                act.wait_ge(done["nrm_pe"], at("nrm_pe", l, f"ss{which}"))
                f(rstd[:, :], PS[:, (5, 0)[which], 0:N], ACT.Sqrt, bias=EPS, scale=1.0 / D).then_inc(T["nrm_act"].mark(f"sqrt{which}"), 1)
                if which == 0:
                    for b in range(4):
                        ada_out(0, b, b)
                act.wait_ge(done["ada_dve"], at("ada_dve", l, ("mod", which * 2)))
                for k in range(KT):
                    if k % (KT // 2) == 0:
                        act.wait_ge(done["nrm_dve"], at("nrm_dve", l, ("xn", which, k // (KT // 2))))
                    for g, a0, a1 in GROUPS:
                        n = 2 * (KT * which + k) + g
                        ins = f(hT[:, k, a0:a1], hT[:, k, a0:a1], ACT.Identity, bias=mod[:, sh + k, g:g + 1],
                                scale=affine[:, n:n + 1])
                ins.then_inc(T["nrm_act"].mark(f"h{which}"), 1)

            prime(act, "act")
            act.wait_ge(T["pre_pe"].sem, T["pre_pe"].at(0, "rows"))
            f(condT[:, :].rearrange("p (k v) -> p v k", v=2), PS[:, 7, 384:400].rearrange("p (v k) -> p v k", v=2), ACT.Silu)
            copy(fin_g[:, :], PS[:, 7, 400:408]).then_inc(T["pre_act"].mark("vec"), 1)
            act.wait_ge(T["pre_pe"].sem, T["pre_pe"].at(0, "x"))
            copy(xT[:, 0:4, :], PS[:, 0:4, 0:N]).then_inc(T["pre_act"].mark("x"), 1)
            act.wait_ge(T["pre_dve"].sem, T["pre_dve"].at(0, "x"))
            act.drain()

            with act.Fori(0, DEPTH) as l:
                act.wait_ge(done["ada_pe"], at("ada_pe", l, "vec"))
                copy(vecT[:, 0:125], PS[:, 6, 0:125]).then_inc(T["ada_act"].mark("vec"), 1)
                act.wait_ge(vec_in, 16 * VEC_LOADS + l * (16 * VEC_LOADS))
                f(neg_rate, a_log_b, ACT.Exp).then_inc(T["ada_act"].mark("rate"), 1)
                norm(l, 0, 0, 0)

                act.wait_ge(done["gate_dve"], at("gate_dve", l, "biased"))
                f(gates[:, :, 0:8], gates[:, :, 0:8], ACT.Exp, scale=-1.0)
                f(soft, soft, ACT.Exp, scale=-1.0)
                act.drain().then_inc(T["gate_act"].mark("exp"), 1)
                f(soft, soft, ACT.Ln, bias=1.0).then_inc(T["gate_act"].mark("ln"), 1)
                act.wait_ge(done["gate_dve"], at("gate_dve", l, "args"))
                f(e_cum, cum[:, :, :, 0:H], ACT.Exp)
                for c in range(2):
                    f(e_chunk[:, c], chunk_tot[:, c, :, :, 0:H], ACT.Exp)
                f(kd_f, kd_f, ACT.Exp).then_inc(T["gate_act"].mark("ecum"), 1)

                for j in range(13):
                    if j < 12:
                        act.wait_ge(done["conv_pe"], at("conv_pe", l, ("p", j)))
                        if j >= 4:
                            act.wait_ge(done["conv_dve"], at("conv_dve", l, ("conv", j - 4)))
                        copy(pads[:, j % 4, 2:2 + SEQ], PS[:, j % 4, 0:SEQ])
                        copy(pads[:, j % 4, 6 + SEQ:6 + N], PS[:, j % 4, SEQ:N]).then_inc(T["conv_act"].mark(("pad", j)), 1)
                    if j:
                        act.wait_ge(done["conv_dve"], at("conv_dve", l, ("conv", j - 1)))
                        f(qkvT[:, j - 1, 0:SEQ], acc[:, (j - 1) % 2, 0:SEQ], ACT.Silu)
                        f(qkvT[:, j - 1, SEQ:N], acc[:, (j - 1) % 2, SEQ + 4:N + 4], ACT.Silu)\
                            .then_inc(T["conv_act"].mark(("silu", j - 1)), 1)
                    act.drain()
                    if 3 <= j < 11:
                        i = j - 3
                        if i >= 2:
                            act.wait_ge(done["conv_pe"], at("conv_pe", l, ("ss", i - 2)))
                        f((X if i % 2 else XT).rearrange("p h s -> p (h s)")[:, 0:N], qkvT[:, i, :], ACT.Square)\
                            .then_inc(T["conv_act"].mark(("sq", i)), 1)
                    if 4 <= j < 12:
                        i = j - 4
                        act.wait_ge(done["conv_pe"], at("conv_pe", l, ("ss", i)))
                        if i >= 2:
                            act.wait_ge(done["conv_dve"], at("conv_dve", l, ("unit", i - 2)))
                        s = 128.0 if i < 4 else 1.0
                        f(nrm[:, i % 2, 0:N], PS[:, 4 + i % 4, 0:N], ACT.Sqrt, bias=EPS * s, scale=s)\
                            .then_inc(T["conv_act"].mark(("root", i)), 1)

                def delta_decay(b):
                    act.wait_ge(done["delta_dve"], at("delta_dve", l, ("d", b)))
                    f(flat(er), PS[:, 0, :], ACT.Exp).then_inc(T["delta_act"].mark(("er", b)), 1)
                    f(flat(dec), flat(dec), ACT.Exp, scale=-1.0).then_inc(T["delta_act"].mark(("dec", b)), 1)

                def z_out(j, bank):
                    act.wait_ge(done["z_pe"], at("z_pe", l, ("z", j)))
                    f(silu_z[:, j, :], PS[:, bank, 0:N], ACT.Silu).then_inc(T["z_act"].mark(("z", j)), 1)

                delta_decay(0)
                for b in range(NB):
                    if b in EARLY_ADA:
                        ada_out(*EARLY_ADA[b], 5)
                    if b in EARLY_Z:
                        z_out(EARLY_Z[b], 5)
                    act.wait_ge(done["delta_pe"], at("delta_pe", l, ("lt", b)))
                    copy(flat(LT), PS[:, 5, :]).then_inc(T["delta_act"].mark(("ltc", b)), 1)
                    if b in LATE_ADA:
                        ada_out(*LATE_ADA[b], 3)
                    if b in LATE_Z:
                        z_out(LATE_Z[b], 3)
                    for i in range(5):
                        for hf in range(2):
                            act.wait_ge(done["delta_pe"], at("delta_pe", l, ("w", b, i, hf)))
                            copy(flat(Wm)[:, 256 * hf:256 * hf + 256], PS[:, 6 - hf, 0:256])\
                                .then_inc(T["delta_act"].mark(("wc", b, i, hf)), 1)
                    act.wait_ge(done["delta_pe"], at("delta_pe", l, ("at", b)))
                    copy(flat(aT), PS[:, 5, :]).then_inc(T["delta_act"].mark(("atc", b)), 1)
                    act.wait_ge(done["delta_pe"], at("delta_pe", l, ("uw", b)))
                    copy(flat(wT), PS[:, 2, :]).then_inc(T["delta_act"].mark(("wtc", b)), 1)
                    if b + 1 < NB:
                        delta_decay(b + 1)

                z_out(3, 4)
                act.wait_ge(done["delta_dve"], at("delta_dve", l, ("s", NB - 1, 1)))
                f(qkvT[:, 4:8, :], yT[0], ACT.Square).then_inc(T["z_act"].mark("sq"), 1)
                act.wait_ge(done["z_pe"], at("z_pe", l, "ss"))
                f(qkvT[:, 4:8, :], PS[:, 4:8, 0:N], ACT.Sqrt, bias=EPS, scale=1.0 / 128).then_inc(T["z_act"].mark("root"), 1)

                for j in range(4):
                    act.wait_ge(done["mp_pe"], at("mp_pe", l, ("qk", j)))
                    f(qkbT[:, j, :], PS[:, j, 0:N], ACT.Copy, scale=1.0 if j < 2 else DKB ** -0.5)\
                        .then_inc(T["mp_act"].mark(("qk", j)), 1)
                act.wait_ge(done["z_dve"], at("z_dve", l, ("y", 0)))
                for t in range(TILES):
                    act.wait_ge(done["mp_pe"], at("mp_pe", l, ("o", t)))
                    f(ob_s[:, t, :], PS[:, t, :], ACT.Sigmoid).then_inc(T["mp_act"].mark(("o", t)), 1)

                def mlstm_exps(b):
                    act.wait_ge(done["ml_dve"], at("ml_dve", l, ("args", b)))
                    f(exps_b[:, b % 2], args_b, ACT.Exp).then_inc(T["ml_act"].mark(("ex", b)), 1)
                    f(flat(Em), flat(Em), ACT.Exp).then_inc(T["ml_act"].mark(("E", b)), 1)

                def gate_of_a(c):
                    act.wait_ge(done["ma_pe"], at("ma_pe", l, ("g", c)))
                    f(sig_a, PS[:, 7, 0:N], ACT.Sigmoid).then_inc(T["ma_act"].mark(("sig", c)), 1)

                mlstm_exps(0)
                gate_of_a(0)
                for b in range(NB):
                    act.wait_ge(done["ml_pe"], at("ml_pe", l, ("pt", b)))
                    copy(flat(PTm), PS[:, 2, :]).then_inc(T["ml_act"].mark(("ptc", b)), 1)
                    if b + 1 < NB:
                        mlstm_exps(b + 1)
                    gate_of_a(b + 1)
                gate_of_a(KT - 1)
                act.wait_ge(done["ml_dve"], at("ml_dve", l, "ss"))
                f(stab[:, 0:12], stab[:, 0:12], ACT.Sqrt, bias=EPS, scale=1.0 / 128).then_inc(T["ml_act"].mark("root"), 1)
                for t in range(TILES):
                    act.wait_ge(done["ml_pe"], at("ml_pe", l, ("yt", t)))
                    copy(yT[1][:, :, 128 * t:128 * t + 128], PS[:, 4 + t, :].rearrange("p (h s) -> p h s", h=4))\
                        .then_inc(T["ml_act"].mark(("yt", t)), 1)

                for j in range(4):
                    act.wait_ge(done["ap_pe"], at("ap_pe", l, ("q", j)))
                    f(qcT[:, j, :], PS[:, j, 0:N], ACT.Copy, scale=DC ** -0.5).then_inc(T["ap_act"].mark(("q", j)), 1)
                act.wait_ge(done["ap_pe"], at("ap_pe", l, "k"))
                copy(kcT, PS[:, 4, 0:N]).then_inc(T["ap_act"].mark("k"), 1)
                act.wait_ge(done["ap_pe"], at("ap_pe", l, "ckT"))
                copy(ckT, PS[:, 0, 0:PAST]).then_inc(T["ap_act"].mark("ckT"), 1)

                def exponentials(u):
                    keys = SEQ if u // 2 == 0 else PAST + DSEQ
                    act.wait_ge(done["at_dve"], at("at_dve", l, ("mx", u)))
                    for j in range(4):
                        f(prob[:, u % 2, j, 0:keys], prob[:, u % 2, j, 0:keys], ACT.Exp, bias=nmax[:, u % 2, j:j + 1],
                          accum_out=sums[:, u % 2, j:j + 1])
                    f(esink[:, u % 2, :], esink[:, u % 2, :], ACT.Exp).then_inc(T["at_act"].mark(("e", u)), 1)

                def outputs_turned(t):
                    act.wait_ge(done["at_pe"], at("at_pe", l, ("yt", t)))
                    copy(yT[2][:, :, 128 * t:128 * t + 128], PS[:, 7, :].rearrange("p (j s) -> p j s", j=4))\
                        .then_inc(T["at_act"].mark(("yt", t)), 1)

                exponentials(0)
                for u in range(6):
                    t, g = u // 2, u % 2
                    keys = SEQ if t == 0 else PAST + DSEQ
                    for m in range(keys // 128):
                        act.wait_ge(done["at_pe"], at("at_pe", l, ("pt", u, m)))
                        ins = copy(probT[:, u % 2, :, 128 * m:128 * m + 128],
                                   PS[:, 4 + m, :].rearrange("p (j s) -> p j s", j=4))
                    ins.then_inc(T["at_act"].mark(("ptc", u)), 1)
                    if g == 0 and u:
                        outputs_turned(t - 1)
                    if u < 5:
                        exponentials(u + 1)
                outputs_turned(TILES - 1)

                for r in (1, 2):
                    for c in range(KT):
                        n = (r - 1) * KT + c
                        act.wait_ge(done["mix_pe"], at("mix_pe", l, ("g", r, c)))
                        if n >= 2:
                            act.wait_ge(done["mix_dve"], at("mix_dve", l, ("m", 1 + (n - 2) // KT, (n - 2) % KT)))
                        f(sig[:, n % 2, :], PS[:, n % 2, 0:N], ACT.Sigmoid).then_inc(T["mix_act"].mark(("sig", r, c)), 1)
                norm(l, 1, 24, 1)

                act.wait_ge(done["rt_dve"], at("rt_dve", l, "max"))
                f(aff, logit, ACT.Exp).then_inc(T["rt_act"].mark("exp"), 1)
                for t in range(TILES):
                    for u in range(2):
                        act.wait_ge(done["rt_pe"], at("rt_pe", l, ("ht", t, u)))
                        copy(h_tok[:, t, 512 * u:512 * u + 512], PS[:, 5 + u, :]).then_inc(T["rt_act"].mark(("ht", t, u)), 1)

                with act.Fori(0, NE // E_UNROLL) as eg:
                    act.wait_ge(done["rt_pool"], at("rt_pool", l, "clear"))
                    for u in range(E_UNROLL):
                        gu = PLAIN_BLOCKS + 3 * u
                        act.wait_ge(done["ring_used"], at_block(l, eg, gu + 1))
                        f(silu_g[64:64 + ROWS], PS[0:ROWS, u % 2, :], ACT.Silu).then_inc(T["ex_act"].mark((u, "silu")), 1)
                        act.wait_ge(done["ex_pe"], at_expert("ex_pe", l, eg, (u, "t")))
                        copy(hidT[:, u % 2].rearrange("p f r -> p (f r)"), PS[:, 2 + u % 2, 0:4 * ROWS])\
                            .then_inc(T["ex_act"].mark((u, "ht")), 1)
                        act.wait_ge(done["ring_used"], at_block(l, eg, gu + 2))
                        o = SLOT_E * (u % 2)
                        copy(ye[o:o + ROWS, u // 2 % 2, 0:512], PS[0:ROWS, 4 + u % 2, :]).then_inc(T["ex_act"].mark((u, "d")), 1)
                T["ex_act"].looped(NE // E_UNROLL, 3 * E_UNROLL)

            act.wait_ge(final_pe, 1)
            f(rstd[:, :], PS[:, 5, 0:N], ACT.Sqrt, bias=EPS, scale=1.0 / D).then_inc(final_act, 1)
            act.wait_ge(final_pe, 2)
            for t in range(TILES):
                for u in range(2):
                    ins = copy(y_tok[:, t, 512 * u:512 * u + 512], PS[:, 2 * t + u if t < 2 else 6 + u, :])
            ins.then_inc(final_act, 1)

        @block.vector
        def _(v):
            V = nc.vector
            TT, TS, STT, RED = V.tensor_tensor, V.tensor_scalar, V.scalar_tensor_tensor, V.tensor_reduce
            flat = lambda a: a.rearrange("p h s -> p (h s)")

            def heads(bank):
                return PS[:, bank, :].rearrange("p (h s) -> p h s", h=H)

            def norm(l, which):
                v.wait_ge(done["nrm_act"], at("nrm_act", l, f"sqrt{which}"))
                V.reciprocal(rstd[:, :], rstd[:, :]).then_inc(T["nrm_dve"].mark(f"rstd{which}"), 1)
                v.drain()
                for half in range(2):
                    ks = slice(KT // 2 * half, KT // 2 * half + KT // 2)
                    TT(hT[:, ks, :], xT[:, ks, :], over(rstd[:, :], 1, KT // 2), ALU.mult)\
                        .then_inc(T["nrm_dve"].mark(("xn", which, half)), 1)

            prime(v, "dve")
            V.memset(ada_rows[:, :], 0.0)
            V.memset(bias_b[:, 0:8], 0.0).then_inc(T["pre_dve"].mark("clear"), 1)
            v.wait_ge(T["pre_pe"].sem, T["pre_pe"].at(0, "x"))
            V.tensor_copy(xT[:, 4:8, :], PS[:, 4:8, 0:N]).then_inc(T["pre_dve"].mark("x"), 1)
            v.wait_ge(T["pre_act"].sem, T["pre_act"].at(0, "x"))
            v.drain()

            with v.Fori(0, DEPTH) as l:
                V.memset(pads, 0.0)
                norm(l, 0)

                def ada_mod(n, bank):
                    v.wait_ge(done["ada_pe"], at("ada_pe", l, ("tr", n)))
                    out = mod[:, 16 * n:16 * n + 16, :].rearrange("p (b q) v -> p b q v", q=4)
                    src = PS[:, bank, :].rearrange("p (b q r) -> p b q r", b=4, q=4)[:, :, :, 0:2]
                    for g in range(2):
                        ins = TT(out[:, :, :, g], src[:, :, :, g],
                                 vecT[:, 16 * n:16 * n + 16].rearrange("p (b q) -> p b q", q=4), ALU.add)
                    if n == 1:
                        ins.then_inc(T["ada_dve"].mark(("mod", n)), 1)
                        return
                    v.drain()
                    m = n // 2
                    STT(affine[:, 16 * m:16 * m + 16].rearrange("p (k v) -> p k v", v=2),
                        mod[:, 24 * m + 8:24 * m + 16, :], 1.0, over(vecT[:, 48 + 8 * m:56 + 8 * m], 2, 2),
                        ALU.add, ALU.mult).then_inc(T["ada_dve"].mark(("mod", n)), 1)

                v.wait_ge(done["ada_act"], at("ada_act", l, "vec"))
                ada_mod(0, 7)

                v.wait_ge(done["gate_pe"], at("gate_pe", l, "proj"))
                TT(gates, PS[:, 4, 0:96].rearrange("p (t c) -> p t c", c=32), over(bias_b, 1, TILES), ALU.add)
                v.drain()
                STT(soft, gates, -1.0, gates, ALU.mult, ALU.max).then_inc(T["gate_dve"].mark("biased"), 1)
                v.wait_ge(done["gate_act"], at("gate_act", l, "ln"))
                v.wait_ge(done["ada_act"], at("ada_act", l, "rate"))
                TS(beta, gates[:, :, 0:8], 1.0, None, ALU.add)
                for d in range(2):
                    STT(g_lf[:, :, d, 0:H], gates[:, :, 8 + 4 * d:12 + 4 * d], 0.0, soft[:, :, 8 + 4 * d:12 + 4 * d],
                        ALU.max, ALU.add)
                    STT(g_lf[:, :, d, H:2 * H], gates[:, :, 24 + 4 * d:28 + 4 * d], 0.0, soft[:, :, 24 + 4 * d:28 + 4 * d],
                        ALU.min, ALU.subtract)
                v.drain()
                V.reciprocal(beta, beta)
                for d in range(2):
                    ins = STT(g_lf[:, :, d, 0:H], g_lf[:, :, d, 0:H], -1.0, over(neg_rate[:, 4 * d:4 * d + 4], 1, TILES),
                              ALU.mult, ALU.mult)
                ins.then_inc(T["gate_dve"].mark("lf"), 1)
                v.wait_ge(done["gate_pe"], at("gate_pe", l, "cum"))
                V.tensor_copy(cum.rearrange("p t d h -> p (t d h)"), PS[:, 6, 0:48])
                V.tensor_copy(tot.rearrange("p t d h -> p (t d h)"), PS[:, 6, 48:96])
                V.tensor_copy(chunk_tot.rearrange("p c t d h -> p (c t d h)"), PS[:, 6, 96:192])
                v.drain()
                TT(kd_f, tot[:, :, :, 0:H], cum[:, :, :, 0:H], ALU.subtract)
                TT(rcol, gates[:, :, 16:24].rearrange("p t (d h) -> p t d h", d=2), cum[:, :, :, H:2 * H], ALU.subtract)\
                    .then_inc(T["gate_dve"].mark("args"), 1)
                v.wait_ge(done["gate_act"], at("gate_act", l, "ecum"))
                TT(kbg_f, beta.rearrange("p t (d h) -> p t d h", d=2), e_cum, ALU.mult)\
                    .then_inc(T["gate_dve"].mark("done"), 1)

                for j in range(12):
                    v.wait_ge(done["conv_act"], at("conv_act", l, ("pad", j)))
                    if j >= 2:
                        v.wait_ge(done["conv_act"], at("conv_act", l, ("silu", j - 2)))
                    o = acc[:, j % 2, :]
                    for k in range(CONV_K):
                        x = pads[:, j % 4, k:k + PADW - 4]
                        n = 64 + 12 * k + j
                        if k == 0:
                            ins = TS(o, x, vecT[:, n:n + 1], None, ALU.mult)
                        else:
                            ins = STT(o, x, vecT[:, n:n + 1], o, ALU.mult, ALU.add)
                        if k < CONV_K - 1:
                            v.drain()
                    ins.then_inc(T["conv_dve"].mark(("conv", j)), 1)
                    if j >= 4:
                        i = j - 4
                        v.wait_ge(done["conv_act"], at("conv_act", l, ("root", i)))
                        V.reciprocal(nrm[:, i % 2, 0:N], nrm[:, i % 2, 0:N])
                        v.drain()
                        TT(qkvT[:, i, :], qkvT[:, i, :], nrm[:, i % 2, 0:N], ALU.mult).then_inc(T["conv_dve"].mark(("unit", i)), 1)

                D_ = T["delta_dve"]

                def delta_g2(b):
                    t, d, g = BATCHES[b]
                    TT(G2, over(K(f"tri{d}"), 1, H), over(g_lf[:, t, d, 0:H], 2, 128), ALU.mult).then_inc(D_.mark(("g2", b)), 1)

                def delta_d(b):
                    t, d, g = BATCHES[b]
                    v.wait_ge(done["delta_pe"], at("delta_pe", l, ("row", b)))
                    for h in range(H):
                        ins = TS(dec[:, h, :], PS[:, 0, 128 * h:128 * h + 128], cum[:, t, d, h:h + 1], 0.0, ALU.subtract, ALU.max)
                    ins.then_inc(D_.mark(("d", b)), 1)

                def delta_vk(b):
                    t, d, g = BATCHES[b]
                    v.wait_ge(done["delta_pe"], at("delta_pe", l, ("tok", b)))
                    TT(vb, heads(2), over(beta[:, t, 4 * d:4 * d + 4], 2, 128), ALU.mult)
                    TT(kbg, heads(1), over(kbg_f[:, t, d, :], 2, 128), ALU.mult).then_inc(D_.mark(("vk", b)), 1)

                def delta_la(b):
                    t, d, g = BATCHES[b]
                    tok = slice(128 * t, 128 * t + 128)
                    v.wait_ge(done["delta_act"], at("delta_act", l, ("er", b)))
                    TT(qd, qkvT[:, 0:4, tok], er, ALU.mult)
                    TT(kd, heads(1), over(kd_f[:, t, d, :], 2, 128), ALU.mult).then_inc(D_.mark(("qk", b)), 1)
                    v.wait_ge(done["delta_act"], at("delta_act", l, ("dec", b)))
                    TT(dstr, dec, over(K(f"strict{d}"), 1, H), ALU.mult)
                    TT(dinc, dec, over(K(f"tri{1 - d}"), 1, H), ALU.mult)
                    v.drain()
                    v.wait_ge(done["delta_pe"], at("delta_pe", l, ("kk", b)))
                    for h in range(H):
                        STT(Lm[:, h, :], PS[:, 3, 128 * h:128 * h + 128], beta[:, t, 4 * d + h:4 * d + h + 1], dstr[:, h, :],
                            ALU.mult, ALU.mult)
                    TT(av, heads(4), dinc, ALU.mult).then_inc(D_.mark(("la", b)), 1)

                for d in range(2):
                    V.memset(states[:, 0, d], 0.0)
                delta_g2(0)
                delta_d(0)
                delta_vk(0)
                delta_la(0)
                for b, (t, d, g) in enumerate(BATCHES):
                    more = b + 1 < NB
                    v.drain()
                    TT(X, Lm, over(K(f"lev{d}_1"), 1, H), ALU.mult)
                    v.wait_ge(done["delta_act"], at("delta_act", l, ("ltc", b)))
                    TT(XT, LT, over(K(f"lev{1 - d}_1"), 1, H), ALU.mult)
                    v.drain()
                    TT(X, over(K("ident"), 1, H), X, ALU.subtract)
                    TT(XT, over(K("ident"), 1, H), XT, ALU.subtract).then_inc(D_.mark(("x0", b)), 1)
                    for i in range(5):
                        for hf in range(2):
                            v.drain()
                            v.wait_ge(done["delta_pe"], at("delta_pe", l, ("y", b, i, hf)))
                            two = slice(2 * hf, 2 * hf + 2)
                            y = PS[:, (7, 0)[hf], :].rearrange("p (m h s) -> p m h s", m=2, h=2)
                            TT(X[:, two], X[:, two], y[:, 0], ALU.subtract)
                            TT(XT[:, two], XT[:, two], y[:, 1], ALU.subtract).then_inc(D_.mark(("x", b, i, hf)), 1)
                    v.wait_ge(done["delta_pe"], at("delta_pe", l, ("uw", b)))
                    V.tensor_copy(flat(uv), PS[:, 1, :]).then_inc(D_.mark(("u", b)), 1)
                    if b in ADA_TURN:
                        ada_mod(ADA_TURN[b], 4)
                    if more:
                        delta_g2(b + 1)
                    v.drain()
                    if b == 2:
                        v.wait_ge(state_in, 16 * 2 + l * (16 * STATE_LOADS))
                    for c in range(2):
                        cc = c if d == 0 else 1 - c
                        ch = slice(CH * cc, CH * cc + CH)
                        S = states[:, g, d]
                        v.wait_ge(done["delta_pe"], at("delta_pe", l, ("ws", b, c)))
                        TT(vn[ch], uv[ch], PS[ch, 5, :].rearrange("p (h s) -> p h s", h=H), ALU.subtract)\
                            .then_inc(D_.mark(("vn", b, c)), 1)
                        TT(Sd, S, over(e_chunk[:, cc, t, d, :], 2, 128), ALU.mult)
                        if more:
                            (delta_d, delta_vk)[c](b + 1)
                        v.drain()
                        v.wait_ge(done["delta_pe"], at("delta_pe", l, ("os", b, c)))
                        o = yT[0][:, :, 128 * t + CH * cc:128 * t + CH * cc + CH]
                        po = PS[:, 6, 0:H * CH].rearrange("p (h s) -> p h s", h=H)
                        if d == 0:
                            V.tensor_copy(o, po)
                        else:
                            TT(o, o, po, ALU.add)
                        TT(S, Sd, heads(7), ALU.add).then_inc(D_.mark(("s", b, c)), 1)
                        v.drain()
                    if more:
                        delta_la(b + 1)

                v.wait_ge(done["z_act"], at("z_act", l, "root"))
                V.reciprocal(qkvT[:, 4:8, :], qkvT[:, 4:8, :]).then_inc(T["z_dve"].mark("root"), 1)
                TS(yT[0], yT[0], vecT[:, 124:125], None, ALU.mult)
                v.drain()
                TT(yT[0], yT[0], qkvT[:, 4:8, :], ALU.mult)
                v.drain()
                TT(yT[0], yT[0], silu_z, ALU.mult).then_inc(T["z_dve"].mark(("y", 0)), 1)

                v.drain()
                V.memset(v_aug[:, :, :, 128:129], 1.0)
                V.memset(m_state[:, 0], 0.0)
                v.wait_ge(done["delta_pe"], at("delta_pe", l, ("os", NB - 1, 1)))
                v.wait_ge(stored, 16 * 2 + l * (16 * STORES))
                V.memset(Cst[:, 0], 0.0).then_inc(T["mp_dve"].mark("ones"), 1)
                for t in range(TILES):
                    v.wait_ge(done["mp_pe"], at("mp_pe", l, ("kt", t)))
                    TS(kb_tok[:, t, :], PS[:, 4 + t % 2, 0:256], DKB ** -0.5, None, ALU.mult).then_inc(T["mp_dve"].mark(("kt", t)), 1)
                for t in range(TILES):
                    v.wait_ge(done["mp_pe"], at("mp_pe", l, ("v", t)))
                    V.tensor_copy(v_aug[:, t, :, 0:128], heads(6 + t % 2)).then_inc(T["mp_dve"].mark(("v", t)), 1)
                v.drain()

                D_ = T["ml_dve"]

                def gate_rows(b):
                    t, d, g = BATCHES[b]
                    TT(G3, over(K("ident"), 1, H), over(gates[:, t, 16 + 4 * d:20 + 4 * d], 2, 128), ALU.mult)
                    TT(g3b, over(K(f"tri{d}"), 1, H), over(g_lf[:, t, d, H:2 * H], 2, 128), ALU.mult)
                    v.drain()
                    TT(G3, G3, g3b, ALU.subtract).then_inc(D_.mark(("g3", b)), 1)

                def front(b):
                    t, d, g = BATCHES[b]
                    v.wait_ge(done["ml_pe"], at("ml_pe", l, ("row", b)))
                    RED(mx, PS[:, 0, :].rearrange("p (a s) -> p a s", s=CH), AX, ALU.max)
                    TT(Rm, heads(0), over(K(f"neg{d}"), 1, H), ALU.add)
                    v.drain()
                    RED(dmx, Rm, AX, ALU.max)
                    c0, c1 = (0, 1) if d == 0 else (1, 0)
                    m0 = m_state[:, g, d]
                    cm = [chunk_tot[:, c, t, d, H:2 * H] for c in range(2)]
                    mm0, m1, mm1, mprev, mmx, mr = (stab[:, 16 + 4 * n:20 + 4 * n] for n in range(6))
                    if b == 2:
                        v.wait_ge(vec_in, 16 * VEC_LOADS + l * (16 * VEC_LOADS))
                    TT(mm0, m0, mx[:, :, c0], ALU.max)
                    v.drain()
                    TT(m1, mm0, cm[c0], ALU.add)
                    v.drain()
                    TT(mm1, m1, mx[:, :, c1], ALU.max)
                    for c, mp, mq in ((c0, m0, mm0), (c1, m1, mm1)):
                        ch = slice(CH * c, CH * c + CH)
                        V.tensor_copy(mprev[ch], mp[ch])
                        if c == c1:
                            v.drain()
                        V.tensor_copy(mmx[ch], mq[ch])
                    v.drain()
                    TT(mr, mprev, dmx, ALU.max)
                    TT(args_b[:, 3, :], m0, mm0, ALU.subtract)
                    TT(args_b[:, 4, :], m1, mm1, ALU.subtract)
                    TT(args_b[:, 1, :], rcol[:, t, d, :], mmx, ALU.subtract)
                    v.drain()
                    TT(m0, mm1, cm[c1], ALU.add)
                    TT(args_b[:, 0, :], mprev, mr, ALU.subtract)
                    TT(Em, Rm, over(mr, 2, 128), ALU.subtract)
                    TT(args_b[:, 2, :], cum[:, t, d, H:2 * H], mr, ALU.add)
                    v.drain()
                    TS(args_b[:, 2, :], args_b[:, 2, :], -1.0, None, ALU.mult).then_inc(D_.mark(("args", b)), 1)

                def product_of_a(c):
                    v.wait_ge(done["ma_pe"], at("ma_pe", l, ("y", c)))
                    v.wait_ge(done["ma_act"], at("ma_act", l, ("sig", c)))
                    TT(mixT[:, c, :], PS[:, 7, 0:N], sig_a, ALU.mult).then_inc(T["ma_dve"].mark(("m", c)), 1)

                gate_rows(0)
                front(0)
                for b, (t, d, g) in enumerate(BATCHES):
                    exps = exps_b[:, b % 2]
                    v.wait_ge(done["ml_pe"], at("ml_pe", l, ("qk", b)))
                    v.wait_ge(done["ml_act"], at("ml_act", l, ("E", b)))
                    for q in range(2):
                        o = Pm.rearrange("p (j q) s -> p q j s", q=2)[:, q]
                        e = Em.rearrange("p (j q) s -> p q j s", q=2)[:, q]
                        ins = TT(o, e, PS[:, 1 + q, 0:256].rearrange("p (j s) -> p j s", j=2), ALU.mult)
                    ins.then_inc(D_.mark(("P", b)), 1)
                    TT(kw, kb_tok[:, t, :].rearrange("p (h s) -> p h s", h=H), over(exps[:, 1, :], 2, DKB), ALU.mult)
                    for q in range(2):
                        r_ = slice(64 * q, 64 * q + 64)
                        ins = V.tensor_copy(wp[r_], exps[r_, 3:5, :].rearrange("p c (j q) -> p q c j", q=2)[:, q])
                    ins.then_inc(D_.mark(("kw", b)), 1)
                    if b + 1 < NB:
                        gate_rows(b + 1)
                    product_of_a(b)
                    v.drain()
                    if b == 2:
                        v.wait_ge(state_in, 16 * 10 + l * (16 * STATE_LOADS))
                    for c in range(2):
                        v.wait_ge(done["ml_pe"], at("ml_pe", l, ("up", b, c)))
                        C_ = Cst[:, g, d, :, 0:129]
                        TT(C_, C_, over(wp[:, c, :], 2, 129), ALU.mult)
                        v.drain()
                        TT(C_, C_, PS[:, 2, 0:2 * VA].rearrange("p (j s) -> p j s", j=2)[:, :, 0:129], ALU.add)\
                            .then_inc(D_.mark(("c", b, c)), 1)
                        v.drain()
                    if b + 1 < NB:
                        front(b + 1)
                    for q in range(2):
                        TT(QCw.rearrange("p (j q) s -> p q j s", q=2)[:, q, :, 0:129],
                           PS[:, 5 + q, 0:2 * VA].rearrange("p (j s) -> p j s", j=2)[:, :, 0:129],
                           over(exps[:, 0, :].rearrange("p (j q) -> p q j", q=2)[:, q], 2, 129), ALU.mult)
                    v.drain()
                    for j in range(2):
                        TT(num[:, 2 * j:2 * j + 2, 0:129], QCw[:, 2 * j:2 * j + 2, 0:129],
                           PS[:, 3 + j, 0:2 * VA].rearrange("p (q s) -> p q s", q=2)[:, :, 0:129], ALU.add)
                    v.drain()
                    STT(rden, num[:, :, 128], -1.0, num[:, :, 128], ALU.mult, ALU.max)
                    v.drain()
                    TT(rden, rden, exps[:, 2, :], ALU.max)
                    v.drain()
                    V.reciprocal(rden, rden)
                    v.drain()
                    if d == 0:
                        TT(hb_tok[:, t], num[:, :, 0:128], over(rden, 2, 128), ALU.mult).then_inc(D_.mark(("h", b)), 1)
                    else:
                        TT(num[:, :, 0:128], num[:, :, 0:128], over(rden, 2, 128), ALU.mult)
                        v.drain()
                        TT(hb_tok[:, t], hb_tok[:, t], num[:, :, 0:128], ALU.add).then_inc(D_.mark(("h", b)), 1)
                    v.drain()
                product_of_a(NB)
                for t in range(TILES):
                    TT(sq_b, hb_tok[:, t], hb_tok[:, t], ALU.mult)
                    v.drain()
                    RED(stab[:, 4 * t:4 * t + 4], sq_b, AX, ALU.add)
                    v.drain()
                v.drain().then_inc(T["ml_dve"].mark("ss"), 1)
                product_of_a(KT - 1)
                v.wait_ge(done["ml_act"], at("ml_act", l, "root"))
                V.reciprocal(stab[:, 0:12], stab[:, 0:12])
                v.drain()
                for t in range(TILES):
                    TT(hb_tok[:, t], hb_tok[:, t], over(stab[:, 4 * t:4 * t + 4], 2, 128), ALU.mult)
                    v.drain()
                    TT(hb_tok[:, t], hb_tok[:, t], over(mnorm_b, 1, H), ALU.mult)
                    v.drain()
                    TT(hb_tok[:, t], hb_tok[:, t], ob_s[:, t, :].rearrange("p (h s) -> p h s", h=H), ALU.mult)\
                        .then_inc(T["ml_dve"].mark(("y", t)), 1)

                v.wait_ge(done["ml_act"], at("ml_act", l, ("yt", 2)))
                for t in range(TILES):
                    v.wait_ge(done["ap_pe"], at("ap_pe", l, ("kv", t)))
                    V.tensor_copy(kv_tok[:, t, :], PS[:, 5 + t, 0:256]).then_inc(T["ap_dve"].mark(("kv", t)), 1)
                v.wait_ge(done["ap_act"], at("ap_act", l, "k"))
                for j in range(5):
                    x = qcT[:, j, SEQ:N] if j < 4 else kcT[:, SEQ:N]
                    TT(rope_a[:, j, :], x, K("cos"), ALU.mult)
                    v.wait_ge(done["ap_pe"], at("ap_pe", l, ("rot", j)))
                    TT(rope_b[:, j, :], PS[:, 1 + j, 0:DSEQ], K("sin"), ALU.mult).then_inc(T["ap_dve"].mark(("cos", j)), 1)
                v.drain()
                TT(qcT[:, :, SEQ:N], rope_a[:, 0:4, :], rope_b[:, 0:4, :], ALU.add)
                TT(kcT[:, SEQ:N], rope_a[:, 4, :], rope_b[:, 4, :], ALU.add).then_inc(T["ap_dve"].mark("rope"), 1)

                def attend_out(u):
                    t, g = u // 2, u % 2
                    v.wait_ge(done["at_act"], at("at_act", l, ("e", u)))
                    r = rinv[:, 4 * g:4 * g + 4]
                    TT(r, sums[:, u % 2, :], esink[:, u % 2, :], ALU.add)
                    v.drain()
                    V.reciprocal(r, r)
                    v.drain()
                    v.wait_ge(done["at_pe"], at("at_pe", l, ("pv", u)))
                    TT(yc_tok[:, 256 * g:256 * g + 256].rearrange("p (j s) -> p j s", j=4),
                       PS[:, 7, 0:256].rearrange("p (j s) -> p j s", j=4), over(r, 2, 64), ALU.mult)\
                        .then_inc(T["at_dve"].mark(("y", u)), 1)
                    v.drain()

                def maxima(u):
                    t, g = u // 2, u % 2
                    keys = SEQ if t == 0 else PAST + DSEQ
                    v.wait_ge(done["at_pe"], at("at_pe", l, ("s", u)))
                    pr = prob[:, u % 2, :, 0:keys]
                    if t == 0:
                        V.tensor_copy(pr, PS[:, 0:4, 0:keys])
                    else:
                        TT(pr, PS[:, 0:4, 0:keys], over(K(f"win{t - 1}"), 1, 4), ALU.add)
                    v.drain()
                    nm = nmax[:, u % 2, :]
                    RED(nm, pr, AX, ALU.max)
                    v.drain()
                    TT(nm, nm, sink_b[:, 4 * g:4 * g + 4], ALU.max)
                    v.drain()
                    TT(esink[:, u % 2, :], sink_b[:, 4 * g:4 * g + 4], nm, ALU.subtract)
                    v.drain()
                    TS(nm, nm, -1.0, None, ALU.mult).then_inc(T["at_dve"].mark(("mx", u)), 1)

                maxima(0)
                for u in range(6):
                    if u < 5:
                        maxima(u + 1)
                    attend_out(u)

                v.wait_ge(stored, 16 * STORES + l * (16 * STORES))
                for r in (1, 2):
                    for c in range(KT):
                        n = (r - 1) * KT + c
                        v.wait_ge(done["mix_act"], at("mix_act", l, ("sig", r, c)))
                        v.wait_ge(done["mix_pe"], at("mix_pe", l, ("y", r, c)))
                        ps, s = PS[:, 2 + n % 2, 0:N], sig[:, n % 2, :]
                        TT(prod[:, n % 2, :], ps, s, ALU.mult)
                        v.drain()
                        TT(mixT[:, c, :], mixT[:, c, :], prod[:, n % 2, :], ALU.add)\
                            .then_inc(T["mix_dve"].mark(("m", r, c)), 1)
                for c in range(KT):
                    v.wait_ge(done["mix_pe"], at("mix_pe", l, ("o", c)))
                    for g, a0, a1 in GROUPS:
                        ins = STT(xT[:, c, a0:a1], PS[:, 4 + c % 4, a0:a1], mod[:, 16 + c, g:g + 1], xT[:, c, a0:a1],
                                  ALU.mult, ALU.add)
                    ins.then_inc(T["mix_dve"].mark(("x", c)), 1)
                v.drain()
                norm(l, 1)

                v.wait_ge(done["rt_pe"], at("rt_pe", l, "logit"))
                lg = PS[:, 7, 0:TILES * NE].rearrange("p (t e) -> p t e", e=NE)
                RED(smx, lg, AX, ALU.max)
                v.drain()
                TT(logit, lg, over(smx, 2, NE), ALU.subtract).then_inc(T["rt_dve"].mark("max"), 1)
                v.wait_ge(done["rt_act"], at("rt_act", l, "exp"))
                RED(smx, aff, AX, ALU.add)
                v.drain()
                V.reciprocal(smx, smx)
                v.drain()
                TT(aff, aff, over(smx, 2, NE), ALU.mult).then_inc(T["rt_dve"].mark("aff"), 1)

                def own_column(t):
                    TT(diag[:, t % 2], over(K("ident"), 1, NE), over(aff[:, t, :], 2, 128), ALU.mult)\
                        .then_inc(T["rt_dve"].mark(("diag", t)), 1)

                v.drain()
                own_column(0)
                v.wait_ge(done["rt_pe"], at("rt_pe", l, "affx"))
                V.tensor_copy(aff_x, PS[:, 7, 64:64 + TILES * NE].rearrange("p (t e) -> p t e", e=NE))\
                    .then_inc(T["rt_dve"].mark("affx"), 1)
                v.drain()
                own_column(1)
                for t in range(TILES):
                    v.wait_ge(done["rt_pe"], at("rt_pe", l, ("R", t)))
                    R = PS[:, 4 * (t % 2):4 * (t % 2) + 4, :].rearrange("p n (e s) -> p (n e) s", s=128)
                    mine = over(aff_x[:, t, :], 2, 128)
                    TT(rk, R, mine, ALU.is_gt)
                    TT(rk_tmp, R, mine, ALU.is_equal)
                    v.drain()
                    TT(rk_m, rk_tmp, over(K("earlier"), 1, NE), ALU.mult)
                    v.drain()
                    TT(rk, rk, rk_m, ALU.add)
                    v.drain()
                    if t == 0:
                        RED(rank[:, 0, :], rk, AX, ALU.add)
                    else:
                        RED(rtmp[:, 0, :], rk, AX, ALU.add)
                        other = 3 - t
                        v.drain()
                        TT(rk, R, over(aff_x[:, other, :], 2, 128), ALU.is_gt if t == 2 else ALU.is_ge)
                        v.drain()
                        RED(rtmp[:, other, :], rk, AX, ALU.add)
                        v.drain()
                        if t == 1:
                            V.tensor_copy(rank[:, 1, :], rtmp[:, 0, :])
                        else:
                            TT(rank[:, 2, :], rtmp[:, 0, :], rtmp[:, 2, :], ALU.add)
                            TT(rank[:, 1, :], rank[:, 1, :], rtmp[:, 1, :], ALU.add)
                    v.drain()
                    v.drain().then_inc(T["rt_dve"].mark(("rank", t)), 1)
                    if t == 0:
                        own_column(2)
                for t in range(TILES):
                    TT(sel[:, t], over(K("slot_s" if t else "slot_p"), 1, NE), over(rank[:, t, :], 2, SLOT_E), ALU.is_equal)
                v.drain()
                TT(selG.rearrange("p t e s -> p (t e) s"), sel.rearrange("p t e s -> p (t e) s"),
                   over(aff.rearrange("p t e -> p (t e)"), 2, SLOT_E), ALU.mult).then_inc(T["rt_dve"].mark("sel"), 1)
                for j in range(NE // 2):
                    v.wait_ge(done["rt_pe"], at("rt_pe", l, ("sg", j)))
                    V.tensor_copy(selGT[:, j, :], PS[:, j % 2, 0:N]).then_inc(T["rt_dve"].mark(("sg", j)), 1)
                for k in range(KT):
                    v.wait_ge(done["rt_pe"], at("rt_pe", l, ("xs", k)))
                    V.tensor_copy(xsT[:, k, :, 0:CAP_S], PS[:, 2 + k % 2, :].rearrange("p (e r) -> p e r", e=NE))
                    V.tensor_copy(xsT[:, k, :, CAP_S:ROWS], PS[:, 4 + k % 2, 0:NE * CAP_P].rearrange("p (e r) -> p e r", e=NE))\
                        .then_inc(T["rt_dve"].mark(("xs", k)), 1)

                def combine(eg, p, blocks=range(KT)):
                    for k in blocks:
                        v.wait_ge(done["exc_pe"], at_pair("exc_pe", l, eg, p, k))
                        for g, a0, a1 in GROUPS:
                            ins = STT(xT[:, k, a0:a1], PS[:, 6 + k % 2, a0:a1], mod[:, 40 + k, g:g + 1], xT[:, k, a0:a1],
                                      ALU.mult, ALU.add)
                        ins.then_inc(T["exc_dve"].mark((p, k)), 1)

                with v.Fori(0, NE // E_UNROLL) as eg:
                    v.wait_ge(done["rt_pool"], at("rt_pool", l, "clear"))
                    for u in range(E_UNROLL):
                        gu = PLAIN_BLOCKS + 3 * u
                        v.wait_ge(done["ex_act"], at_expert("ex_act", l, eg, (u, "silu")))
                        TT(hid[0:ROWS, u % 2, :], silu_g[64:64 + ROWS], PS[64:64 + ROWS, u % 2, :], ALU.mult)\
                            .then_inc(T["ex_dve"].mark((u, "hid")), 1)
                        if u >= 2:
                            combine(eg, u // 2 - 1, range(4 * (u % 2), 4 * (u % 2) + 4))
                        v.wait_ge(done["ring_used"], at_block(l, eg, gu + 2))
                        o = SLOT_E * (u % 2)
                        V.tensor_copy(ye[o:o + ROWS, u // 2 % 2, 512:1024], PS[64:64 + ROWS, 4 + u % 2, :]).then_inc(T["ex_dve"].mark((u, "d")), 1)
                    combine(eg, E_UNROLL // 2 - 1)
                    v.drain()
                T["ex_dve"].looped(NE // E_UNROLL, 2 * E_UNROLL)
                T["exc_dve"].looped(NE // E_UNROLL, E_UNROLL // 2 * KT)
                v.drain()


            TT(norm_sq, xT, xT, ALU.mult).then_inc(final_dve, 1)
            v.wait_ge(final_act, 1)
            V.reciprocal(rstd[:, :], rstd[:, :])
            v.drain()
            TT(hT, xT, over(rstd[:, :], 1, KT), ALU.mult)
            v.drain()
            for k in range(KT):
                ins = TS(hT[:, k, :], hT[:, k, :], fin_g[:, k:k + 1], None, ALU.mult)
            ins.then_inc(final_dve, 1)


_INS = ["x_prompt", "x_sample", "cache_attn_k", "cache_attn_v", "state_delta", "state_mlstm_c", "state_mlstm_n",
        "state_mlstm_m", "c", "c_ctx", "ada_w", "ada_b", "norm1_g", "norm2_g", "w_in", "conv_qkv_a", "delta_a_log",
        "delta_dt_bias", "delta_norm_g", "mlstm_i_bias", "mlstm_f_bias", "mlstm_norm_g", "attn_sink", "w_branch_a",
        "w_branch_b", "w_branch_c", "w_out", "w_router", "w_expert_gate", "w_expert_up", "w_expert_down",
        "final_norm_g"]
_OUTS = [(1, SEQ, D), (1, DSEQ, D), (1, DEPTH, SEQ, 2, DC), (1, DEPTH, SEQ, 2, DC), (1, DEPTH, 2, H, 128, 128),
         (1, DEPTH, 2, H, DKB, 128), (1, DEPTH, 2, H, DKB), (1, DEPTH, 2, H)]


def kernel(**inputs):
    import numpy as _np
    import concourse.bacc as _bacc
    from concourse import mybir as _mybir
    from concourse.bass_utils import run_bass_kernel_spmd as _run

    nc = _bacc.Bacc("TRN2", target_bir_lowering=False, num_devices=1)
    arrays, args = {}, []
    for name in _INS:
        a = _np.ascontiguousarray(inputs[name])
        arrays[f"in_{name}_dram"] = a
        args.append(nc.dram_tensor(f"in_{name}_dram", a.shape, _mybir.dt.from_np(a.dtype), kind="ExternalInput").ap())
    a = const_columns()[0]
    arrays["in_consts_dram"] = a
    args.append(nc.dram_tensor("in_consts_dram", a.shape, F32, kind="ExternalInput").ap())
    for i, shape in enumerate(_OUTS):
        args.append(nc.dram_tensor(f"out_{i}_dram", shape, F32, kind="ExternalOutput").ap())
    build_step(nc, args)
    r = _run(nc, [arrays], core_ids=[0])
    return tuple(r.results[0][f"out_{i}_dram"] for i in range(len(_OUTS)))
```
